# Optimizing a Trainium2 kernel written in Bass

```python
import jax, jax.numpy as jnp
from jax import lax
import numpy as np

D_MODEL = 1024
BATCH = 1
SEQ = 1024
DEPTH = 1

HEAD_DIM = 64
SB_HEADS = 8
SB_WIDTH = SB_HEADS * HEAD_DIM
SC_WIDTH = 512
SC_KERNEL = 3
DSA_HEADS = 8
DSA_WIDTH = DSA_HEADS * HEAD_DIM
IDX_HEADS = 8
IDX_DIM = 64
DSA_TOPK_MAX = 256
MEM_LEN = 256
XA_HEADS = 4
XA_HEAD_DIM = D_MODEL // XA_HEADS
D_FF = 2816
FFN_KERNEL = 3
Q_BLOCK = 128
N_BRANCH = 3
RMS_EPS = 1e-6
IN_SIZES = (3 * SB_WIDTH, 3 * SC_WIDTH, 3 * DSA_WIDTH, IDX_HEADS * IDX_DIM, IDX_DIM, IDX_HEADS, N_BRANCH * D_MODEL)
D_IN = sum(IN_SIZES)

kernel_name = "hybrid_stickbreak_shortconv_dsa_gated_block"

F32 = jnp.float32

def rmsnorm(x, g):
    xf = x.astype(F32)
    y = xf * lax.rsqrt(jnp.mean(xf * xf, axis=-1, keepdims=True) + RMS_EPS)
    return (y * g.astype(F32)).astype(x.dtype)

def causal_dwconv(u, w):
    K = w.shape[0]
    S = u.shape[1]
    up = jnp.pad(u, ((0, 0), (K - 1, 0), (0, 0)))
    return sum(w[k] * up[:, k:k + S] for k in range(K))

def to_blocks(a):
    B, S = a.shape[:2]
    return a.reshape((B, S // Q_BLOCK, Q_BLOCK) + a.shape[2:]).swapaxes(0, 1)

def from_blocks(a):
    a = a.swapaxes(0, 1)
    return a.reshape((a.shape[0], a.shape[1] * a.shape[2]) + a.shape[3:])

def stick_breaking_attention(q, k, v):
    B, S, H, Dh = q.shape
    nb = S // Q_BLOCK
    scale = Dh ** -0.5
    kf = k.astype(F32)
    vf = v.astype(F32)
    key_pos = jnp.arange(S)

    def block(args):
        qi, i = args
        z = jnp.einsum('bqhd,bshd->bhqs', qi.astype(F32), kf) * scale
        q_pos = i * Q_BLOCK + jnp.arange(Q_BLOCK)
        causal = key_pos[None, :] < q_pos[:, None]
        log_1m = jnp.where(causal, jax.nn.log_sigmoid(-z), 0.0)
        after = lax.cumsum(log_1m, axis=3, reverse=True) - log_1m
        w = jnp.where(causal, jnp.exp(jax.nn.log_sigmoid(z) + after), 0.0)
        return jnp.einsum('bhqs,bshd->bqhd', w, vf)

    out = lax.map(block, (to_blocks(q), jnp.arange(nb)))
    return from_blocks(out).astype(q.dtype)

def dsa_attention(q, k, v, q_idx, k_idx, w_idx):
    B, S, H, Dh = q.shape
    nb = S // Q_BLOCK
    top_k = min(DSA_TOPK_MAX, S // 4)
    kif = k_idx.astype(F32)
    key_pos = jnp.arange(S)

    def gather_rows(a, idx):
        return jax.vmap(lambda ab, ib: ab[ib])(a, idx)

    def block(args):
        qi, qii, wi, i = args
        q_pos = i * Q_BLOCK + jnp.arange(Q_BLOCK)
        idx_logits = jnp.einsum('bqhd,bsd->bqhs', qii.astype(F32), kif) * (IDX_DIM ** -0.5)
        score = jnp.einsum('bqh,bqhs->bqs', wi.astype(F32) * (IDX_HEADS ** -0.5), jax.nn.relu(idx_logits))
        admissible = key_pos[None, :] <= q_pos[:, None]
        score = jnp.where(admissible[None], score, -jnp.inf)
        _, sel = lax.top_k(score, top_k)
        valid = sel <= q_pos[None, :, None]
        flat = sel.reshape(B, Q_BLOCK * top_k)
        ks = gather_rows(k, flat).reshape(B, Q_BLOCK, top_k, H, Dh).astype(F32)
        vs = gather_rows(v, flat).reshape(B, Q_BLOCK, top_k, H, Dh).astype(F32)
        logits = jnp.einsum('bqhd,bqkhd->bhqk', qi.astype(F32), ks) * (Dh ** -0.5)
        logits = jnp.where(valid[:, None], logits, -jnp.inf)
        p = jax.nn.softmax(logits, axis=-1)
        return jnp.einsum('bhqk,bqkhd->bqhd', p, vs)

    out = lax.map(block, (to_blocks(q), to_blocks(q_idx), to_blocks(w_idx), jnp.arange(nb)))
    return from_blocks(out).astype(q.dtype)

def hybrid_mixer(h, w_in, sc_conv_w, w_sb_out, w_sc_out, w_dsa_out, w_mix_o):
    B, S, _ = h.shape
    z = h @ w_in
    sb_qkv, sc_bcx, dsa_qkv, idx_q, idx_k, idx_w, gates = jnp.split(z, list(np.cumsum(IN_SIZES)[:-1]), axis=-1)
    sb = sb_qkv.reshape(B, S, 3, SB_HEADS, HEAD_DIM)
    y_a = stick_breaking_attention(sb[:, :, 0], sb[:, :, 1], sb[:, :, 2]).reshape(B, S, SB_WIDTH)
    b_gate, c_gate, x_in = jnp.split(sc_bcx, 3, axis=-1)
    y_b = b_gate * causal_dwconv(c_gate * x_in, sc_conv_w)
    dq = dsa_qkv.reshape(B, S, 3, DSA_HEADS, HEAD_DIM)
    y_c = dsa_attention(dq[:, :, 0], dq[:, :, 1], dq[:, :, 2],
                        idx_q.reshape(B, S, IDX_HEADS, IDX_DIM), idx_k, idx_w).reshape(B, S, DSA_WIDTH)
    g = jax.nn.sigmoid(gates.reshape(B, S, N_BRANCH, D_MODEL).astype(F32)).astype(h.dtype)
    merged = g[:, :, 0] * (y_a @ w_sb_out) + g[:, :, 1] * (y_b @ w_sc_out) + g[:, :, 2] * (y_c @ w_dsa_out)
    return merged @ w_mix_o

def memory_cross_attention(h, mem_n, w_q, w_kv, w_o):
    B, S, _ = h.shape
    M = mem_n.shape[1]
    q = (h @ w_q).reshape(B, S, XA_HEADS, XA_HEAD_DIM).astype(F32)
    kv = (mem_n @ w_kv).reshape(B, M, 2, XA_HEADS, XA_HEAD_DIM).astype(F32)
    logits = jnp.einsum('bshd,bmhd->bhsm', q, kv[:, :, 0]) * (XA_HEAD_DIM ** -0.5)
    p = jax.nn.softmax(logits, axis=-1)
    o = jnp.einsum('bhsm,bmhd->bshd', p, kv[:, :, 1]).astype(h.dtype)
    return o.reshape(B, S, D_MODEL) @ w_o

def conv_ffn(h, w_in, conv_w, conv_b, w_down):
    a, u = jnp.split(h @ w_in, 2, axis=-1)
    a = causal_dwconv(a, conv_w) + conv_b
    return (jax.nn.gelu(a) * u) @ w_down

def setup_inputs(seed: int = 0) -> dict:
    key = jax.random.key(seed)
    ks = jax.random.split(key, 24)

    def nrm(k, shape, fan_in):
        return jax.random.normal(k, shape, F32) * (fan_in ** -0.5)

    def gain(k, shape):
        return 1.0 + 0.05 * jax.random.normal(k, shape, F32)

    L = DEPTH
    return {
        "x": jax.random.normal(ks[0], (BATCH, SEQ, D_MODEL), F32),
        "mem": jax.random.normal(ks[1], (BATCH, MEM_LEN, D_MODEL), F32),
        "norm_mix": gain(ks[2], (L, D_MODEL)),
        "w_in": nrm(ks[3], (L, D_MODEL, D_IN), D_MODEL),
        "sc_conv_w": nrm(ks[4], (L, SC_KERNEL, SC_WIDTH), SC_KERNEL),
        "w_sb_out": nrm(ks[5], (L, SB_WIDTH, D_MODEL), SB_WIDTH),
        "w_sc_out": nrm(ks[6], (L, SC_WIDTH, D_MODEL), SC_WIDTH),
        "w_dsa_out": nrm(ks[7], (L, DSA_WIDTH, D_MODEL), DSA_WIDTH),
        "w_mix_o": nrm(ks[8], (L, D_MODEL, D_MODEL), D_MODEL),
        "norm_xa": gain(ks[9], (L, D_MODEL)),
        "norm_mem": gain(ks[10], (L, D_MODEL)),
        "w_xa_q": nrm(ks[11], (L, D_MODEL, D_MODEL), D_MODEL),
        "w_xa_kv": nrm(ks[12], (L, D_MODEL, 2 * D_MODEL), D_MODEL),
        "w_xa_o": nrm(ks[13], (L, D_MODEL, D_MODEL), D_MODEL),
        "norm_ffn": gain(ks[14], (L, D_MODEL)),
        "w_ffn_in": nrm(ks[15], (L, D_MODEL, 2 * D_FF), D_MODEL),
        "ffn_conv_w": nrm(ks[16], (L, FFN_KERNEL, D_FF), FFN_KERNEL),
        "ffn_conv_b": 0.02 * jax.random.normal(ks[17], (L, D_FF), F32),
        "w_ffn_down": nrm(ks[18], (L, D_FF, D_MODEL), D_FF),
        "norm_final": gain(ks[19], (D_MODEL,)),
    }

def reference(x, mem, norm_mix, w_in, sc_conv_w, w_sb_out, w_sc_out, w_dsa_out, w_mix_o,
              norm_xa, norm_mem, w_xa_q, w_xa_kv, w_xa_o,
              norm_ffn, w_ffn_in, ffn_conv_w, ffn_conv_b, w_ffn_down, norm_final):
    for l in range(DEPTH):
        h = rmsnorm(x, norm_mix[l])
        x = x + hybrid_mixer(h, w_in[l], sc_conv_w[l], w_sb_out[l], w_sc_out[l], w_dsa_out[l], w_mix_o[l])
        h = rmsnorm(x, norm_xa[l])
        x = x + memory_cross_attention(h, rmsnorm(mem, norm_mem[l]), w_xa_q[l], w_xa_kv[l], w_xa_o[l])
        h = rmsnorm(x, norm_ffn[l])
        x = x + conv_ffn(h, w_ffn_in[l], ffn_conv_w[l], ffn_conv_b[l], w_ffn_down[l])
    return rmsnorm(x, norm_final)


_drawn_inputs = setup_inputs


def setup_inputs(seed=0):
    import zlib

    import numpy as np

    out = dict(_drawn_inputs(seed))
    spreads = {}
    factors = {'norm_xa': 8.0, 'norm_mem': 8.0, 'ffn_conv_b': 33.825, 'norm_ffn': 8.0}
    for name, (base, spread) in spreads.items():
        noise = np.random.default_rng([zlib.crc32(name.encode()), seed]).standard_normal(out[name].shape)
        drawn = base * np.exp(spread * noise) if base else spread * noise
        out[name] = __import__('jax').numpy.asarray(drawn.astype(out[name].dtype))
    for name, factor in factors.items():
        out[name] = (out[name] * factor).astype(out[name].dtype)
    return out
```

```python
from contextlib import ExitStack

import concourse.bass as bass
import numpy as np
from concourse import mybir

F32 = mybir.dt.float32
F32R = mybir.dt.float32r
BF16 = mybir.dt.bfloat16
ACT = mybir.ActivationFunctionType
ALU = mybir.AluOpType
AX = mybir.AxisListType

P = 128
D = 1024
S = 1024
KT = D // P
HALF = 512
WORDS = KT * P
DFF = 2816
FT = DFF // P
EPS = 1e-6
PASSES = ((0, 0), (0, 1), (1, 0))


def cols(half):
    return slice(half * HALF, (half + 1) * HALF)


def sbuf_map(nc):
    base = (nc.sbuf_base + 31) // 32 * 32
    room = (nc.sbuf_usable_end - base) // 4

    def at(name, word, shape, dtype=F32):
        size = int(np.prod(shape[1:])) * (2 if dtype == BF16 else 4)
        assert word * 4 + size <= room * 4, (name, word, size, room)
        return nc.alloc_sbuf_tensor_at(name, shape, dtype, offset=base + word * 4)

    return at


def tile_of(t, n):
    if isinstance(n, int):
        return t[:, n]
    return t[:, bass.ds(n, 1)].rearrange("p a w -> p (a w)")


def item_of(w, n):
    if isinstance(n, int):
        return w[n]
    return w[bass.ds(n, 1)].rearrange("a p w -> p (a w)")


def build_ffn(nc, ctx, at, psum, shared, w_items, conv_w, conv_b, x2_dram, out_dram):
    UP = 2 * FT
    DOWN = FT // 2
    GROUPS = 2
    GM = KT // GROUPS
    x, ssq, gains, ones, eps = (shared[n] for n in ("x", "ssq", "gains", "ones", "eps"))
    g_ffn, g_final = 3 * KT, 4 * KT
    with ExitStack() as scope:
        def sem(name):
            return ctx.enter_context(nc.semaphore("f_" + name))

        act = at("f_act", 0, [P, FT, S])
        h_hi = at("f_h_hi", 22528, [P, KT, S], F32R)
        h_lo = at("f_h_lo", 30720, [P, KT, S], F32R)
        w_stage = at("f_w_stage", 38912, [P, 2, WORDS])
        w_hi = at("f_w_hi", 40960, [P, 2, WORDS], F32R)
        w_lo = at("f_w_lo", 43008, [P, 2, WORDS], F32R)
        rstd = at("f_rstd", 48136, [P, S])
        a_pad = at("f_a_pad", 45056, [P, S + 2])
        conv = at("f_conv", 46088, [P, S])
        gel = at("f_gel", 47112, [P, S])
        x2_ring = at("f_x2_ring", 48136, [P, 2, S])
        cw = at("f_cw", 50184, [P, FT, 3])
        cb = at("f_cb", 50256, [P, FT])
        x3 = at("f_x3", 22528, [P, KT, S])
        k_hi = at("f_k_hi", 30720, [P, 2, S], F32R)
        k_lo = at("f_k_lo", 32768, [P, 2, S], F32R)
        sq = at("f_sq", 34816, [P, 2, HALF])
        y_out = at("f_y_out", 36864, [P, 2, S])
        rstd_y = at("f_rstd_y", 45056, [P, S])
        H = (h_hi, h_lo)
        W = (w_hi, w_lo)
        K = (k_hi, k_lo)

        consts_in = sem("consts_in")
        norm_sum = sem("norm_sum")
        norm_root = sem("norm_root")
        norm_rstd = sem("norm_rstd")
        h_scaled = sem("h_scaled")
        h_hi_done = sem("h_hi_done")
        h_lo_dve = sem("h_lo_dve")
        h_lo_pool = sem("h_lo_pool")
        w_in = [sem(f"w_in{j}") for j in range(2)]
        w_hi_done = sem("w_hi_done")
        w_ready = sem("w_ready")
        halves_done = sem("halves_done")
        bank_free = [sem(f"bank_free{j}") for j in range(2)]
        pad_zero = sem("pad_zero")
        conv_step = sem("conv_step")
        gelu_done = sem("gelu_done")
        k_hi_done = sem("k_hi_done")
        k_ready = sem("k_ready")
        k_done = sem("k_done")
        x3_done = sem("x3_done")
        x2_in = [sem(f"x2_in{j}") for j in range(2)]
        sq_done = sem("sq_done")
        ssq_step = sem("ssq_step")
        ssq_zero = sem("ssq_zero")
        y_done = sem("y_done")
        y_stored = [sem(f"y_stored{j}") for j in range(2)]

        acc_order = [(m, half) for m in (1, 2, 3, 0) for half in range(2)]
        out_order = [g * GM + m for g in range(GROUPS) for m, half in acc_order if half == 0]

        block = scope.enter_context(nc.Block())

        @block.sync
        def _(sp):
            sp.dma_start(cw[:], conv_w).then_inc(consts_in, 16)
            sp.dma_start(cb[:], conv_b).then_inc(consts_in, 16)
            def weights(first, end):
                with sp.Fori(first // 2, end // 2) as i:
                    for j in range(2):
                        sp.wait_ge(w_ready, 2 * i + j + 1)
                        sp.dma_start(w_stage[:, j], item_of(w_items, 2 * i + j)).then_inc(w_in[j], 16)

            def residual(first, end):
                for c in range(first, end):
                    if c >= 2:
                        sp.wait_ge(x3_done, 2 * (c - 1))
                    sp.dma_start(x2_ring[:, c % 2], x2_dram[out_order[c]]).then_inc(x2_in[c % 2], 16)

            weights(0, UP + 2)
            residual(0, 2)
            weights(UP + 2, UP + DOWN + 1)
            residual(2, 6)
            weights(UP + DOWN + 1, UP + GROUPS * DOWN)
            residual(6, 8)
            for m in range(KT):
                sp.wait_ge(y_done, m + 1)
                sp.dma_start(out_dram[m], y_out[:, m % 2]).then_inc(y_stored[m % 2], 16)
            for j in range(2):
                sp.wait_ge(y_stored[j], 16 * KT // 2)

        @block.tensor
        def _(pe):
            pe.sem_inc(halves_done, 4)
            pe.sem_inc(k_done, 2)

            def column_sums():
                for half in range(2):
                    last = nc.tensor.matmul(psum[:, half], ones[:], ssq[:, cols(half)], start=True, stop=True)
                last.then_inc(norm_sum, 1)

            def up_item(n, j, first=False):
                pe.wait_ge(w_ready, n + 3)
                for half in range(2):
                    if not first:
                        pe.wait_ge(bank_free[half], n)
                    for k in range(KT):
                        if first and half == 0:
                            pe.wait_ge(h_lo_pool if k % 2 else h_lo_dve, k // 2 + 1)
                        for a, b in PASSES:
                            last = nc.tensor.matmul(psum[:, half], W[a][:, j, k * P:(k + 1) * P], H[b][:, k, cols(half)],
                                                    start=(k == 0 and (a, b) == (0, 0)), stop=(k == KT - 1 and a == 1))
                    last.then_inc(halves_done, 1)

            column_sums()
            pe.wait_ge(norm_root, 2)
            up_item(0, 0, first=True)
            up_item(1, 1)
            with pe.Fori(1, FT) as f:
                for j in range(2):
                    up_item(2 * f + j, j)

            def down_item(g, i, j, start=False, stop=False):
                for kk in range(2):
                    pe.wait_ge(k_ready, g * FT + 2 * i + kk + 1)
                    if kk == 0:
                        pe.wait_ge(w_ready, UP + g * DOWN + i + 3)
                    for q, (m, half) in enumerate(acc_order):
                        if start and kk == 0 and g == 1:
                            pe.wait_ge(x3_done, q + 1)
                        elif start and kk == 0 and m == 0:
                            pe.wait_ge(bank_free[half], UP)
                        for a, b in PASSES:
                            last = nc.tensor.matmul(psum[:, 2 * m + half], W[a][:, j, (kk * GM + m) * P:(kk * GM + m + 1) * P],
                                                    K[b][:, kk, cols(half)], start=(start and kk == 0 and (a, b) == (0, 0)),
                                                    stop=(stop and kk == 1 and a == 1))
                    last.then_inc(k_done, 1)

            for g in range(GROUPS):
                slot = g * DOWN % 2
                down_item(g, 0, slot, start=True)
                with pe.Fori(0, (DOWN - 3) // 2) as i:
                    down_item(g, 2 * i + 1, 1 - slot)
                    down_item(g, 2 * i + 2, slot)
                down_item(g, DOWN - 2, 1 - slot)
                down_item(g, DOWN - 1, slot, stop=True)
            pe.wait_ge(ssq_step, 2 * KT)
            pe.wait_ge(x3_done, 2 * KT)
            column_sums()

        @block.scalar
        def _(act_e):
            def split_hi(j):
                nc.scalar.activation(w_hi[:, j], w_stage[:, j], ACT.Copy).then_inc(w_hi_done, 1)

            def roots(n, dst):
                act_e.wait_ge(norm_sum, n + 1)
                for half in range(2):
                    nc.scalar.activation(dst[:, cols(half)], psum[:, half], ACT.Sqrt, bias=eps[:], scale=1.0 / D).then_inc(norm_root, 1)

            act_e.wait_ge(w_in[0], 16)
            split_hi(0)
            roots(0, rstd)
            for k in range(KT):
                act_e.wait_ge(h_scaled, k + 1)
                nc.scalar.activation(h_hi[:, k], x[:, k], ACT.Copy).then_inc(h_hi_done, 1)
            act_e.wait_ge(pad_zero, 1)
            with act_e.Fori(0, FT) as f:
                act_e.wait_ge(w_in[1], 16 * f + 16)
                act_e.wait_ge(halves_done, 4 * f + 4)
                split_hi(1)
                act_e.wait_ge(conv_step, 3 * f + 3)
                for half in range(2):
                    act_e.wait_ge(halves_done, 4 * f + half + 5)
                    nc.scalar.activation(a_pad[:, 2 + half * HALF:2 + (half + 1) * HALF], psum[:, half], ACT.Copy).then_inc(bank_free[half], 1)
                act_e.wait_ge(w_in[0], 16 * f + 32)
                act_e.wait_ge(halves_done, 4 * f + 6)
                split_hi(0)
                for half in range(2):
                    act_e.wait_ge(bank_free[half], 2 * f)
                act_e.wait_ge(conv_step, 3 * f + 6)
                nc.scalar.activation(gel[:], conv[:], ACT.Gelu_apprx_tanh).then_inc(gelu_done, 1)
            act_e.wait_ge(halves_done, 4 + 2 * UP)
            for half in range(2):
                act_e.wait_ge(bank_free[half], UP)

            def w_arrived(d, e=0):
                act_e.wait_ge(w_in[d % 2], 16 * ((UP + d) // 2 + 1) + 16 * e)

            def squares(g):
                for q, (m, half) in enumerate(acc_order):
                    n = g * 2 * GM + q
                    act_e.wait_ge(x3_done, n + 1)
                    if n >= 2:
                        act_e.wait_ge(ssq_step, n - 1)
                    nc.scalar.activation(sq[:, n % 2], x3[:, g * GM + m, cols(half)], ACT.Square).then_inc(sq_done, 1)

            def k_tiles(i, used):
                for kk in range(2):
                    act_e.wait_ge(k_done, used + kk)
                    nc.scalar.activation(k_hi[:, kk], tile_of(act, 2 * i + kk), ACT.Copy).then_inc(k_hi_done, 1)

            for g in range(GROUPS):
                if g:
                    w_arrived(DOWN)
                    act_e.wait_ge(k_done, 2 * DOWN)
                    split_hi(DOWN % 2)
                k_tiles(0, 2 * g * DOWN + 1)
                if g:
                    squares(0)
                with act_e.Fori(0, (DOWN - 1) // 2) as e:
                    for o in range(2):
                        d = g * DOWN + o + 1
                        w_arrived(d, e)
                        act_e.wait_ge(k_done, 2 * d + 4 * e)
                        split_hi(d % 2)
                        k_tiles(2 * e + o + 1, 2 * d + 1 + 4 * e)
            squares(1)
            roots(1, rstd_y)

        @block.gpsimd
        def _(pool):
            def split_lo(n, j):
                pool.wait_ge(w_hi_done, n + 1)
                nc.gpsimd.tensor_tensor(w_lo[:, j], w_stage[:, j], w_hi[:, j].bitcast(F32), ALU.subtract).then_inc(w_ready, 1)

            pool.sem_inc(w_ready, 2)
            split_lo(0, 0)
            for k in range(1, KT, 2):
                pool.wait_ge(h_hi_done, k + 1)
                nc.gpsimd.tensor_tensor(h_lo[:, k], x[:, k], h_hi[:, k].bitcast(F32), ALU.subtract).then_inc(h_lo_pool, 1)
            nc.gpsimd.memset(a_pad[:, 0:2], 0.0).then_inc(pad_zero, 1)
            split_lo(1, 1)
            with pool.Fori(1, (UP + GROUPS * DOWN) // 2) as i:
                for j in range(2):
                    split_lo(2 * i + j, j)

        @block.vector
        def _(dve):
            dve.sem_inc(conv_step, 3)

            def reciprocals(n, dst):
                for half in range(2):
                    dve.wait_ge(norm_root, 2 * n + half + 1)
                    nc.vector.reciprocal(dst[:, cols(half)], dst[:, cols(half)]).then_inc(norm_rstd, 1)
                dve.wait_ge(norm_rstd, 2 * n + 2)

            def scale(k):
                nc.vector.scalar_tensor_tensor(x[:, k], x[:, k], gains[:, g_ffn + k:g_ffn + k + 1], rstd[:],
                                               ALU.mult, ALU.mult).then_inc(h_scaled, 1)

            reciprocals(0, rstd)
            nc.vector.memset(ssq[:], 0.0).then_inc(ssq_zero, 1)
            for k in range(0, KT, 2):
                scale(k)
                scale(k + 1)
                dve.wait_ge(h_hi_done, k + 1)
                nc.vector.tensor_tensor(h_lo[:, k], x[:, k], h_hi[:, k].bitcast(F32), ALU.subtract).then_inc(h_lo_dve, 1)
            dve.wait_ge(consts_in, 32)
            dve.wait_ge(h_lo_pool, KT // 2)
            dve.wait_ge(h_lo_dve, KT // 2)

            def tap(w, f):
                return cw[:, bass.ds(f, 1), w:w + 1].rearrange("p a b -> p (a b)")

            with dve.Fori(0, FT) as f:
                for half in range(2):
                    dve.wait_ge(bank_free[half], 2 * f + 1)
                dve.wait_ge(gelu_done, f)
                nc.vector.tensor_scalar(conv[:], a_pad[:, 2:S + 2], tap(2, f), cb[:, bass.ds(f, 1)],
                                        ALU.mult, ALU.add).then_inc(conv_step, 1)
                for w in (1, 0):
                    dve.wait_ge(conv_step, 3 * f + 5 - w)
                    nc.vector.scalar_tensor_tensor(conv[:], a_pad[:, w:S + w], tap(w, f), conv[:],
                                                   ALU.mult, ALU.add).then_inc(conv_step, 1)
                dve.wait_ge(gelu_done, f + 1)
                for half in range(2):
                    dve.wait_ge(halves_done, 4 * f + 7 + half)
                    nc.vector.tensor_tensor(act[:, bass.ds(f, 1), cols(half)].rearrange("p a t -> p (a t)"),
                                            gel[:, cols(half)], psum[:, half], ALU.mult).then_inc(bank_free[half], 1)

            def k_lo_part(i, n):
                for kk in range(2):
                    dve.wait_ge(k_hi_done, n + kk + 1)
                    nc.vector.tensor_tensor(k_lo[:, kk], tile_of(act, 2 * i + kk), k_hi[:, kk].bitcast(F32),
                                            ALU.subtract).then_inc(k_ready, 1)

            def read_out(g):
                dve.wait_ge(k_done, 2 + (g + 1) * FT)
                for q in range(2 * GM + 1):
                    if q < 2 * GM:
                        m, half = acc_order[q]
                        n = g * 2 * GM + q
                        c = n // 2
                        dve.wait_ge(x2_in[c % 2], 16 * (c // 2 + 1))
                        nc.vector.tensor_tensor(x3[:, g * GM + m, cols(half)], psum[:, 2 * m + half],
                                                x2_ring[:, c % 2, cols(half)], ALU.add).then_inc(x3_done, 1)
                    if q:
                        half = acc_order[q - 1][1]
                        n = g * 2 * GM + q - 1
                        dve.wait_ge(sq_done, n + 1)
                        if n >= 2:
                            dve.wait_ge(ssq_step, n - 1)
                        nc.vector.tensor_tensor(ssq[:, cols(half)], ssq[:, cols(half)], sq[:, n % 2], ALU.add).then_inc(ssq_step, 1)

            dve.wait_ge(ssq_zero, 1)
            for g in range(GROUPS):
                k_lo_part(0, g * FT)
                if g:
                    read_out(0)
                with dve.Fori(0, (DOWN - 1) // 2) as e:
                    for o in range(2):
                        k_lo_part(2 * e + o + 1, g * FT + 2 * (o + 1) + 4 * e)
            read_out(1)
            reciprocals(1, rstd_y)
            for m in range(KT):
                if m >= 2:
                    dve.wait_ge(y_stored[m % 2], 16 * (m // 2))
                nc.vector.scalar_tensor_tensor(y_out[:, m % 2], x3[:, m], gains[:, g_final + m:g_final + m + 1], rstd_y[:],
                                               ALU.mult, ALU.mult).then_inc(y_done, 1)


MEM = 256
XA_HEADS = 4
XA_DIM = D // XA_HEADS


def build_cross(nc, ctx, at, psum, shared, w_items, mem_dram, x2_dram):
    x, ssq, gains, ones, ident, eps = (shared[n] for n in ("x", "ssq", "gains", "ones", "ident", "eps"))
    g_xa, g_mem = KT, 2 * KT
    MT = MEM // P
    DT = XA_DIM // P
    QB = HALF // P
    SCALE = XA_DIM ** -0.5
    N_KV = 2 * KT
    N_ITEMS = N_KV + 2 * XA_HEADS + 2 * XA_HEADS
    with ExitStack() as scope:
        def sem(name):
            return ctx.enter_context(nc.semaphore("c_" + name))

        h_hi = at("c_h_hi", 8192, [P, KT, S], F32R)
        h_lo = at("c_h_lo", 16384, [P, KT, S], F32R)
        w_stage = at("c_w_stage", 24576, [P, 2, WORDS])
        w_hi = at("c_w_hi", 26624, [P, 2, WORDS], F32R)
        w_lo = at("c_w_lo", 28672, [P, 2, WORDS], F32R)
        k_hi = at("c_k_hi", 30720, [P, KT, MEM], F32R)
        k_lo = at("c_k_lo", 32768, [P, KT, MEM], F32R)
        v_hi = at("c_v_hi", 34816, [P, MT, D], F32R)
        v_lo = at("c_v_lo", 36864, [P, MT, D], F32R)
        q_hi = at("c_q_hi", 38912, [P, DT, S], F32R)
        q_lo = at("c_q_lo", 40960, [P, DT, S], F32R)
        pt_hi = at("c_pt_hi", 43008, [P, MT, HALF], F32R)
        pt_lo = at("c_pt_lo", 44032, [P, MT, HALF], F32R)
        y_hi = at("c_y_hi", 45056, [P, DT, S], F32R)
        y_lo = at("c_y_lo", 47104, [P, DT, S], F32R)
        p_buf = at("c_p", 49152, [P, 2, QB, MEM])
        stats = at("c_stats", 52600, [P, 4, 2, QB])
        m_hi = at("c_m_hi", 38912, [P, KT, MEM], F32R)
        m_lo = at("c_m_lo", 40960, [P, KT, MEM], F32R)
        m_raw = at("c_m_raw", 43008, [P, KT, MEM])
        m_sq = at("c_m_sq", 45056, [P, KT, MEM])
        m_ssq = at("c_m_ssq", 47104, [P, MEM])
        m_rstd = at("c_m_rstd", 47360, [P, MEM])
        rstd = at("c_rstd", 47616, [P, S])
        h_f32 = at("c_h_f32", 49152, [P, 2, S])
        sq = at("c_sq", 43008, [P, 2, HALF])
        H, W, K, V, Q = (h_hi, h_lo), (w_hi, w_lo), (k_hi, k_lo), (v_hi, v_lo), (q_hi, q_lo)
        PT, Y, M = (pt_hi, pt_lo), (y_hi, y_lo), (m_hi, m_lo)
        ZB, TB, OB = 2, 4, 6

        mem_in = sem("mem_in")
        m_sq_done = sem("m_sq_done")
        m_step = sem("m_step")
        m_sum = sem("m_sum")
        m_root = sem("m_root")
        m_hi_done = sem("m_hi_done")
        m_lo_done = sem("m_lo_done")
        norm_sum = sem("norm_sum")
        norm_root = sem("norm_root")
        norm_rstd = sem("norm_rstd")
        h_scaled = sem("h_scaled")
        h_hi_done = sem("h_hi_done")
        h_lo_dve = sem("h_lo_dve")
        h_lo_pool = sem("h_lo_pool")
        w_in = [sem(f"w_in{j}") for j in range(2)]
        w_hi_done = sem("w_hi_done")
        w_ready = sem("w_ready")
        use_done = sem("use_done")
        use_hi = sem("use_hi")
        use_free = [sem(f"use_free{j}") for j in range(2)]
        v_done = sem("v_done")
        v_hi_done = sem("v_hi_done")
        v_lo_done = sem("v_lo_done")
        z_done = sem("z_done")
        max_done = sem("max_done")
        neg_done = sem("neg_done")
        exp_done = sem("exp_done")
        rec_done = sem("rec_done")
        p_done = sem("p_done")
        t_done = sem("t_done")
        pt_hi_done = sem("pt_hi_done")
        pt_lo_done = sem("pt_lo_done")
        pv_done = sem("pv_done")
        y_hi_done = sem("y_hi_done")
        y_lo_done = sem("y_lo_done")
        sq_done = sem("sq_done")
        ssq_step = sem("ssq_step")
        x_stored = sem("x_stored")

        item_kind = (["k"] * KT + ["v"] * KT + ["q"] * 2
                     + sum((["o"] * 2 * (h > 0) + ["q"] * 2 * (h < XA_HEADS - 1) for h in range(XA_HEADS)), []) + ["o"] * 2)
        assert len(item_kind) == N_ITEMS
        uses = {"k": 1, "v": 0, "q": 2, "o": 8}
        first_use = [sum(uses[c] for c in item_kind[:n]) for n in range(N_ITEMS + 1)]
        q_items = [[n for n in range(N_ITEMS) if item_kind[n] == "q"][2 * h:2 * h + 2] for h in range(XA_HEADS)]
        o_items = [[n for n in range(N_ITEMS) if item_kind[n] == "o"][2 * h:2 * h + 2] for h in range(XA_HEADS)]

        def wait_item_used(eng, n):
            if item_kind[n] == "v":
                eng.wait_ge(v_done, n - KT + 1)
            else:
                eng.wait_ge(use_done, first_use[n + 1])

        def wait_q(eng, h):
            last = first_use[q_items[h][1] + 1]
            for j in range(2):
                eng.wait_ge(use_free[j], last // 2)

        def wait_x2(eng, v):
            u = first_use[o_items[XA_HEADS - 1][0]] + v
            eng.wait_ge(use_free[u % 2], u // 2 + 1)

        block = scope.enter_context(nc.Block())

        @block.sync
        def _(sp):
            sp.dma_start(m_raw[:], mem_dram.rearrange("k p t -> p k t")).then_inc(mem_in, 16)
            for j in range(2):
                sp.dma_start(w_stage[:, j], w_items[j]).then_inc(w_in[j], 16)
            with sp.Fori(1, N_ITEMS // 2) as i:
                for j in range(2):
                    sp.wait_ge(w_ready, 2 * i + j - 1)
                    sp.dma_start(w_stage[:, j], item_of(w_items, 2 * i + j)).then_inc(w_in[j], 16)
            for m in range(KT):
                for half in range(2):
                    wait_x2(sp, 2 * m + half)
                sp.dma_start(x2_dram[m], x[:, m]).then_inc(x_stored, 16)
            sp.wait_ge(x_stored, 16 * KT)

        @block.tensor
        def _(pe):
            def column_sums(bank, width, src, done):
                last = nc.tensor.matmul(psum[:, bank, 0:width], ones[:], src, start=True, stop=True)
                last.then_inc(done, 1)

            def three(out, lhs, rhs, start, stop):
                for a, b in PASSES:
                    last = nc.tensor.matmul(out, lhs(a), rhs(b), start=(start and (a, b) == (0, 0)), stop=(stop and a == 1))
                return last

            for half in range(2):
                column_sums(half, HALF, ssq[:, cols(half)], norm_sum)
            pe.wait_ge(m_step, 1)
            column_sums(ZB, MEM, m_ssq[:], m_sum)

            def wait_use(u):
                if u >= 2:
                    pe.wait_ge(use_free[u % 2], u // 2)

            def wait_item(n):
                pe.wait_ge(w_ready, n + 1)

            pe.wait_ge(norm_root, 2)
            pe.wait_ge(m_lo_done, 1)
            for n in range(KT):
                wait_item(n)
                wait_use(n)
                for k in range(KT):
                    last = three(psum[:, n % 2, 0:MEM], lambda a: W[a][:, n % 2, k * P:(k + 1) * P],
                                 lambda b: M[b][:, k], k == 0, k == KT - 1)
                last.then_inc(use_done, 1)
            pe.wait_ge(m_root, 1)
            for c in range(2):
                for kq in range(KT // 2):
                    n = KT + c * KT // 2 + kq
                    wait_item(n)
                    for kk in range(2):
                        k = 2 * kq + kk
                        for mt in range(MT):
                            for a, b in PASSES:
                                last = nc.tensor.matmul(psum[:, ZB + 2 * c + mt], M[b][:, k, mt * P:(mt + 1) * P],
                                                        W[a][:, n % 2, kk * HALF:(kk + 1) * HALF],
                                                        start=(k == 0 and (a, b) == (0, 0)), stop=(k == KT - 1 and a == 1))
                    last.then_inc(v_done, 1)

            def q_item(h, i):
                n = q_items[h][i]
                wait_item(n)
                for half in range(2):
                    wait_use(first_use[n] + half)
                    for k in range(KT):
                        if h == 0 and i == 0 and half == 0:
                            pe.wait_ge(h_lo_pool if k % 2 else h_lo_dve, k // 2 + 1)
                        last = three(psum[:, half], lambda a: W[a][:, n % 2, k * P:(k + 1) * P],
                                     lambda b: H[b][:, k, cols(half)], k == 0, k == KT - 1)
                    last.then_inc(use_done, 1)

            def o_item(h, i):
                n = o_items[h][i]
                wait_item(n)
                if i == 0:
                    pe.wait_ge(y_lo_done, 4 * h + 4)
                for m in range(KT // 2):
                    for half in range(2):
                        wait_use(first_use[n] + 2 * m + half)
                        for kk in range(DT):
                            last = three(psum[:, half], lambda a: W[a][:, n % 2, (kk * 4 + m) * P:(kk * 4 + m + 1) * P],
                                         lambda b: Y[b][:, kk, cols(half)], kk == 0, kk == DT - 1)
                        last.then_inc(use_done, 1)

            def logits(h, half):
                s = 2 * h + half
                if half == 0:
                    wait_q(pe, h)
                if s:
                    pe.wait_ge(exp_done, QB * s)
                else:
                    pe.wait_ge(v_lo_done, 4)
                for qb in range(QB):
                    for kt in range(DT):
                        last = three(psum[:, ZB + qb // 2, qb % 2 * MEM:(qb % 2 + 1) * MEM],
                                     lambda a: Q[a][:, kt, half * HALF + qb * P:half * HALF + (qb + 1) * P],
                                     lambda b: K[b][:, DT * h + kt], kt == 0, kt == DT - 1)
                last.then_inc(z_done, 1)

            def transposes(h, half):
                s = 2 * h + half
                pe.wait_ge(p_done, s + 1)
                if s:
                    pe.wait_ge(pt_lo_done, 2 * s)
                for mt in range(MT):
                    for qb in range(QB):
                        last = nc.tensor.transpose(psum[:, TB + mt, qb * P:(qb + 1) * P],
                                                   p_buf[:, s % 2, qb, mt * P:(mt + 1) * P], ident[:])
                last.then_inc(t_done, 1)

            def values(h, half):
                s = 2 * h + half
                pe.wait_ge(pt_lo_done, 2 * s + 2)
                if s:
                    pe.wait_ge(y_lo_done, 2 * s)
                for dt in range(DT):
                    for mt in range(MT):
                        at_v = h * XA_DIM + dt * P
                        last = three(psum[:, OB + dt], lambda a: V[a][:, mt, at_v:at_v + P],
                                     lambda b: PT[b][:, mt], mt == 0, mt == MT - 1)
                last.then_inc(pv_done, 1)

            for i in range(DT):
                q_item(0, i)
            for h in range(XA_HEADS):
                logits(h, 0)
                if h:
                    for i in range(2):
                        o_item(h - 1, i)
                transposes(h, 0)
                logits(h, 1)
                values(h, 0)
                if h < XA_HEADS - 1:
                    for i in range(DT):
                        q_item(h + 1, i)
                transposes(h, 1)
                values(h, 1)
            for i in range(2):
                o_item(XA_HEADS - 1, i)

        @block.scalar
        def _(act_e):
            def split_hi(n):
                if n < N_ITEMS:
                    act_e.wait_ge(w_in[n % 2], 16 * (n // 2 + 1))
                    if n >= 2:
                        wait_item_used(act_e, n - 2)
                    nc.scalar.activation(w_hi[:, n % 2], w_stage[:, n % 2], ACT.Copy).then_inc(w_hi_done, 1)

            split_hi(0)
            act_e.wait_ge(norm_sum, 2)
            for half in range(2):
                nc.scalar.activation(rstd[:, cols(half)], psum[:, half], ACT.Sqrt, bias=eps[:], scale=1.0 / D).then_inc(norm_root, 1)
            act_e.wait_ge(mem_in, 16)
            nc.scalar.activation(m_sq[:], m_raw[:], ACT.Square).then_inc(m_sq_done, 1)
            act_e.wait_ge(m_sum, 1)
            nc.scalar.activation(m_rstd[:], psum[:, ZB, 0:MEM], ACT.Sqrt, bias=eps[:], scale=1.0 / D).then_inc(m_root, 1)
            act_e.wait_ge(m_step, 2 + KT)
            nc.scalar.activation(m_hi[:], m_raw[:], ACT.Copy).then_inc(m_hi_done, 1)

            def h_hi_part(k):
                act_e.wait_ge(h_scaled, k + 1)
                nc.scalar.activation(h_hi[:, k], h_f32[:, k % 2], ACT.Copy).then_inc(h_hi_done, 1)

            for n in range(KT):
                split_hi(n + 1)
                act_e.wait_ge(use_done, n + 1)
                nc.scalar.activation(k_hi[:, n], psum[:, n % 2, 0:MEM], ACT.Copy).then_inc(use_hi, 1)
                h_hi_part(n)
            for c in range(2):
                for kq in range(KT // 2):
                    n = KT + c * KT // 2 + kq
                    split_hi(n + 1)
                act_e.wait_ge(v_done, (c + 1) * KT // 2)
                for mt in range(MT):
                    nc.scalar.activation(v_hi[:, mt, cols(c)], psum[:, ZB + 2 * c + mt], ACT.Copy).then_inc(v_hi_done, 1)

            def q_part(h, i):
                n = q_items[h][i]
                split_hi(n + 1)
                for half in range(2):
                    act_e.wait_ge(use_done, first_use[n] + half + 1)
                    if h:
                        act_e.wait_ge(z_done, 2 * h)
                    nc.scalar.activation(q_hi[:, i, cols(half)], psum[:, half], ACT.Copy).then_inc(use_hi, 1)

            def exps(h, half):
                s = 2 * h + half
                act_e.wait_ge(neg_done, s + 1)
                if s >= 2:
                    act_e.wait_ge(t_done, s - 1)
                for qb in range(QB):
                    nc.scalar.activation(p_buf[:, s % 2, qb], psum[:, ZB + qb // 2, qb % 2 * MEM:(qb % 2 + 1) * MEM], ACT.Exp,
                                         bias=stats[:, 1, s % 2, qb:qb + 1], scale=SCALE,
                                         accum_out=stats[:, 2, s % 2, qb:qb + 1]).then_inc(exp_done, 1)

            def pt_part(h, half):
                s = 2 * h + half
                act_e.wait_ge(t_done, s + 1)
                if s:
                    act_e.wait_ge(pv_done, s)
                for mt in range(MT):
                    nc.scalar.activation(pt_hi[:, mt], psum[:, TB + mt], ACT.Copy).then_inc(pt_hi_done, 1)

            def y_part(h, half):
                s = 2 * h + half
                act_e.wait_ge(pv_done, s + 1)
                if h and half == 0:
                    wait_item_used(act_e, o_items[h - 1][1])
                for dt in range(DT):
                    nc.scalar.activation(y_hi[:, dt, cols(half)], psum[:, OB + dt], ACT.Copy).then_inc(y_hi_done, 1)

            for i in range(DT):
                q_part(0, i)
            for h in range(XA_HEADS):
                exps(h, 0)
                if h:
                    for n in o_items[h - 1]:
                        split_hi(n + 1)
                pt_part(h, 0)
                exps(h, 1)
                y_part(h, 0)
                if h < XA_HEADS - 1:
                    for i in range(DT):
                        q_part(h + 1, i)
                else:
                    pass
                pt_part(h, 1)
                y_part(h, 1)
            split_hi(o_items[XA_HEADS - 1][0] + 1)
            for u in range(2 * KT):
                wait_x2(act_e, u)
                if u >= 2:
                    act_e.wait_ge(ssq_step, u - 1)
                else:
                    act_e.wait_ge(pt_lo_done, 4 * XA_HEADS)
                    act_e.wait_ge(pv_done, 2 * XA_HEADS)
                nc.scalar.activation(sq[:, u % 2], x[:, u // 2, cols(u % 2)], ACT.Square).then_inc(sq_done, 1)

        @block.gpsimd
        def _(pool):
            def split_lo(n, j):
                pool.wait_ge(w_hi_done, n + 1)
                nc.gpsimd.tensor_tensor(w_lo[:, j], w_stage[:, j], w_hi[:, j].bitcast(F32), ALU.subtract).then_inc(w_ready, 1)

            for n in range(KT):
                split_lo(n, n % 2)
                if n % 2:
                    pool.wait_ge(h_hi_done, n + 1)
                    nc.gpsimd.tensor_tensor(h_lo[:, n], h_f32[:, n % 2], h_hi[:, n].bitcast(F32), ALU.subtract).then_inc(h_lo_pool, 1)
            with pool.Fori(KT // 2, N_ITEMS // 2) as i:
                for j in range(2):
                    split_lo(2 * i + j, j)

        @block.vector
        def _(dve):
            def free(ins, u):
                ins.then_inc(use_free[u % 2], 1)

            for half in range(2):
                dve.wait_ge(norm_root, half + 1)
                nc.vector.reciprocal(rstd[:, cols(half)], rstd[:, cols(half)]).then_inc(norm_rstd, 1)
            dve.wait_ge(m_sq_done, 1)
            nc.vector.tensor_reduce(m_ssq[:], m_sq[:].rearrange("p k t -> p t k"), AX.X, ALU.add).then_inc(m_step, 1)
            nc.vector.memset(ssq[:], 0.0).then_inc(ssq_step, 1)
            dve.wait_ge(m_root, 1)
            nc.vector.reciprocal(m_rstd[:], m_rstd[:]).then_inc(m_step, 1)
            dve.wait_ge(m_step, 2)
            for k in range(KT):
                nc.vector.scalar_tensor_tensor(m_raw[:, k], m_raw[:, k], gains[:, g_mem + k:g_mem + k + 1], m_rstd[:],
                                               ALU.mult, ALU.mult).then_inc(m_step, 1)
            dve.wait_ge(m_hi_done, 1)
            nc.vector.tensor_tensor(m_lo[:], m_raw[:], m_hi[:].bitcast(F32), ALU.subtract).then_inc(m_lo_done, 1)
            dve.wait_ge(norm_rstd, 2)

            def h_scale(k):
                if k >= 2:
                    dve.wait_ge(h_lo_pool if k % 2 else h_lo_dve, k // 2)
                nc.vector.scalar_tensor_tensor(h_f32[:, k % 2], x[:, k], gains[:, g_xa + k:g_xa + k + 1], rstd[:],
                                               ALU.mult, ALU.mult).then_inc(h_scaled, 1)

            h_scale(0)
            for n in range(KT):
                dve.wait_ge(use_hi, n + 1)
                free(nc.vector.tensor_tensor(k_lo[:, n], psum[:, n % 2, 0:MEM], k_hi[:, n].bitcast(F32), ALU.subtract), n)
                if n % 2 == 0:
                    dve.wait_ge(h_hi_done, n + 1)
                    nc.vector.tensor_tensor(h_lo[:, n], h_f32[:, 0], h_hi[:, n].bitcast(F32), ALU.subtract).then_inc(h_lo_dve, 1)
                if n + 1 < KT:
                    h_scale(n + 1)
            for c in range(2):
                for mt in range(MT):
                    dve.wait_ge(v_hi_done, 2 * c + mt + 1)
                    nc.vector.tensor_tensor(v_lo[:, mt, cols(c)], psum[:, ZB + 2 * c + mt], v_hi[:, mt, cols(c)].bitcast(F32),
                                            ALU.subtract).then_inc(v_lo_done, 1)

            def q_part(h, i):
                u = first_use[q_items[h][i]]
                taken = KT + 4 * h + 2 * i
                for half in range(2):
                    dve.wait_ge(use_hi, taken + half + 1)
                    free(nc.vector.tensor_tensor(q_lo[:, i, cols(half)], psum[:, half], q_hi[:, i, cols(half)].bitcast(F32),
                                                 ALU.subtract), u + half)

            def z_step(h, half):
                s = 2 * h + half
                z = psum[:, ZB:ZB + 2, :].rearrange("p b (q m) -> p (b q) m", m=MEM)
                dve.wait_ge(z_done, s + 1)
                nc.vector.tensor_reduce(stats[:, 0, s % 2], z, AX.X, ALU.max).then_inc(max_done, 1)
                dve.wait_ge(max_done, s + 1)
                nc.vector.tensor_scalar(stats[:, 1, s % 2], stats[:, 0, s % 2], -SCALE, None, ALU.mult).then_inc(neg_done, 1)
                dve.wait_ge(exp_done, QB * (s + 1))
                nc.vector.reciprocal(stats[:, 3, s % 2], stats[:, 2, s % 2]).then_inc(rec_done, 1)
                dve.wait_ge(rec_done, s + 1)
                nc.vector.tensor_tensor(p_buf[:, s % 2], p_buf[:, s % 2],
                                        stats[:, 3, s % 2].unsqueeze(2).to_broadcast([P, QB, MEM]), ALU.mult).then_inc(p_done, 1)

            def pt_part(h, half):
                s = 2 * h + half
                for mt in range(MT):
                    dve.wait_ge(pt_hi_done, 2 * s + mt + 1)
                    nc.vector.tensor_tensor(pt_lo[:, mt], psum[:, TB + mt], pt_hi[:, mt].bitcast(F32), ALU.subtract).then_inc(pt_lo_done, 1)

            def y_part(h, half):
                s = 2 * h + half
                for dt in range(DT):
                    dve.wait_ge(y_hi_done, 2 * s + dt + 1)
                    nc.vector.tensor_tensor(y_lo[:, dt, cols(half)], psum[:, OB + dt], y_hi[:, dt, cols(half)].bitcast(F32),
                                            ALU.subtract).then_inc(y_lo_done, 1)

            def o_part(h, i):
                n = o_items[h][i]
                for q in range(8):
                    u = first_use[n] + q
                    dve.wait_ge(use_done, u + 1)
                    dst = x[:, 4 * i + q // 2, cols(q % 2)]
                    ins = nc.vector.tensor_tensor(dst, dst, psum[:, q % 2], ALU.add)
                    free(ins, u)
                    if h == XA_HEADS - 1 and 8 * i + q:
                        add_square(8 * i + q - 1)

            def add_square(u):
                dve.wait_ge(sq_done, u + 1)
                dve.wait_ge(ssq_step, max(u, 1))
                nc.vector.tensor_tensor(ssq[:, cols(u % 2)], ssq[:, cols(u % 2)], sq[:, u % 2], ALU.add).then_inc(ssq_step, 1)

            for i in range(DT):
                q_part(0, i)
            for h in range(XA_HEADS):
                z_step(h, 0)
                if h:
                    for i in range(2):
                        o_part(h - 1, i)
                pt_part(h, 0)
                z_step(h, 1)
                y_part(h, 0)
                if h < XA_HEADS - 1:
                    for i in range(DT):
                        q_part(h + 1, i)
                pt_part(h, 1)
                y_part(h, 1)
            for i in range(2):
                o_part(XA_HEADS - 1, i)
            add_square(2 * KT - 1)


HEADS = 8
HD = 64
PAIRS = HEADS // 2
SC = 512
BT = SC // P
QT = S // P
TOPK = 256
FULL = TOPK // P
NEG = -1e30
NOT_CAUSAL = -2e38
TAKEN = -3e38


def build_mixer(nc, ctx, at, psum, shared, w_items, x_dram, wi_dram, taps_dram, spill, merged_dram, yc_dram):
    x, ssq, gains, ones, ident, eps = (shared[n] for n in ("x", "ssq", "gains", "ones", "ident", "eps"))
    I_IDX = 0
    I_CONV = I_IDX + BT + 1
    I_A = I_CONV + 3 * BT
    I_C0 = I_A + 3 * PAIRS
    N_C0 = 4
    I_BM = I_C0 + N_C0
    I_C1 = I_BM + 2 * KT
    I_AM = I_C1 + 3 * PAIRS - N_C0
    I_CM = I_AM + 2 * KT
    I_MIX = I_CM + 2 * KT
    N_ITEMS = I_MIX + KT
    assert I_C1 - I_A - 3 * PAIRS == N_C0 + 2 * KT and 3 * PAIRS - N_C0 == 2 * PAIRS
    STEPS = 2 * QT
    SCALE = HD ** -0.5
    LAG = 2

    def groups(i):
        n = i // 2 + 1
        return [(t, min(4, n - t)) for t in range(0, n, 4)]

    VG = 2
    g_base = [VG + sum(len(groups(j)) for j in range(i)) for i in range(STEPS + 1)]
    NG = g_base[STEPS]
    assert NG % 2 == 0
    FILL_A = {-1: [(0, 0)], 2: [(0, 1)], 4: [(1, 0)], 16: [(1, 1)]}
    FILL_C = {-1: [(0, 0)], 2: [(0, 1)], 4: [(1, 0), (1, 1)], 6: [(2, 0)], 9: [(2, 1)], 12: [(3, 0)], 16: [(3, 1)]}

    with ExitStack() as scope:
        def sem(name):
            return ctx.enter_context(nc.semaphore("m_" + name))

        h_hi = at("m_h_hi", 8192, [P, KT, S], F32R)
        h_lo = at("m_h_lo", 16384, [P, KT, S], F32R)
        w_hi = at("m_w_hi", 24576, [P, 2, WORDS], F32R)
        w_lo = at("m_w_lo", 26624, [P, 2, WORDS], F32R)
        y_hi = at("m_y_hi", 28672, [P, BT, S], F32R)
        y_lo = at("m_y_lo", 32768, [P, BT, S], F32R)
        q_hi = at("m_q_hi", 36864, [P, S], F32R)
        q_lo = at("m_q_lo", 37888, [P, S], F32R)
        k_hi = at("m_k_hi", 38912, [P, S], F32R)
        k_lo = at("m_k_lo", 39936, [P, S], F32R)
        v_hi = at("m_v_hi", 40960, [P, QT, 3 * HD], F32R)
        v_lo = at("m_v_lo", 42496, [P, QT, 3 * HD], F32R)
        t_hi = at("m_t_hi", 44032, [P, 2, HALF], F32R)
        t_lo = at("m_t_lo", 45056, [P, 2, HALF], F32R)
        w_stage = at("m_w_stage", 46080, [P, 2, WORDS])
        v_stage = at("m_v_stage", 48128, [P, S])
        small = at("m_small", 52528, [P, 232])
        bias_at = [52768, 52832, 52960, 49152, 49408, 49728, 50112, 50560]
        bias = [at(f"m_bias{qb}", bias_at[qb], [P, (qb + 1) * P], BF16) for qb in range(QT)]
        est = at("m_est", 51200, [P, 2, HALF])
        iq_hi, iq_lo = y_hi, y_lo
        ik_hi = at("m_ik_hi", 36864, [P, S], F32R)
        ik_lo = at("m_ik_lo", 37888, [P, S], F32R)
        wi = at("m_wi", 38912, [P, KT, HEADS])
        wi_hi = at("m_wi_hi", 38976, [P, KT, HEADS], F32R)
        wi_lo = at("m_wi_lo", 39040, [P, KT, HEADS], F32R)
        score_at = {qb: sum((b + 1) * P for b in range(FULL, qb)) for qb in range(FULL, QT)}
        score = {qb: at(f"m_score{qb}", score_at[qb], [P, (qb + 1) * P]) for qb in range(FULL, QT)}
        relu = at("m_relu", 4224, [P, 2, S])
        norm_sq = at("m_norm_sq", 28672, [P, 2, S])
        rstd = at("m_rstd", 30720, [P, S])
        u_pad = at("m_u_pad", 4224, [P, S + 2])
        c_buf = at("m_c_buf", 5256, [P, S])
        x_buf = at("m_x_buf", 6280, [P, S])
        c_acc = v_stage
        b_buf = at("m_b_buf", 51200, [P, S])
        proj = at("m_proj", 5120, [P, 2, HALF])
        gate = at("m_gate", 6144, [P, 2, HALF])
        prev = at("m_prev", 7168, [P, 2, HALF])
        q_stage = at("m_q_stage", 0, [P, S])
        k_stage = at("m_k_stage", 1024, [P, S])
        p_buf = at("m_p_buf", 2048, [P, 3, S])
        r_buf = at("m_r_buf", 5120, [P, 2, S + 8])
        yc_at = [0, 1024, 48128, 4096 + 1024]
        yc = [at("m_yc0", 0, [P, S]), at("m_yc1", 1024, [P, S]), at("m_yc2", 48128, [P, S]), at("m_yc3", 7168, [P, S])]
        m_far = at("m_m_far", 0, [P, KT // 2, S])
        m_hi = at("m_m_hi", 36864, [P, KT // 2, S], F32R)
        m_lo = at("m_m_lo", 40960, [P, KT // 2, S], F32R)
        n_hi = at("m_n_hi", 8192, [P, KT // 2, S], F32R)
        n_lo = at("m_n_lo", 12288, [P, KT // 2, S], F32R)
        x_again = at("m_x_again", 16384, [P, KT, S])
        mix_sq = at("m_mix_sq", 45056, [P, 2, HALF])
        taps = small[:, 0:12]
        top8 = small[:, 16:24]
        wi_q = small[:, 24:88]
        stats = small[:, 88:96]
        H, W, Y = (h_hi, h_lo), (w_hi, w_lo), (y_hi, y_lo)
        IQ, IK, WI = (iq_hi, iq_lo), (ik_hi, ik_lo), (wi_hi, wi_lo)
        Q, K, V, T = (q_hi, q_lo), (k_hi, k_lo), (v_hi, v_lo), (t_hi, t_lo)
        ZB, TB, OB = 2, 4, 6

        x_in = [sem(f"x_in{j}") for j in range(4)]
        consts_in = sem("consts_in")
        const_set = sem("const_set")
        norm_sq_done = sem("norm_sq_done")
        ssq_step = sem("ssq_step")
        norm_sum = sem("norm_sum")
        norm_root = sem("norm_root")
        norm_rstd = sem("norm_rstd")
        h_scaled = sem("h_scaled")
        h_hi_done = sem("h_hi_done")
        h_lo_dve = sem("h_lo_dve")
        h_lo_pool = sem("h_lo_pool")
        w_in = [sem(f"w_in{j}") for j in range(2)]
        w_hi_done = sem("w_hi_done")
        w_ready = sem("w_ready")
        halves_done = sem("halves_done")
        bank_free = [sem(f"bank_free{j}") for j in range(2)]
        idx_hi = sem("idx_hi")
        wi_hi_done = sem("wi_hi_done")
        wi_lo_done = sem("wi_lo_done")
        wi_sum = sem("wi_sum")
        wi_done = sem("wi_done")
        iz_done = sem("iz_done")
        relu_done = sem("relu_done")
        score_step = sem("score_step")
        masked = sem("masked")
        topk_step = sem("topk_step")
        bias_done = sem("bias_done")
        bias_first = sem("bias_first")
        c_act = sem("c_act")
        c_pool = sem("c_pool")
        spilled = [sem(f"spilled{j}") for j in range(2)]
        gate_done = sem("gate_done")
        proj_done = sem("proj_done")
        merge_mult = sem("merge_mult")
        merge_done = sem("merge_done")
        prev_in = [sem(f"prev_in{j}") for j in range(2)]
        merged_out = [sem(f"merged_out{j}") for j in range(2)]
        q_in, k_in, v_in = sem("q_in"), sem("k_in"), sem("v_in")
        qk_hi_done = sem("qk_hi_done")
        qk_lo_done = sem("qk_lo_done")
        z_done = sem("z_done")
        sig_done = sem("sig_done")
        sel_done = sem("sel_done")
        scan_done = sem("scan_done")
        p_done = sem("p_done")
        t_done = sem("t_done")
        t_hi_done = sem("t_hi_done")
        t_lo_done = sem("t_lo_done")
        pv_done = sem("pv_done")
        o_hi_done = sem("o_hi_done")
        o_free = [sem(f"o_free{j}") for j in range(2)]
        add_done = sem("add_done")
        max_done = sem("max_done")
        neg_done = sem("neg_done")
        exp_done = sem("exp_done")
        rec_done = sem("rec_done")
        yc_in = sem("yc_in")
        yc_hi_done = sem("yc_hi_done")
        yc_lo_done = sem("yc_lo_done")
        m_hi_done = sem("m_hi_done")
        m_lo_done = sem("m_lo_done")
        n_hi_done = sem("n_hi_done")
        n_lo_done = sem("n_lo_done")
        x_again_in = sem("x_again_in")
        mix_sq_done = sem("mix_sq_done")
        mix_ssq = sem("mix_ssq")
        dve_passed, pool_passed = sem("dve_passed"), sem("pool_passed")

        def v_place(v, r):
            return v[:, 4 * r:4 * r + 4].rearrange("p s (c d) -> p s c d", c=3)[:, :, 0:3:2]

        def v_bank(r):
            return psum[:, TB + r].rearrange("p (s c d) -> p s c d", s=4, c=2)

        FIRST_SCORES = (QT - FULL) * HEADS
        SPILLS = 6 * PAIRS

        block = scope.enter_context(nc.Block())

        @block.sync
        def _(sp):
            for j in range(4):
                sp.dma_start(x[:, 2 * j:2 * j + 2], x_dram[2 * j:2 * j + 2].rearrange("k p t -> p k t")).then_inc(x_in[j], 16)
            sp.dma_start(wi[:], wi_dram).then_inc(consts_in, 16)
            sp.dma_start(taps, taps_dram).then_inc(consts_in, 16)
            sp.dma_start(gains[:], shared["gains_dram"]).then_inc(consts_in, 16)

            def weight(n, slot, words=WORDS):
                sp.wait_ge(w_ready, n + 1)
                sp.dma_start(w_stage[:, slot, 0:words], item_of(w_items, n)[:, 0:words]).then_inc(w_in[slot], 16)

            def store_merged(m, merged=merge_done):
                for half in range(2):
                    sp.wait_ge(merged, 2 * m + half + 1)
                    sp.dma_start(item_of(merged_dram, m)[:, cols(half)], gate[:, half]).then_inc(merged_out[half], 16)

            weight(0, 0)
            with sp.Fori(0, (I_BM - 1) // 2) as i:
                for o in range(2):
                    weight(2 * i + o + 1, 1 - o)
            weight(I_BM, I_BM % 2)
            weight(I_BM + 1, 1 - I_BM % 2, HALF)
            with sp.Fori(0, KT - 1) as m:
                weight(2 * m + I_BM + 2, I_BM % 2)
                weight(2 * m + I_BM + 3, 1 - I_BM % 2, HALF)
                store_merged(m, merge_mult)
            weight(I_C1, I_C1 % 2)
            store_merged(KT - 1, merge_mult)

            def qkv(g):
                for c, (dst, done) in enumerate(((q_stage, q_in), (k_stage, k_in), (v_stage, v_in))):
                    if c == 0:
                        sp.wait_ge(qk_lo_done, 2 * g)
                    if c == 2:
                        sp.wait_ge(t_done, NG * (g - 1) + VG if not isinstance(g, int) or g else 0)
                    sp.dma_start(dst[:], item_of(spill, 3 * g + c)).then_inc(done, 16)

            for half in range(2):
                sp.wait_ge(spilled[half], 16 * 3 * PAIRS)
            sp.wait_ge(bias_done, QT - FULL)
            sp.wait_ge(bias_first, FULL)
            qkv(0)
            with sp.Fori(1, PAIRS) as p:
                for o in range(2):
                    weight(2 * p + I_C1 - 1 + o, (I_C1 + 1 + o) % 2)
                qkv(p)
            for o in range(2):
                weight(I_AM - 1 + o, (I_AM + 1 + o) % 2)
            for half in range(2):
                sp.wait_ge(spilled[half], 16 * SPILLS)

            def merge_loads(m, base):
                for half in range(2):
                    sp.wait_ge(merge_done, 2 * m)
                    sp.dma_start(prev[:, half], item_of(merged_dram, m)[:, cols(half)]).then_inc(prev_in[half], 16)
                weight(base + 1, 1 - I_AM % 2, HALF)
                weight(base + 2, I_AM % 2)

            sp.wait_ge(merged_out[0], 16 * KT)
            sp.wait_ge(merged_out[1], 16 * KT)
            qkv(PAIRS)
            sp.wait_ge(p_done, STEPS * PAIRS)
            with sp.Fori(1, PAIRS) as p:
                merge_loads(2 * p - 2, 4 * p + I_AM - 4)
                store_merged(2 * p - 2)
                qkv(p + PAIRS)
                merge_loads(2 * p - 1, 4 * p + I_AM - 2)
                store_merged(2 * p - 1)
            for m in range(KT - 2, KT):
                merge_loads(m, I_AM + 2 * m)
                store_merged(m)
            for half in range(2):
                sp.wait_ge(spilled[half], 16 * (SPILLS + PAIRS))
                sp.wait_ge(merged_out[half], 16 * 2 * KT)
            for k in range(BT):
                sp.dma_start(yc[k][:], yc_dram[k]).then_inc(yc_in, 16)
            weight(I_CM + 1, 1 - I_CM % 2, HALF)
            sp.wait_ge(yc_lo_done, BT)

            def prev_load(m):
                for half in range(2):
                    sp.wait_ge(merge_done, 2 * KT + 2 * m)
                    sp.dma_start(prev[:, half], item_of(merged_dram, m)[:, cols(half)]).then_inc(prev_in[half], 16)

            prev_load(0)
            with sp.Fori(1, KT) as m:
                weight(2 * m + I_CM, I_CM % 2)
                weight(2 * m + I_CM + 1, 1 - I_CM % 2, HALF)
                prev_load(m)
            sp.wait_ge(halves_done, 4 + 2 * (I_MIX - 1))
            for m in range(KT):
                sp.dma_start(x_again[:, m], x_dram[m]).then_inc(x_again_in, 16)
            with sp.Fori(0, KT // 2) as i:
                for o in range(2):
                    weight(2 * i + I_MIX + o, (I_MIX + o) % 2)

        @block.tensor
        def _(pe):
            def three(out, lhs, rhs, start, stop):
                for a, b in PASSES:
                    last = nc.tensor.matmul(out, lhs(a), rhs(b), start=(start and (a, b) == (0, 0)), stop=(stop and a == 1))
                return last

            def item_half(n, slot, half, tiles, src, ready=None):
                if half == 0:
                    pe.wait_ge(w_ready, n + 3)
                pe.wait_ge(bank_free[half], n)
                for k in range(tiles):
                    if ready:
                        ready(k)
                    last = three(psum[:, half], lambda a: W[a][:, slot, k * P:(k + 1) * P],
                                 lambda b: src(b, k)[:, cols(half)], k == 0, k == tiles - 1)
                last.then_inc(halves_done, 1)

            def of_h(b, k):
                return H[b][:, k]

            def of_y(b, k):
                return Y[b][:, k]

            def h_ready(k):
                pe.wait_ge(h_lo_pool if k % 2 else h_lo_dve, k // 2 + 1)

            pe.sem_inc(halves_done, 4)
            pe.sem_inc(pv_done, 2)
            pe.wait_ge(ssq_step, KT)
            pe.wait_ge(const_set, 2)
            for half in range(2):
                last = nc.tensor.matmul(psum[:, half], ones[:], ssq[:, cols(half)], start=True, stop=True)
            last.then_inc(norm_sum, 1)
            pe.wait_ge(norm_root, 2)
            item_half(0, 0, 0, KT, of_h, h_ready)
            item_half(0, 0, 1, KT, of_h)
            for n in range(1, I_CONV):
                for half in range(2):
                    item_half(n, n % 2, half, KT, of_h)
            pe.wait_ge(wi_lo_done, 1)
            for t in range(QT):
                for k in range(KT):
                    for a, b in PASSES:
                        last = nc.tensor.matmul(psum[:, OB, t * HEADS:(t + 1) * HEADS], H[b][:, k, t * P:(t + 1) * P], WI[a][:, k],
                                                start=(k == 0 and (a, b) == (0, 0)), stop=(k == KT - 1 and a == 1))
            last.then_inc(wi_sum, 1)
            for half in range(2):
                pe.wait_ge(bank_free[half], I_CONV)
            s = 0
            for qb in range(FULL, QT):
                width = (qb + 1) * P
                for h in range(HEADS):
                    lanes = slice(h % 2 * HD, h % 2 * HD + HD)
                    if s >= 2:
                        pe.wait_ge(relu_done, s - 1)
                    for c in range(0, width, HALF):
                        w = min(HALF, width - c)
                        last = three(psum[:, ZB + 2 * (s % 2) + c // HALF, 0:w], lambda a: IQ[a][lanes, h // 2, qb * P:(qb + 1) * P],
                                     lambda b: IK[b][lanes, c:c + w], True, True)
                    last.then_inc(iz_done, 1)
                    s += 1
            with pe.Fori(0, (I_BM - I_CONV) // 2) as i:
                for o in range(2):
                    for half in range(2):
                        item_half(2 * i + I_CONV + o, (I_CONV + o) % 2, half, KT, of_h)
            pe.wait_ge(c_pool, 5 * BT)
            with pe.Fori(0, KT) as m:
                for o, (tiles, src) in enumerate(((KT, of_h), (BT, of_y))):
                    for half in range(2):
                        item_half(2 * m + I_BM + o, (I_BM + o) % 2, half, tiles, src)

            def v_transposes(g):
                pe.wait_ge(v_in, 16 * g + 16)
                for r in range(VG):
                    pe.wait_ge(t_lo_done, NG * g + r + 1)
                    for st in range(4):
                        last = nc.tensor.transpose(psum[:, TB + r, st * P:(st + 1) * P],
                                                   v_stage[:, (4 * r + st) * P:(4 * r + st + 1) * P], ident[:])
                    last.then_inc(t_done, 1)

            def logits(i):
                qb, h = i // 2, i % 2
                lanes = slice(h * HD, h * HD + HD)
                width = (qb + 1) * P
                for c in range(0, width, HALF):
                    w = min(HALF, width - c)
                    last = three(psum[:, ZB + c // HALF, 0:w], lambda a: Q[a][lanes, qb * P:(qb + 1) * P],
                                 lambda b: K[b][lanes, c:c + w], True, True)
                last.then_inc(z_done, 1)

            def transposes(g, i, left):
                pe.wait_ge(p_done, STEPS * g + i + 1)
                for r, (t0, count) in enumerate(groups(i)):
                    e = g_base[i] + r
                    pe.wait_ge(t_lo_done, NG * g + e + 1)
                    for st in range(count):
                        at_p = left + (t0 + st) * P
                        last = nc.tensor.transpose(psum[:, TB + e % 2, st * P:(st + 1) * P],
                                                   p_buf[:, i % 3, at_p:at_p + P], ident[:])
                    last.then_inc(t_done, 1)

            def values(g, i):
                qb, h = i // 2, i % 2
                if i in (0, STEPS // 2):
                    pe.wait_ge(o_free[qb // 4], g)
                for r, (t0, count) in enumerate(groups(i)):
                    e = g_base[i] + r
                    pe.wait_ge(t_lo_done, NG * g + e + 3)
                    for st in range(count):
                        last = three(psum[:, OB + qb // 4, qb % 4 * P:(qb % 4 + 1) * P],
                                     lambda a: V[a][:, t0 + st, h * HD:h * HD + P],
                                     lambda b: T[b][:, e % 2, st * P:(st + 1) * P],
                                     h == 0 and t0 + st == 0, h == 1 and t0 + st == qb)
                    last.then_inc(pv_done, 1)

            def attention(g, fill, filler, z_read, left):
                def fill_at(i):
                    for o, half in fill.get(i, ()):
                        filler(o, half)

                fill_at(-1)
                v_transposes(g)
                pe.wait_ge(qk_lo_done, 2 * g + 2)
                for i in range(STEPS + LAG):
                    if i >= LAG:
                        transposes(g, i - LAG, left(i - LAG))
                    if i < STEPS:
                        z_read(i)
                        logits(i)
                    fill_at(i)
                    if i >= LAG:
                        values(g, i - LAG)

            pe.wait_ge(const_set, 7)
            with pe.Fori(0, PAIRS) as p:
                attention(p, FILL_A, lambda o, half: item_half(2 * p + I_C1 + o, (I_C1 + o) % 2, half, KT, of_h),
                          lambda i: pe.wait_ge(sig_done, 2 * STEPS * p + 2 * i),
                          lambda i: S - (i // 2 + 1) * P)

            def merge_half(n0, o, half):
                item_half(n0 + o, (I_AM + o) % 2, half, *((BT, of_y) if o % 2 else (KT, of_h)))

            with pe.Fori(0, PAIRS) as p:
                attention(p + PAIRS, FILL_C, lambda o, half: merge_half(4 * p + I_AM, o, half),
                          lambda i: pe.wait_ge(add_done, STEPS * p + i), lambda i: 0)
            with pe.Fori(0, KT) as m:
                for half in range(2):
                    item_half(2 * m + I_CM, I_CM % 2, half, KT, of_h)
                pe.wait_ge(yc_lo_done, BT)
                for half in range(2):
                    item_half(2 * m + I_CM + 1, 1 - I_CM % 2, half, BT, of_y)

            def of_m(b, k):
                if k < KT // 2:
                    return (m_hi, m_lo)[b][:, k]
                return (n_hi, n_lo)[b][:, k - KT // 2]

            def m_ready(k):
                if k < KT // 2:
                    pe.wait_ge(m_lo_done, 2 * k + 2)
                else:
                    pe.wait_ge(n_lo_done, k - KT // 2 + 1)

            item_half(I_MIX, I_MIX % 2, 0, KT, of_m, m_ready)
            item_half(I_MIX, I_MIX % 2, 1, KT, of_m)
            for half in range(2):
                item_half(I_MIX + 1, 1 - I_MIX % 2, half, KT, of_m)
            with pe.Fori(1, KT // 2) as i:
                for o in range(2):
                    for half in range(2):
                        item_half(2 * i + I_MIX + o, (I_MIX + o) % 2, half, KT, of_m)

        @block.scalar
        def _(act_e):
            def split_hi(n, slot, words=WORDS):
                act_e.wait_ge(w_in[slot], 8 * (n - slot) + 16)
                act_e.wait_ge(halves_done, 2 * n + 2)
                nc.scalar.activation(w_hi[:, slot, 0:words], w_stage[:, slot, 0:words], ACT.Copy).then_inc(w_hi_done, 1)

            def arrived(n, half):
                act_e.wait_ge(halves_done, 2 * n + half + 5)

            for k in range(KT):
                act_e.wait_ge(x_in[k // 2], 16)
                if k >= 2:
                    act_e.wait_ge(ssq_step, k - 1)
                nc.scalar.activation(norm_sq[:, k % 2], x[:, k], ACT.Square).then_inc(norm_sq_done, 1)
            act_e.wait_ge(const_set, 2)
            act_e.wait_ge(norm_sum, 1)
            for half in range(2):
                nc.scalar.activation(rstd[:, cols(half)], psum[:, half], ACT.Sqrt, bias=eps[:], scale=1.0 / D).then_inc(norm_root, 1)
            split_hi(0, 0)
            act_e.wait_ge(consts_in, 48)
            nc.scalar.activation(wi_hi[:], wi[:], ACT.Copy).then_inc(wi_hi_done, 1)
            for k in range(KT):
                act_e.wait_ge(h_scaled, k + 1)
                nc.scalar.activation(h_hi[:, k], x[:, k], ACT.Copy).then_inc(h_hi_done, 1)
            for n in range(I_CONV):
                split_hi(n + 1, (n + 1) % 2)
                for half in range(2):
                    arrived(n, half)
                    dst = iq_hi[:, n, cols(half)] if n < BT else ik_hi[:, cols(half)]
                    nc.scalar.activation(dst, psum[:, half], ACT.Copy).then_inc(idx_hi, 1)
            s = 0
            for qb in range(FULL, QT):
                width = (qb + 1) * P
                for h in range(HEADS):
                    act_e.wait_ge(iz_done, s + 1)
                    if s >= 2:
                        act_e.wait_ge(score_step, s - 1)
                    z = psum[:, ZB + 2 * (s % 2):ZB + 2 * (s % 2) + 2, :].rearrange("p b c -> p (b c)")
                    nc.scalar.activation(relu[:, s % 2, 0:width], z[:, 0:width], ACT.Relu, scale=HD ** -0.5).then_inc(relu_done, 1)
                    s += 1
            act_e.wait_ge(score_step, FIRST_SCORES)

            def copies(n, dst, before=None):
                for half in range(2):
                    arrived(n, half)
                    if before:
                        before(half)
                    nc.scalar.activation(dst(half), psum[:, half], ACT.Copy).then_inc(bank_free[half], 1)

            with act_e.Fori(0, BT // 2) as i:
                for tt in range(2):
                    t, n, slot = 2 * i + tt, 6 * i + I_CONV + 3 * tt, (I_CONV + 3 * tt) % 2
                    tap = lambda w: taps[:, bass.ds(3 * t + w, 1)]
                    split_hi(n + 1, 1 - slot)
                    act_e.wait_ge(c_pool, 5 * t)
                    copies(n, lambda half: c_buf[:, cols(half)])
                    split_hi(n + 2, slot)
                    copies(n + 1, lambda half: x_buf[:, cols(half)])
                    split_hi(n + 3, 1 - slot)
                    act_e.wait_ge(c_pool, 5 * t + 1)
                    nc.scalar.activation(c_acc[:], u_pad[:, 2:S + 2], ACT.Copy, scale=tap(2)).then_inc(c_act, 1)
                    nc.scalar.activation(x_buf[:], u_pad[:, 1:S + 1], ACT.Copy, scale=tap(1)).then_inc(c_act, 1)
                    act_e.wait_ge(c_pool, 5 * t + 2)
                    nc.scalar.activation(x_buf[:], u_pad[:, 0:S], ACT.Copy, scale=tap(0)).then_inc(c_act, 1)
                    copies(n + 2, lambda half: b_buf[:, cols(half)])
                    act_e.wait_ge(c_pool, 5 * t + 4)
                    nc.scalar.activation(tile_of(y_hi, t), c_acc[:], ACT.Copy).then_inc(c_act, 1)

            def spill_half(n, tile, half):
                arrived(n, half)
                act_e.wait_ge(spilled[half], 16 * tile)
                nc.scalar.activation(est[:, half], psum[:, half], ACT.Copy).then_inc(bank_free[half], 1)

            def spill_store(n, tile, half):
                act_e.wait_ge(bank_free[half], n + 1)
                act_e.dma_start(item_of(spill, tile)[:, cols(half)], est[:, half]).then_inc(spilled[half], 16)

            act_e.wait_ge(c_pool, 5 * BT)
            with act_e.Fori(0, (I_BM - I_A) // 2) as i:
                for o in range(2):
                    n, tile = 2 * i + I_A + o, 2 * i + o
                    split_hi(n + 1, (I_A + o + 1) % 2)
                    for half in range(2):
                        spill_half(n, tile, half)
                        spill_store(n, tile, half)

            def gate_half(n, half, stored):
                arrived(n, half)
                act_e.wait_ge(merged_out[half], stored)
                nc.scalar.activation(gate[:, half], psum[:, half], ACT.Sigmoid).then_inc(bank_free[half], 1)

            def proj_half(n, half, mults):
                arrived(n, half)
                act_e.wait_ge(merge_mult, mults)
                nc.scalar.activation(proj[:, half], psum[:, half], ACT.Copy).then_inc(bank_free[half], 1)

            with act_e.Fori(0, KT) as m:
                n = 2 * m + I_BM
                split_hi(n + 1, (I_BM + 1) % 2, HALF)
                for half in range(2):
                    gate_half(n, half, 16 * m)
                split_hi(n + 2, I_BM % 2)
                for half in range(2):
                    proj_half(n + 1, half, 2 * m)

            def qk_split(g):
                act_e.wait_ge(z_done, STEPS * g)
                for c, (dst, src, done) in enumerate(((q_hi, q_stage, q_in), (k_hi, k_stage, k_in))):
                    act_e.wait_ge(done, 16 * g + 16)
                    nc.scalar.activation(dst[:], src[:], ACT.Copy).then_inc(qk_hi_done, 1)

            def v_parts(g):
                act_e.wait_ge(pv_done, (NG - VG) * g + 2)
                for r in range(VG):
                    act_e.wait_ge(t_done, NG * g + r + 1)
                    nc.scalar.activation(v_place(v_hi, r), v_bank(r), ACT.Copy).then_inc(t_hi_done, 1)

            def t_parts(g, i):
                for r, (t0, count) in enumerate(groups(i)):
                    e = g_base[i] + r
                    act_e.wait_ge(t_done, NG * g + e + 1)
                    act_e.wait_ge(pv_done, (NG - VG) * g + e - VG + 1)
                    nc.scalar.activation(t_hi[:, e % 2, 0:count * P], psum[:, TB + e % 2, 0:count * P], ACT.Copy).then_inc(t_hi_done, 1)

            def p_free(g, i):
                act_e.wait_ge(t_done, NG * g + (g_base[i - 2] if i >= 3 else 0))

            with act_e.Fori(0, PAIRS) as p:
                n, tile = 2 * p + I_C1, 2 * p + 3 * PAIRS + N_C0

                def fill_at(i):
                    for o, half in FILL_A.get(i, ()):
                        if half == 0:
                            split_hi(n + o + 1, (I_C1 + o + 1) % 2)
                        spill_half(n + o, tile + o, half)
                        spill_store(n + o, tile + o, half)

                qk_split(p)
                fill_at(-1)
                v_parts(p)
                for i in range(STEPS + LAG):
                    if i >= LAG:
                        t_parts(p, i - LAG)
                    if i < STEPS:
                        qb = i // 2
                        left = S - (qb + 1) * P
                        z = psum[:, ZB:ZB + 2, :].rearrange("p b c -> p (b c)")[:, 0:S - left]
                        act_e.wait_ge(z_done, STEPS * p + i + 1)
                        act_e.wait_ge(p_done, STEPS * p + max(i - 1, 0))
                        nc.scalar.activation(r_buf[:, i % 2, left:S], z, ACT.Sigmoid, scale=-SCALE).then_inc(sig_done, 1)
                        p_free(p, i)
                        nc.scalar.activation(p_buf[:, i % 3, left:S], z, ACT.Sigmoid, scale=SCALE).then_inc(sig_done, 1)
                    fill_at(i)
                    if i - LAG in (STEPS // 2 - 1, STEPS - 1):
                        half = (i - LAG) // (STEPS // 2)
                        act_e.wait_ge(pv_done, (NG - VG) * p + g_base[i - LAG + 1] - VG + 2)
                        nc.scalar.activation(tile_of(y_hi, p)[:, cols(half)], psum[:, OB + half], ACT.Copy).then_inc(o_hi_done, 1)

            with act_e.Fori(0, PAIRS) as p:
                g, n = p + PAIRS, 4 * p + I_AM

                def fill_at(i):
                    for o, half in FILL_C.get(i, ()):
                        m = 2 * p + o // 2
                        if half == 0:
                            split_hi(n + o + 1, (I_AM + o + 1) % 2, WORDS if o % 2 else HALF)
                        if o % 2 == 0:
                            gate_half(n + o, half, 16 * m + 16 * KT)
                        else:
                            proj_half(n + o, half, 2 * m + 2 * KT)

                qk_split(g)
                fill_at(-1)
                v_parts(g)
                for i in range(STEPS + LAG):
                    if i >= LAG:
                        t_parts(g, i - LAG)
                    if i < STEPS:
                        width = (i // 2 + 1) * P
                        act_e.wait_ge(neg_done, STEPS * p + i + 1)
                        pc = p_buf[:, i % 3, 0:width]
                        nc.scalar.activation(pc, pc, ACT.Exp, bias=stats[:, 2 + i % 2:3 + i % 2], scale=SCALE,
                                             accum_out=stats[:, 4 + i % 2:5 + i % 2]).then_inc(exp_done, 1)
                    fill_at(i)
                    if i - LAG in (STEPS // 2 - 1, STEPS - 1):
                        half = (i - LAG) // (STEPS // 2)
                        act_e.wait_ge(pv_done, (NG - VG) * g + g_base[i - LAG + 1] - VG + 2)
                        act_e.wait_ge(spilled[half], 16 * p + 16 * SPILLS)
                        nc.scalar.activation(est[:, half], psum[:, OB + half], ACT.Copy).then_inc(o_free[half], 1)
                        act_e.wait_ge(o_free[half], g + 1)
                        act_e.dma_start(item_of(yc_dram, p)[:, cols(half)], est[:, half]).then_inc(spilled[half], 16)
            split_hi(I_CM + 1, 1 - I_CM % 2, HALF)
            for half in range(2):
                gate_half(I_CM, half, 16 * 2 * KT)
            act_e.wait_ge(yc_in, 16 * BT)
            act_e.wait_ge(halves_done, 4 + 2 * I_CM)
            for k in range(BT):
                nc.scalar.activation(y_hi[:, k], yc[k][:], ACT.Copy).then_inc(yc_hi_done, 1)
            split_hi(I_CM + 2, I_CM % 2)
            for half in range(2):
                proj_half(I_CM + 1, half, 2 * 2 * KT)

            def m_part(m):
                for half in range(2):
                    act_e.wait_ge(merge_done, 2 * m + 2 * KT + half + 1)
                    nc.scalar.activation(tile_of(m_hi, m)[:, cols(half)], gate[:, half], ACT.Copy).then_inc(m_hi_done, 1)

            def merge_tile(m, gate_used):
                n = 2 * m + I_CM
                split_hi(n + 1, 1 - I_CM % 2, HALF)
                for half in range(2):
                    arrived(n, half)
                    gate_used(half)
                    nc.scalar.activation(gate[:, half], psum[:, half], ACT.Sigmoid).then_inc(bank_free[half], 1)
                split_hi(n + 2, I_CM % 2)
                for half in range(2):
                    proj_half(n + 1, half, 2 * m + 4 * KT)

            with act_e.Fori(0, KT // 2) as m:
                m_part(m)
                merge_tile(m + 1, lambda half: act_e.wait_ge(m_lo_done, 2 * m + half + 1))
            with act_e.Fori(KT // 2 + 1, KT) as m:
                merge_tile(m, lambda half: act_e.wait_ge(merge_done, 2 * m + 2 * KT - 1 + half))
            act_e.wait_ge(halves_done, 4 + 2 * (I_MIX - 1))
            for k in range(KT // 2):
                act_e.wait_ge(merge_done, 2 * KT + KT + 2 * k + 2)
                nc.scalar.activation(n_hi[:, k], m_far[:, k], ACT.Copy).then_inc(n_hi_done, 1)
            split_hi(I_MIX + 1, 1 - I_MIX % 2)
            for m in range(KT):
                if m and m + 1 < KT:
                    split_hi(I_MIX + m + 1, (I_MIX + m + 1) % 2)
                for half in range(2):
                    v = 2 * m + half
                    act_e.wait_ge(bank_free[half], I_MIX + m + 1)
                    if v >= 2:
                        act_e.wait_ge(mix_ssq, v - 1)
                    nc.scalar.activation(mix_sq[:, half], x[:, m, cols(half)], ACT.Square).then_inc(mix_sq_done, 1)

        @block.gpsimd
        def _(pool):
            def split_lo(n, slot, words=WORDS):
                pool.wait_ge(w_hi_done, n + 1)
                nc.gpsimd.tensor_tensor(w_lo[:, slot, 0:words], w_stage[:, slot, 0:words], w_hi[:, slot, 0:words].bitcast(F32),
                                        ALU.subtract).then_inc(w_ready, 1)

            pool.sem_inc(w_ready, 2)
            nc.gpsimd.memset(ones[:], 1.0).then_inc(const_set, 1)
            nc.gpsimd.memset(eps[:], EPS).then_inc(const_set, 1)
            nc.gpsimd.memset(ident[:], 0.0).then_inc(const_set, 1)
            pool.wait_ge(const_set, 3)
            nc.gpsimd.affine_select(out=ident[:], in_=ident[:], compare_op=ALU.not_equal, fill=1.0, base=0,
                                    pattern=[[-1, P]], channel_multiplier=1).then_inc(const_set, 1)
            for qb in range(FULL):
                nc.gpsimd.memset(bias[qb][:], 0.0).then_inc(const_set, 1)
            pool.wait_ge(const_set, 6)
            for qb in range(FULL):
                diag = bias[qb][:, qb * P:(qb + 1) * P]
                nc.gpsimd.affine_select(out=diag, in_=diag, compare_op=ALU.is_ge, fill=NEG, base=0,
                                        pattern=[[-1, P]], channel_multiplier=1).then_inc(bias_first, 1)
            split_lo(0, 0)
            for k in range(1, KT, 2):
                pool.wait_ge(h_hi_done, k + 1)
                nc.gpsimd.tensor_tensor(h_lo[:, k], x[:, k], h_hi[:, k].bitcast(F32), ALU.subtract).then_inc(h_lo_pool, 1)
            for n in range(I_CONV):
                split_lo(n + 1, (n + 1) % 2)
            for qb in range(FULL, QT):
                pool.wait_ge(score_step, (qb - FULL + 1) * HEADS)
                diag = score[qb][:, qb * P:(qb + 1) * P]
                nc.gpsimd.affine_select(out=diag, in_=diag, compare_op=ALU.is_ge, fill=NOT_CAUSAL, base=0,
                                        pattern=[[-1, P]], channel_multiplier=1).then_inc(masked, 1)
            nc.gpsimd.memset(u_pad[:, 0:2], 0.0).then_inc(const_set, 1)
            pool.wait_ge(const_set, 7)
            with pool.Fori(0, BT // 2) as i:
                for tt in range(2):
                    t, n, slot = 2 * i + tt, 6 * i + I_CONV + 3 * tt, (I_CONV + 3 * tt) % 2
                    split_lo(n + 1, 1 - slot)
                    split_lo(n + 2, slot)
                    for half in range(2):
                        pool.wait_ge(bank_free[half], n + 2)
                    pool.wait_ge(c_act, 4 * t)
                    nc.gpsimd.tensor_tensor(u_pad[:, 2:S + 2], c_buf[:], x_buf[:], ALU.mult).then_inc(c_pool, 1)
                    split_lo(n + 3, 1 - slot)
                    for w in range(2):
                        pool.wait_ge(c_act, 4 * t + 2 + w)
                        nc.gpsimd.tensor_tensor(c_acc[:], c_acc[:], x_buf[:], ALU.add).then_inc(c_pool, 1)
                    for half in range(2):
                        pool.wait_ge(bank_free[half], n + 3)
                    pool.wait_ge(c_pool, 5 * t + 3)
                    nc.gpsimd.tensor_tensor(c_acc[:], c_acc[:], b_buf[:], ALU.mult).then_inc(c_pool, 1)
                    pool.wait_ge(c_act, 4 * t + 4)
                    nc.gpsimd.tensor_tensor(tile_of(y_lo, t), c_acc[:], tile_of(y_hi, t).bitcast(F32), ALU.subtract).then_inc(c_pool, 1)
            with pool.Fori(0, (I_BM - I_A) // 2) as i:
                for o in range(2):
                    split_lo(2 * i + I_A + o + 1, (I_A + o + 1) % 2)

            def mult(n, m, half):
                pool.wait_ge(bank_free[half], n + 2)
                nc.gpsimd.tensor_tensor(gate[:, half], gate[:, half], proj[:, half], ALU.mult).then_inc(merge_mult, 1)

            with pool.Fori(0, KT) as m:
                n = 2 * m + I_BM
                split_lo(n + 1, (I_BM + 1) % 2, HALF)
                split_lo(n + 2, I_BM % 2)
                for half in range(2):
                    mult(n, m, half)

            def qk_split(g):
                for dst, hi, src, c in ((q_lo, q_hi, q_stage, 0), (k_lo, k_hi, k_stage, 1)):
                    pool.wait_ge(qk_hi_done, 2 * g + c + 1)
                    nc.gpsimd.tensor_tensor(dst[:], src[:], hi[:].bitcast(F32), ALU.subtract).then_inc(qk_lo_done, 1)

            pool.wait_ge(bias_done, QT - FULL)
            for v in (v_hi, v_lo):
                nc.gpsimd.memset(v[:, :, HD:2 * HD].bitcast(F32), 0.0).then_inc(const_set, 1)
            for half in range(2):
                pool.wait_ge(merged_out[half], 16 * KT)
            nc.gpsimd.memset(r_buf[:, :, S:S + 1], 1.0).then_inc(const_set, 1)
            pool.wait_ge(const_set, 10)
            with pool.Fori(0, PAIRS) as p:
                n = 2 * p + I_C1

                def fill_at(i):
                    for o, half in FILL_A.get(i, ()):
                        if half == 0:
                            split_lo(n + o + 1, (I_C1 + o + 1) % 2)

                def weigh(i):
                    left = S - (i // 2 + 1) * P
                    pool.wait_ge(sel_done, 2 * STEPS * p + 2 * i + 2)
                    pool.wait_ge(scan_done, STEPS * p + i + 1)
                    nc.gpsimd.tensor_tensor(p_buf[:, i % 3, left:S], p_buf[:, i % 3, left:S], r_buf[:, i % 2, left + 1:S + 1],
                                            ALU.mult).then_inc(p_done, 1)

                qk_split(p)
                fill_at(-1)
                for i in range(STEPS + 1):
                    if i < STEPS:
                        for c, (buf, fill) in enumerate(((r_buf[:, i % 2], 1.0), (p_buf[:, i % 3], 0.0))):
                            pool.wait_ge(sig_done, 2 * STEPS * p + 2 * i + c + 1)
                            pool.sem_inc(pool_passed, 1)
                            diag = buf[:, S - P:S]
                            nc.gpsimd.affine_select(out=diag, in_=diag, compare_op=ALU.is_gt, fill=fill, base=0,
                                                    pattern=[[-1, P]], channel_multiplier=1).then_inc(sel_done, 1)
                    if i:
                        weigh(i - 1)
                    fill_at(i)
            with pool.Fori(0, PAIRS) as p:
                g, n = p + PAIRS, 4 * p + I_AM

                def fill_at(i):
                    for o, half in FILL_C.get(i, ()):
                        m = 2 * p + o // 2
                        if half == 0:
                            split_lo(n + o + 1, (I_AM + o + 1) % 2, WORDS if o % 2 else HALF)
                        if o % 2:
                            mult(n + o - 1, m, half)
                            pool.wait_ge(merge_mult, 2 * m + 2 * KT + half + 1)
                            pool.wait_ge(prev_in[half], 16 * m + 16)
                            nc.gpsimd.tensor_tensor(gate[:, half], gate[:, half], prev[:, half], ALU.add).then_inc(merge_done, 1)

                qk_split(g)
                fill_at(-1)
                for i in range(STEPS + 1):
                    if i:
                        j = i - 1
                        width = (j // 2 + 1) * P
                        pool.wait_ge(rec_done, STEPS * p + j + 1)
                        pool.sem_inc(pool_passed, 1)
                        pc = p_buf[:, j % 3, 0:width]
                        nc.gpsimd.tensor_scalar(pc, pc, stats[:, 6 + j % 2:7 + j % 2], 1.0, ALU.mult, ALU.mult).then_inc(p_done, 1)
                    fill_at(i)

            def merge_tile(m, dst):
                n = 2 * m + I_CM
                split_lo(n + 1, 1 - I_CM % 2, HALF)
                split_lo(n + 2, I_CM % 2)
                for half in range(2):
                    mult(n, m, half)
                    pool.wait_ge(merge_mult, 2 * m + 4 * KT + half + 1)
                    pool.wait_ge(prev_in[half], 16 * m + 16 * KT + 16)
                    nc.gpsimd.tensor_tensor(dst(half), gate[:, half], prev[:, half], ALU.add).then_inc(merge_done, 1)

            with pool.Fori(0, KT // 2) as m:
                merge_tile(m, lambda half: gate[:, half])
            with pool.Fori(KT // 2, KT) as m:
                merge_tile(m, lambda half: tile_of(m_far, m - KT // 2)[:, cols(half)])
            for n in range(I_MIX + 1, N_ITEMS):
                split_lo(n, n % 2)

        @block.vector
        def _(dve):
            dve.sem_inc(t_lo_done, 2)
            for k in range(KT):
                dve.wait_ge(norm_sq_done, k + 1)
                if k == 0:
                    nc.vector.tensor_copy(ssq[:], norm_sq[:, 0]).then_inc(ssq_step, 1)
                else:
                    dve.wait_ge(ssq_step, k)
                    nc.vector.tensor_tensor(ssq[:], ssq[:], norm_sq[:, k % 2], ALU.add).then_inc(ssq_step, 1)
            for half in range(2):
                dve.wait_ge(norm_root, half + 1)
                nc.vector.reciprocal(rstd[:, cols(half)], rstd[:, cols(half)]).then_inc(norm_rstd, 1)
            dve.wait_ge(norm_rstd, 2)
            dve.wait_ge(consts_in, 48)

            def scale(k):
                nc.vector.scalar_tensor_tensor(x[:, k], x[:, k], gains[:, k:k + 1], rstd[:], ALU.mult, ALU.mult).then_inc(h_scaled, 1)

            for k in range(0, KT, 2):
                scale(k)
                scale(k + 1)
                dve.wait_ge(h_hi_done, k + 1)
                nc.vector.tensor_tensor(h_lo[:, k], x[:, k], h_hi[:, k].bitcast(F32), ALU.subtract).then_inc(h_lo_dve, 1)
            dve.wait_ge(wi_hi_done, 1)
            nc.vector.tensor_tensor(wi_lo[:], wi[:], wi_hi[:].bitcast(F32), ALU.subtract).then_inc(wi_lo_done, 1)
            for n in range(I_CONV):
                for half in range(2):
                    dve.wait_ge(idx_hi, 2 * n + half + 1)
                    hi, lo = ((iq_hi[:, n], iq_lo[:, n]) if n < BT else (ik_hi[:], ik_lo[:]))
                    nc.vector.tensor_tensor(lo[:, cols(half)], psum[:, half], hi[:, cols(half)].bitcast(F32), ALU.subtract).then_inc(bank_free[half], 1)
            dve.wait_ge(wi_sum, 1)
            nc.vector.tensor_scalar(wi_q, psum[:, OB, 0:QT * HEADS], HEADS ** -0.5, None, ALU.mult).then_inc(wi_done, 1)
            dve.wait_ge(wi_done, 1)
            dve.wait_ge(h_lo_pool, KT // 2)
            s = 0
            for qb in range(FULL, QT):
                for h in range(HEADS):
                    dve.wait_ge(relu_done, s + 1)
                    r = relu[:, s % 2, 0:(qb + 1) * P]
                    w = wi_q[:, qb * HEADS + h:qb * HEADS + h + 1]
                    if h == 0:
                        nc.vector.tensor_scalar(score[qb][:], r, w, None, ALU.mult).then_inc(score_step, 1)
                    else:
                        dve.wait_ge(score_step, s)
                        nc.vector.scalar_tensor_tensor(score[qb][:], r, w, score[qb][:], ALU.mult, ALU.add).then_inc(score_step, 1)
                    s += 1
            ROUNDS = TOPK // 8
            UNROLL = 4
            for b, qb in enumerate(range(FULL, QT)):
                dve.wait_ge(masked, b + 1)
                with dve.Fori(0, ROUNDS // UNROLL) as i:
                    for u in range(UNROLL):
                        step = 2 * UNROLL * i + 2 * ROUNDS * b + 2 * u
                        dve.wait_ge(topk_step, step)
                        dve.sem_inc(dve_passed, 1)
                        nc.vector.max(top8, score[qb][:]).then_inc(topk_step, 1)
                        dve.wait_ge(topk_step, step + 1)
                        dve.sem_inc(dve_passed, 1)
                        nc.vector.match_replace(out=score[qb][:], in_to_replace=top8, in_values=score[qb][:], imm_value=TAKEN).then_inc(topk_step, 1)
                dve.wait_ge(topk_step, 2 * ROUNDS * (b + 1))
                nc.vector.tensor_scalar(bias[qb][:], score[qb][:], (NOT_CAUSAL + TAKEN) / 2, NEG, ALU.is_gt, ALU.mult).then_inc(bias_done, 1)

            def v_parts(g):
                for r in range(VG):
                    dve.wait_ge(t_hi_done, NG * g + r + 1)
                    nc.vector.tensor_tensor(v_place(v_lo, r), v_bank(r), v_place(v_hi, r).bitcast(F32), ALU.subtract).then_inc(t_lo_done, 1)

            def t_parts(g, i):
                for r, (t0, count) in enumerate(groups(i)):
                    e = g_base[i] + r
                    dve.wait_ge(t_hi_done, NG * g + e + 1)
                    nc.vector.tensor_tensor(t_lo[:, e % 2, 0:count * P], psum[:, TB + e % 2, 0:count * P],
                                            t_hi[:, e % 2, 0:count * P].bitcast(F32), ALU.subtract).then_inc(t_lo_done, 1)

            dve.wait_ge(const_set, 10)
            with dve.Fori(0, PAIRS) as p:
                v_parts(p)
                for i in range(STEPS + LAG):
                    if i >= LAG:
                        t_parts(p, i - LAG)
                    if i < STEPS:
                        left = S - (i // 2 + 1) * P
                        dve.wait_ge(sel_done, 2 * STEPS * p + 2 * i + 1)
                        r = r_buf[:, i % 2, left:S][:, ::-1]
                        nc.vector.tensor_tensor_scan(r, r, r, 1.0, ALU.mult, ALU.bypass).then_inc(scan_done, 1)
                    if i - LAG in (STEPS // 2 - 1, STEPS - 1):
                        half = (i - LAG) // (STEPS // 2)
                        dve.wait_ge(o_hi_done, 2 * p + half + 1)
                        nc.vector.tensor_tensor(tile_of(y_lo, p)[:, cols(half)], psum[:, OB + half],
                                                tile_of(y_hi, p)[:, cols(half)].bitcast(F32), ALU.subtract).then_inc(o_free[half], 1)
            with dve.Fori(0, PAIRS) as p:
                g = p + PAIRS

                def invert(i):
                    dve.wait_ge(exp_done, STEPS * p + i + 1)
                    dve.wait_ge(p_done, STEPS * g + max(i - 1, 0))
                    nc.vector.reciprocal(stats[:, 6 + i % 2:7 + i % 2], stats[:, 4 + i % 2:5 + i % 2]).then_inc(rec_done, 1)

                v_parts(g)
                for i in range(STEPS + LAG):
                    if i >= LAG:
                        t_parts(g, i - LAG)
                    if i < STEPS:
                        qb = i // 2
                        width = (qb + 1) * P
                        pc = p_buf[:, i % 3, 0:width]
                        z = psum[:, ZB:ZB + 2, :].rearrange("p b c -> p (b c)")[:, 0:width]
                        dve.wait_ge(z_done, STEPS * g + i + 1)
                        dve.wait_ge(t_done, NG * g + (g_base[i - 2] if i >= 3 else 0))
                        nc.vector.tensor_tensor(pc, z, bias[qb][:], ALU.add).then_inc(add_done, 1)
                        dve.wait_ge(add_done, STEPS * p + i + 1)
                        nc.vector.tensor_reduce(stats[:, i % 2:i % 2 + 1], pc, AX.X, ALU.max).then_inc(max_done, 1)
                        dve.wait_ge(max_done, STEPS * p + i + 1)
                        dve.wait_ge(exp_done, STEPS * p + max(i - 1, 0))
                        nc.vector.tensor_scalar(stats[:, 2 + i % 2:3 + i % 2], stats[:, i % 2:i % 2 + 1], -SCALE, None, ALU.mult).then_inc(neg_done, 1)
                    if 0 < i <= STEPS:
                        invert(i - 1)
            dve.wait_ge(halves_done, 4 + 2 * I_CM)
            for k in range(BT):
                dve.wait_ge(yc_hi_done, k + 1)
                nc.vector.tensor_tensor(y_lo[:, k], yc[k][:], y_hi[:, k].bitcast(F32), ALU.subtract).then_inc(yc_lo_done, 1)
            with dve.Fori(0, KT // 2) as m:
                for half in range(2):
                    dve.wait_ge(m_hi_done, 2 * m + half + 1)
                    nc.vector.tensor_tensor(tile_of(m_lo, m)[:, cols(half)], gate[:, half],
                                            tile_of(m_hi, m)[:, cols(half)].bitcast(F32), ALU.subtract).then_inc(m_lo_done, 1)
            for k in range(KT // 2):
                dve.wait_ge(n_hi_done, k + 1)
                nc.vector.tensor_tensor(n_lo[:, k], m_far[:, k], n_hi[:, k].bitcast(F32), ALU.subtract).then_inc(n_lo_done, 1)
            dve.wait_ge(n_lo_done, KT // 2)
            dve.wait_ge(x_again_in, 16 * KT)
            for v in range(2 * KT + 1):
                if v < 2 * KT:
                    m, half = v // 2, v % 2
                    dve.wait_ge(halves_done, 4 + 2 * I_MIX + v + 1)
                    nc.vector.tensor_tensor(x[:, m, cols(half)], psum[:, half], x_again[:, m, cols(half)], ALU.add).then_inc(bank_free[half], 1)
                if v:
                    half = (v - 1) % 2
                    dve.wait_ge(mix_sq_done, v)
                    if v >= 3:
                        dve.wait_ge(mix_ssq, v - 2)
                        nc.vector.tensor_tensor(ssq[:, cols(half)], ssq[:, cols(half)], mix_sq[:, half], ALU.add).then_inc(mix_ssq, 1)
                    else:
                        nc.vector.tensor_copy(ssq[:, cols(half)], mix_sq[:, half]).then_inc(mix_ssq, 1)


def build(nc, arrays, out):
    with ExitStack() as ctx:
        at = sbuf_map(nc)
        psum = ctx.enter_context(nc.psum_tensor("psum", [P, 8, HALF], F32))
        shared = {
            "x": at("x", 0, [P, KT, S]),
            "ssq": at("ssq", 51200, [P, S]),
            "gains": at("gains", 52224, [P, 5 * KT]),
            "ones": at("ones", 52264, [P, P]),
            "ident": at("ident", 52392, [P, P]),
            "eps": at("eps", 52520, [P, 1]),
            "gains_dram": arrays["gains"],
        }
        scratch = {name: nc.dram_tensor(name, shape, F32, kind="Internal").ap() for name, shape in
                   (("qkv_dram", [6 * PAIRS, P, S]), ("merged_dram", [KT, P, S]), ("yc_dram", [BT, P, S]), ("x2_dram", [KT, P, S]))}
        build_mixer(nc, ctx, at, psum, shared, arrays["mixer_w"], arrays["x"], arrays["idx_w"], arrays["taps"],
                    scratch["qkv_dram"], scratch["merged_dram"], scratch["yc_dram"])
        build_cross(nc, ctx, at, psum, shared, arrays["cross_w"], arrays["mem"], scratch["x2_dram"])
        build_ffn(nc, ctx, at, psum, shared, arrays["ffn_w"], arrays["ffn_conv_w"], arrays["ffn_conv_b"], scratch["x2_dram"], out)


def kernel(x, mem, norm_mix, w_in, sc_conv_w, w_sb_out, w_sc_out, w_dsa_out, w_mix_o, norm_xa, norm_mem, w_xa_q, w_xa_kv,
           w_xa_o, norm_ffn, w_ffn_in, ffn_conv_w, ffn_conv_b, w_ffn_down, norm_final):
    import concourse.bacc as bacc
    from concourse.bass_utils import run_bass_kernel_spmd

    def tiles(w):
        k, m = w.shape[0] // P, w.shape[1] // P
        return w.reshape(k, P, m, P).transpose(2, 1, 0, 3).reshape(m, P, k * P)

    def columns(w, start, width):
        return tiles(w[:, start:start + width])

    def trio(a, b, c):
        return [w for t in range(len(a)) for w in (a[t], b[t], c[t])]

    w_in = np.asarray(w_in)[0]
    SB, CONV, DSA, IDX, IDX_K = 0, 3 * SC, 6 * SC, 9 * SC, 10 * SC
    IDX_W, GATES = IDX_K + HD, IDX_K + HD + HEADS
    idx_k = w_in[:, IDX_K:IDX_K + HD]
    b, c, u = (columns(w_in, CONV + i * SC, SC) for i in range(3))
    conv = trio(c, u, b)
    sb = trio(*(columns(w_in, SB + i * SC, SC) for i in range(3)))
    dsa = trio(*(columns(w_in, DSA + i * SC, SC) for i in range(3)))

    def merge(branch, w):
        gates, proj = columns(w_in, GATES + branch * D, D), tiles(np.asarray(w)[0])
        proj = np.concatenate([proj, np.zeros_like(proj)], axis=2)
        return [w for m in range(KT) for w in (gates[m], proj[m])]

    mixer_w = [*columns(w_in, IDX, SC), *tiles(np.concatenate([idx_k, idx_k], axis=1)), *conv, *sb, *dsa[:4],
               *merge(1, w_sc_out), *dsa[4:], *merge(0, w_sb_out), *merge(2, w_dsa_out), *tiles(np.asarray(w_mix_o)[0])]

    w_kv, w_q, w_o = (np.asarray(w)[0] for w in (w_xa_kv, w_xa_q, w_xa_o))
    xk, xq = tiles(w_kv[:, :D]), tiles(w_q)
    xv = w_kv[:, D:].reshape(KT // 2, 2, P, 2, HALF).transpose(3, 0, 2, 1, 4).reshape(KT, P, WORDS)
    xo = w_o.reshape(XA_HEADS, 2, P, 2, 4, P).transpose(0, 3, 2, 1, 4, 5).reshape(XA_HEADS, 2, P, WORDS)
    cross_w = [*xk, *xv, xq[0], xq[1]]
    for h in range(XA_HEADS):
        cross_w += ([*xo[h - 1]] if h else []) + ([*xq[2 * h + 2:2 * h + 4]] if h + 1 < XA_HEADS else [])
    cross_w += [*xo[XA_HEADS - 1]]

    w_up, w_down = np.asarray(w_ffn_in)[0], np.asarray(w_ffn_down)[0]
    fa, fu = tiles(w_up[:, :DFF]), tiles(w_up[:, DFF:])
    down = w_down.reshape(FT // 2, 2, P, 2, 4, P).transpose(3, 0, 2, 1, 4, 5).reshape(FT, P, WORDS)
    ffn_w = [w for f in range(FT) for w in (fa[f], fu[f])] + [*down]

    gains = np.stack([np.asarray(g).reshape(KT, P) for g in (norm_mix, norm_xa, norm_mem, norm_ffn, norm_final)])
    arrays = {
        "x": np.asarray(x)[0].T.reshape(KT, P, S),
        "mem": np.asarray(mem)[0].T.reshape(KT, P, MEM),
        "gains": gains.transpose(2, 0, 1).reshape(P, 5 * KT),
        "mixer_w": np.stack(mixer_w),
        "idx_w": w_in[:, IDX_W:IDX_W + HEADS].reshape(KT, P, HEADS).transpose(1, 0, 2),
        "taps": np.asarray(sc_conv_w)[0].reshape(3, BT, P).transpose(2, 1, 0).reshape(P, 3 * BT),
        "cross_w": np.stack(cross_w),
        "ffn_w": np.stack(ffn_w),
        "ffn_conv_w": np.asarray(ffn_conv_w)[0].reshape(3, FT, P).transpose(2, 1, 0),
        "ffn_conv_b": np.asarray(ffn_conv_b)[0].reshape(FT, P).T,
    }
    arrays = {name: np.ascontiguousarray(a) for name, a in arrays.items()}
    nc = bacc.Bacc("TRN2", target_bir_lowering=False, num_devices=1)
    drams = {name: nc.dram_tensor(name + "_in", list(a.shape), F32, kind="ExternalInput").ap() for name, a in arrays.items()}
    out = nc.dram_tensor("out", [KT, P, S], F32, kind="ExternalOutput").ap()
    build(nc, drams, out)
    result = run_bass_kernel_spmd(nc, [{name + "_in": a for name, a in arrays.items()}], core_ids=[0])
    return result.results[0]["out"].reshape(D, S).T[None]
```

```python
from contextlib import ExitStack

import concourse.bass as bass
import numpy as np
from concourse import mybir

F32 = mybir.dt.float32
F32R = mybir.dt.float32r
BF16 = mybir.dt.bfloat16
ACT = mybir.ActivationFunctionType
ALU = mybir.AluOpType
AX = mybir.AxisListType

P = 128
D = 1024
S = 1024
KT = D // P
HALF = 512
WORDS = KT * P
DFF = 2816
FT = DFF // P
EPS = 1e-6
PASSES = ((0, 0), (0, 1), (1, 0))


def cols(half):
    return slice(half * HALF, (half + 1) * HALF)


def sbuf_map(nc):
    base = (nc.sbuf_base + 31) // 32 * 32
    room = (nc.sbuf_usable_end - base) // 4

    def at(name, word, shape, dtype=F32):
        size = int(np.prod(shape[1:])) * (2 if dtype == BF16 else 4)
        assert word * 4 + size <= room * 4, (name, word, size, room)
        return nc.alloc_sbuf_tensor_at(name, shape, dtype, offset=base + word * 4)

    return at


def tile_of(t, n):
    if isinstance(n, int):
        return t[:, n]
    return t[:, bass.ds(n, 1)].rearrange("p a w -> p (a w)")


def item_of(w, n):
    if isinstance(n, int):
        return w[n]
    return w[bass.ds(n, 1)].rearrange("a p w -> p (a w)")


SUM_BANK, WIDE_BANK = 5, 6


def token_sums(nc, psum, ssq, ones):
    for t in range(S // P):
        last = nc.tensor.matmul(psum[:, SUM_BANK, t:t + 1], ssq[:, t * P:(t + 1) * P], ones[:, 0:1], start=True, stop=True)
    return last


def spread_factors(nc, psum, rstd, ident, half):
    for t in range(HALF // P):
        block = half * (HALF // P) + t
        last = nc.tensor.matmul(psum[:, WIDE_BANK + half, t * P:(t + 1) * P], rstd[:, block:block + 1].to_broadcast([P, P]), ident[:],
                                start=True, stop=True)
    return last


def build_ffn(nc, ctx, at, psum, shared, w_items, conv_w, conv_b, x2_dram, out_dram):
    UP = 2 * FT
    DOWN = FT // 2
    GROUPS = 2
    GM = KT // GROUPS
    x, ssq, gains, ones, ident, eps = (shared[n] for n in ("x", "ssq", "gains", "ones", "ident", "eps"))
    g_ffn, g_final = 3 * KT, 4 * KT
    with ExitStack() as scope:
        def sem(name):
            return ctx.enter_context(nc.semaphore("f_" + name))

        act = at("f_act", 0, [P, FT, S])
        h_hi = at("f_h_hi", 22528, [P, KT, S], F32R)
        h_lo = at("f_h_lo", 30720, [P, KT, S], F32R)
        w_stage = at("f_w_stage", 38912, [P, 2, WORDS])
        w_hi = at("f_w_hi", 40960, [P, 2, WORDS], F32R)
        w_lo = at("f_w_lo", 43008, [P, 2, WORDS], F32R)
        rstd = at("f_rstd", 52528, [P, S // P])
        a_pad = at("f_a_pad", 45056, [P, S + 2])
        conv = at("f_conv", 46088, [P, S])
        gel = at("f_gel", 47112, [P, S])
        x2_ring = at("f_x2_ring", 48136, [P, 2, S])
        cw = at("f_cw", 50184, [P, FT, 3])
        cb = at("f_cb", 50256, [P, FT])
        x3 = at("f_x3", 22528, [P, KT, S])
        k_hi = at("f_k_hi", 30720, [P, 2, S], F32R)
        k_lo = at("f_k_lo", 32768, [P, 2, S], F32R)
        sq = at("f_sq", 34816, [P, 2, HALF])
        H = (h_hi, h_lo)
        W = (w_hi, w_lo)
        K = (k_hi, k_lo)

        consts_in = sem("consts_in")
        norm_sum = sem("norm_sum")
        norm_root = sem("norm_root")
        norm_rstd = sem("norm_rstd")
        norm_wide = sem("norm_wide")
        h_scaled = sem("h_scaled")
        h_hi_done = sem("h_hi_done")
        h_lo_dve = sem("h_lo_dve")
        h_lo_pool = sem("h_lo_pool")
        w_in = [sem(f"w_in{j}") for j in range(2)]
        w_hi_done = sem("w_hi_done")
        w_ready = sem("w_ready")
        halves_done = sem("halves_done")
        bank_free = [sem(f"bank_free{j}") for j in range(2)]
        pad_zero = sem("pad_zero")
        conv_step = sem("conv_step")
        gelu_done = sem("gelu_done")
        k_hi_done = sem("k_hi_done")
        k_ready = sem("k_ready")
        k_done = sem("k_done")
        x3_done = sem("x3_done")
        x2_in = [sem(f"x2_in{j}") for j in range(2)]
        sq_done = sem("sq_done")
        ssq_step = sem("ssq_step")
        ssq_zero = sem("ssq_zero")
        y_done = sem("y_done")
        y_stored = sem("y_stored")

        acc_order = [(m, half) for m in (1, 2, 3, 0) for half in range(2)]
        out_order = [g * GM + m for g in range(GROUPS) for m, half in acc_order if half == 0]

        block = scope.enter_context(nc.Block())

        @block.sync
        def _(sp):
            sp.dma_start(cw[:], conv_w).then_inc(consts_in, 16)
            sp.dma_start(cb[:], conv_b).then_inc(consts_in, 16)
            def weights(first, end):
                with sp.Fori(first // 2, end // 2) as i:
                    for j in range(2):
                        sp.wait_ge(w_ready, 2 * i + j + 1)
                        sp.dma_start(w_stage[:, j], item_of(w_items, 2 * i + j)).then_inc(w_in[j], 16)

            def residual(first, end):
                for c in range(first, end):
                    if c >= 2:
                        sp.wait_ge(x3_done, 2 * (c - 1))
                    sp.dma_start(x2_ring[:, c % 2], x2_dram[out_order[c]]).then_inc(x2_in[c % 2], 16)

            weights(0, UP + 2)
            residual(0, 2)
            weights(UP + 2, UP + DOWN + 1)
            residual(2, 6)
            weights(UP + DOWN + 1, UP + GROUPS * DOWN)
            residual(6, 8)
            for half in range(2):
                for m in range(KT):
                    sp.wait_ge(y_done, half * KT + m + 1)
                    sp.dma_start(out_dram[m][:, cols(half)], x3[:, m, cols(half)]).then_inc(y_stored, 16)
            sp.wait_ge(y_stored, 16 * 2 * KT)

        @block.tensor
        def _(pe):
            pe.sem_inc(halves_done, 4)
            pe.sem_inc(k_done, 2)

            def norm_factors(n):
                token_sums(nc, psum, ssq, ones).then_inc(norm_sum, 1)
                pe.wait_ge(norm_rstd, n + 1)
                for half in range(2):
                    spread_factors(nc, psum, rstd, ident, half).then_inc(norm_wide, 1)

            def up_item(n, j, first=False):
                pe.wait_ge(w_ready, n + 3)
                for half in range(2):
                    if not first:
                        pe.wait_ge(bank_free[half], n + 1)
                    for k in range(KT):
                        if first:
                            pe.wait_ge(h_lo_pool if k % 2 else h_lo_dve, half * KT // 2 + k // 2 + 1)
                        for a, b in PASSES:
                            last = nc.tensor.matmul(psum[:, half], W[a][:, j, k * P:(k + 1) * P], H[b][:, k, cols(half)],
                                                    start=(k == 0 and (a, b) == (0, 0)), stop=(k == KT - 1 and a == 1))
                    last.then_inc(halves_done, 1)

            norm_factors(0)
            up_item(0, 0, first=True)
            up_item(1, 1)
            with pe.Fori(1, FT) as f:
                for j in range(2):
                    up_item(2 * f + j, j)

            def down_item(g, i, j, start=False, stop=False):
                for kk in range(2):
                    pe.wait_ge(k_ready, g * FT + 2 * i + kk + 1)
                    if kk == 0:
                        pe.wait_ge(w_ready, UP + g * DOWN + i + 3)
                    for q, (m, half) in enumerate(acc_order):
                        if start and kk == 0 and g == 1:
                            pe.wait_ge(x3_done, q + 1)
                        elif start and kk == 0 and m == 0:
                            pe.wait_ge(bank_free[half], UP + 1)
                        for a, b in PASSES:
                            last = nc.tensor.matmul(psum[:, 2 * m + half], W[a][:, j, (kk * GM + m) * P:(kk * GM + m + 1) * P],
                                                    K[b][:, kk, cols(half)], start=(start and kk == 0 and (a, b) == (0, 0)),
                                                    stop=(stop and kk == 1 and a == 1))
                    last.then_inc(k_done, 1)

            for g in range(GROUPS):
                slot = g * DOWN % 2
                down_item(g, 0, slot, start=True)
                with pe.Fori(0, (DOWN - 3) // 2) as i:
                    down_item(g, 2 * i + 1, 1 - slot)
                    down_item(g, 2 * i + 2, slot)
                down_item(g, DOWN - 2, 1 - slot)
                down_item(g, DOWN - 1, slot, stop=True)
            pe.wait_ge(ssq_step, 2 * KT)
            pe.wait_ge(x3_done, 2 * KT)
            norm_factors(1)

        @block.scalar
        def _(act_e):
            def split_hi(j):
                nc.scalar.activation(w_hi[:, j], w_stage[:, j], ACT.Copy).then_inc(w_hi_done, 1)

            def roots(n):
                act_e.wait_ge(norm_sum, n + 1)
                nc.scalar.activation(rstd[:], psum[:, SUM_BANK, 0:S // P], ACT.Sqrt, bias=eps[:], scale=1.0 / D).then_inc(norm_root, 1)

            act_e.wait_ge(w_in[0], 16)
            split_hi(0)
            roots(0)
            for half in range(2):
                for k in range(KT):
                    act_e.wait_ge(h_scaled, half * KT + k + 1)
                    nc.scalar.activation(h_hi[:, k, cols(half)], x[:, k, cols(half)], ACT.Copy).then_inc(h_hi_done, 1)
            act_e.wait_ge(pad_zero, 1)
            with act_e.Fori(0, FT) as f:
                act_e.wait_ge(w_in[1], 16 * f + 16)
                act_e.wait_ge(halves_done, 4 * f + 4)
                split_hi(1)
                act_e.wait_ge(conv_step, 3 * f + 3)
                for half in range(2):
                    act_e.wait_ge(halves_done, 4 * f + half + 5)
                    nc.scalar.activation(a_pad[:, 2 + half * HALF:2 + (half + 1) * HALF], psum[:, half], ACT.Copy).then_inc(bank_free[half], 1)
                act_e.wait_ge(w_in[0], 16 * f + 32)
                act_e.wait_ge(halves_done, 4 * f + 6)
                split_hi(0)
                for half in range(2):
                    act_e.wait_ge(bank_free[half], 2 * f + 1)
                act_e.wait_ge(conv_step, 3 * f + 6)
                nc.scalar.activation(gel[:], conv[:], ACT.Gelu_apprx_tanh).then_inc(gelu_done, 1)
            act_e.wait_ge(halves_done, 4 + 2 * UP)
            for half in range(2):
                act_e.wait_ge(bank_free[half], UP + 1)

            def w_arrived(d, e=0):
                act_e.wait_ge(w_in[d % 2], 16 * ((UP + d) // 2 + 1) + 16 * e)

            def squares(g):
                for q, (m, half) in enumerate(acc_order):
                    n = g * 2 * GM + q
                    act_e.wait_ge(x3_done, n + 1)
                    if n >= 2:
                        act_e.wait_ge(ssq_step, n - 1)
                    nc.scalar.activation(sq[:, n % 2], x3[:, g * GM + m, cols(half)], ACT.Square).then_inc(sq_done, 1)

            def k_tiles(i, used):
                for kk in range(2):
                    act_e.wait_ge(k_done, used + kk)
                    nc.scalar.activation(k_hi[:, kk], tile_of(act, 2 * i + kk), ACT.Copy).then_inc(k_hi_done, 1)

            for g in range(GROUPS):
                if g:
                    w_arrived(DOWN)
                    act_e.wait_ge(k_done, 2 * DOWN)
                    split_hi(DOWN % 2)
                k_tiles(0, 2 * g * DOWN + 1)
                if g:
                    squares(0)
                with act_e.Fori(0, (DOWN - 1) // 2) as e:
                    for o in range(2):
                        d = g * DOWN + o + 1
                        w_arrived(d, e)
                        act_e.wait_ge(k_done, 2 * d + 4 * e)
                        split_hi(d % 2)
                        k_tiles(2 * e + o + 1, 2 * d + 1 + 4 * e)
            squares(1)
            roots(1)

        @block.gpsimd
        def _(pool):
            def split_lo(n, j):
                pool.wait_ge(w_hi_done, n + 1)
                nc.gpsimd.tensor_tensor(w_lo[:, j], w_stage[:, j], w_hi[:, j].bitcast(F32), ALU.subtract).then_inc(w_ready, 1)

            pool.sem_inc(w_ready, 2)
            split_lo(0, 0)
            for half in range(2):
                for k in range(1, KT, 2):
                    pool.wait_ge(h_hi_done, half * KT + k + 1)
                    nc.gpsimd.tensor_tensor(h_lo[:, k, cols(half)], x[:, k, cols(half)], h_hi[:, k, cols(half)].bitcast(F32),
                                            ALU.subtract).then_inc(h_lo_pool, 1)
            nc.gpsimd.memset(a_pad[:, 0:2], 0.0).then_inc(pad_zero, 1)
            split_lo(1, 1)
            with pool.Fori(1, (UP + GROUPS * DOWN) // 2) as i:
                for j in range(2):
                    split_lo(2 * i + j, j)

        @block.vector
        def _(dve):
            dve.sem_inc(conv_step, 3)
            for start_at_1 in (gelu_done, *bank_free):
                dve.sem_inc(start_at_1, 1)

            def reciprocals(n):
                dve.wait_ge(norm_root, n + 1)
                nc.vector.reciprocal(rstd[:], rstd[:]).then_inc(norm_rstd, 1)

            def scale(k, half):
                h = x[:, k, cols(half)]
                nc.vector.scalar_tensor_tensor(h, h, gains[:, g_ffn + k:g_ffn + k + 1], psum[:, WIDE_BANK + half],
                                               ALU.mult, ALU.mult).then_inc(h_scaled, 1)

            reciprocals(0)
            for half in range(2):
                dve.wait_ge(norm_wide, half + 1)
                for k in range(0, KT, 2):
                    scale(k, half)
                    scale(k + 1, half)
                    dve.wait_ge(h_hi_done, half * KT + k + 1)
                    nc.vector.tensor_tensor(h_lo[:, k, cols(half)], x[:, k, cols(half)], h_hi[:, k, cols(half)].bitcast(F32),
                                            ALU.subtract).then_inc(h_lo_dve, 1)
            nc.vector.memset(ssq[:], 0.0).then_inc(ssq_zero, 1)
            dve.wait_ge(consts_in, 32)
            dve.wait_ge(h_lo_pool, KT)
            dve.wait_ge(h_lo_dve, KT)

            def tap(w, f):
                return cw[:, bass.ds(f, 1), w:w + 1].rearrange("p a b -> p (a b)")

            with dve.Fori(0, FT) as f:
                for half in range(2):
                    dve.wait_ge(bank_free[half], 2 * f + 2)
                dve.wait_ge(gelu_done, f + 1)
                nc.vector.tensor_scalar(conv[:], a_pad[:, 2:S + 2], tap(2, f), cb[:, bass.ds(f, 1)],
                                        ALU.mult, ALU.add).then_inc(conv_step, 1)
                for w in (1, 0):
                    dve.wait_ge(conv_step, 3 * f + 5 - w)
                    nc.vector.scalar_tensor_tensor(conv[:], a_pad[:, w:S + w], tap(w, f), conv[:],
                                                   ALU.mult, ALU.add).then_inc(conv_step, 1)
                dve.wait_ge(gelu_done, f + 2)
                for half in range(2):
                    dve.wait_ge(halves_done, 4 * f + 7 + half)
                    nc.vector.tensor_tensor(act[:, bass.ds(f, 1), cols(half)].rearrange("p a t -> p (a t)"),
                                            gel[:, cols(half)], psum[:, half], ALU.mult).then_inc(bank_free[half], 1)

            def k_lo_part(i, n):
                for kk in range(2):
                    dve.wait_ge(k_hi_done, n + kk + 1)
                    nc.vector.tensor_tensor(k_lo[:, kk], tile_of(act, 2 * i + kk), k_hi[:, kk].bitcast(F32),
                                            ALU.subtract).then_inc(k_ready, 1)

            def read_out(g):
                dve.wait_ge(k_done, 2 + (g + 1) * FT)
                for q in range(2 * GM + 1):
                    if q < 2 * GM:
                        m, half = acc_order[q]
                        n = g * 2 * GM + q
                        c = n // 2
                        dve.wait_ge(x2_in[c % 2], 16 * (c // 2 + 1))
                        nc.vector.tensor_tensor(x3[:, g * GM + m, cols(half)], psum[:, 2 * m + half],
                                                x2_ring[:, c % 2, cols(half)], ALU.add).then_inc(x3_done, 1)
                    if q:
                        half = acc_order[q - 1][1]
                        n = g * 2 * GM + q - 1
                        dve.wait_ge(sq_done, n + 1)
                        if n >= 2:
                            dve.wait_ge(ssq_step, n - 1)
                        nc.vector.tensor_tensor(ssq[:, cols(half)], ssq[:, cols(half)], sq[:, n % 2], ALU.add).then_inc(ssq_step, 1)

            dve.wait_ge(ssq_zero, 1)
            for g in range(GROUPS):
                k_lo_part(0, g * FT)
                if g:
                    read_out(0)
                with dve.Fori(0, (DOWN - 1) // 2) as e:
                    for o in range(2):
                        k_lo_part(2 * e + o + 1, g * FT + 2 * (o + 1) + 4 * e)
            read_out(1)
            reciprocals(1)
            for half in range(2):
                dve.wait_ge(norm_wide, 2 + half + 1)
                for m in range(KT):
                    y = x3[:, m, cols(half)]
                    nc.vector.scalar_tensor_tensor(y, y, gains[:, g_final + m:g_final + m + 1], psum[:, WIDE_BANK + half],
                                                   ALU.mult, ALU.mult).then_inc(y_done, 1)


MEM = 256
XA_HEADS = 4
XA_DIM = D // XA_HEADS


def build_cross(nc, ctx, at, psum, shared, w_items, x2_dram):
    x, ssq, gains, ones, ident, eps = (shared[n] for n in ("x", "ssq", "gains", "ones", "ident", "eps"))
    g_xa = KT
    MT = MEM // P
    DT = XA_DIM // P
    QB = HALF // P
    SCALE = XA_DIM ** -0.5
    N_KV = 2 * KT
    N_ITEMS = N_KV + 2 * XA_HEADS + 2 * XA_HEADS
    with ExitStack() as scope:
        def sem(name):
            return ctx.enter_context(nc.semaphore("c_" + name))

        h_hi = at("c_h_hi", 8192, [P, KT, S], F32R)
        h_lo = at("c_h_lo", 16384, [P, KT, S], F32R)
        w_stage = at("c_w_stage", 24576, [P, 2, WORDS])
        w_hi = at("c_w_hi", 26624, [P, 2, WORDS], F32R)
        w_lo = at("c_w_lo", 28672, [P, 2, WORDS], F32R)
        k_hi = at("c_k_hi", 38912, [P, KT, MEM], F32R)
        k_lo = at("c_k_lo", 40960, [P, KT, MEM], F32R)
        v_hi = at("c_v_hi", 43008, [P, MT, D], F32R)
        v_lo = at("c_v_lo", 45056, [P, MT, D], F32R)
        q_hi = at("c_q_hi", 30720, [P, DT, S], F32R)
        q_lo = at("c_q_lo", 32768, [P, DT, S], F32R)
        pt_hi = at("c_pt_hi", 34816, [P, MT, HALF], F32R)
        pt_lo = at("c_pt_lo", 35840, [P, MT, HALF], F32R)
        y_hi = at("c_y_hi", 36864, [P, DT, S], F32R)
        y_lo = at("c_y_lo", 47104, [P, DT, S], F32R)
        p_buf = at("c_p", 49152, [P, 2, QB, MEM])
        stats = at("c_stats", 52600, [P, 4, 2, QB])
        w_extra = at("c_w_extra", 34816, [P, 2, WORDS])
        w_hi_extra = at("c_w_hi_extra", 36864, [P, WORDS], F32R)[:]
        w_lo_extra = at("c_w_lo_extra", 37888, [P, WORDS], F32R)[:]
        rstd = at("c_rstd", 47616, [P, S])
        h_f32 = at("c_h_f32", 49152, [P, 2, S])
        sq = at("c_sq", 34816, [P, 2, HALF])
        H, K, V, Q = (h_hi, h_lo), (k_hi, k_lo), (v_hi, v_lo), (q_hi, q_lo)
        PT, Y, M = (pt_hi, pt_lo), (y_hi, y_lo), shared["memory"]
        ZB, TB, OB = 2, 4, 6

        norm_sum = sem("norm_sum")
        norm_root = sem("norm_root")
        norm_rstd = sem("norm_rstd")
        h_scaled = sem("h_scaled")
        h_hi_done = sem("h_hi_done")
        h_lo_done = sem("h_lo_done")
        w_in = [sem(f"w_in{j}") for j in range(4)]
        w_hi_done = sem("w_hi_done")
        w_ready = sem("w_ready")
        use_done = sem("use_done")
        use_hi = sem("use_hi")
        use_free = [sem(f"use_free{j}") for j in range(2)]
        v_done = sem("v_done")
        v_hi_done = sem("v_hi_done")
        v_lo_done = sem("v_lo_done")
        z_done = sem("z_done")
        max_done = sem("max_done")
        neg_done = sem("neg_done")
        exp_done = sem("exp_done")
        rec_done = sem("rec_done")
        p_done = sem("p_done")
        t_done = sem("t_done")
        pt_hi_done = sem("pt_hi_done")
        pt_lo_done = sem("pt_lo_done")
        pv_done = sem("pv_done")
        y_hi_done = sem("y_hi_done")
        y_lo_done = sem("y_lo_done")
        sq_done = sem("sq_done")
        ssq_step = sem("ssq_step")
        x_stored = sem("x_stored")

        item_kind = (["k"] * KT + ["v"] * KT + ["q"] * 2
                     + sum((["o"] * 2 * (h > 0) + ["q"] * 2 * (h < XA_HEADS - 1) for h in range(XA_HEADS)), []) + ["o"] * 2)
        assert len(item_kind) == N_ITEMS
        uses = {"k": 1, "v": 0, "q": 2, "o": 8}
        first_use = [sum(uses[c] for c in item_kind[:n]) for n in range(N_ITEMS + 1)]
        q_items = [[n for n in range(N_ITEMS) if item_kind[n] == "q"][2 * h:2 * h + 2] for h in range(XA_HEADS)]
        o_items = [[n for n in range(N_ITEMS) if item_kind[n] == "o"][2 * h:2 * h + 2] for h in range(XA_HEADS)]

        def stage_of(n):
            return (w_stage[:, n % 2], w_stage[:, n % 2], w_extra[:, 0], w_extra[:, 1])[n % 4] if n < N_KV else w_stage[:, n % 2]

        def slot_of(n):
            return n % 3 if n < N_KV else n % 2

        def parts_of(n):
            slot = slot_of(n)
            return (w_hi_extra, w_lo_extra) if slot == 2 else (w_hi[:, slot], w_lo[:, slot])

        def wait_item_in(eng, n):
            if n < N_KV:
                eng.wait_ge(w_in[n % 4], 16 * (n // 4 + 1))
            else:
                eng.wait_ge(w_in[n % 2], 16 * (N_KV // 4 + (n - N_KV) // 2 + 1))

        def wait_item_used(eng, n):
            if item_kind[n] == "v":
                eng.wait_ge(v_done, n - KT + 1)
            else:
                eng.wait_ge(use_done, first_use[n + 1])

        def wait_q(eng, h):
            last = first_use[q_items[h][1] + 1]
            for j in range(2):
                eng.wait_ge(use_free[j], last // 2)

        def wait_x2(eng, v):
            u = first_use[o_items[XA_HEADS - 1][0]] + v
            eng.wait_ge(use_free[u % 2], u // 2 + 1)

        block = scope.enter_context(nc.Block())

        @block.sync
        def _(sp):
            for j in range(4):
                sp.dma_start(stage_of(j), w_items[j]).then_inc(w_in[j], 16)
            with sp.Fori(1, N_KV // 4) as i:
                for j in range(4):
                    sp.wait_ge(w_ready, 4 * i + j - 3)
                    sp.dma_start(stage_of(j), item_of(w_items, 4 * i + j)).then_inc(w_in[j], 16)
            with sp.Fori(N_KV // 2, N_ITEMS // 2) as i:
                for j in range(2):
                    sp.wait_ge(w_ready, 2 * i + j - 1)
                    sp.dma_start(w_stage[:, j], item_of(w_items, 2 * i + j)).then_inc(w_in[j], 16)
            for m in range(KT):
                for half in range(2):
                    wait_x2(sp, 2 * m + half)
                sp.dma_start(x2_dram[m], x[:, m]).then_inc(x_stored, 16)
            sp.wait_ge(x_stored, 16 * KT)

        @block.tensor
        def _(pe):
            def column_sums(bank, width, src, done):
                last = nc.tensor.matmul(psum[:, bank, 0:width], ones[:], src, start=True, stop=True)
                last.then_inc(done, 1)

            def three(out, lhs, rhs, start, stop):
                for a, b in PASSES:
                    last = nc.tensor.matmul(out, lhs(a), rhs(b), start=(start and (a, b) == (0, 0)), stop=(stop and a == 1))
                return last

            for half in range(2):
                column_sums(half, HALF, ssq[:, cols(half)], norm_sum)

            def wait_use(u):
                if u >= 2:
                    pe.wait_ge(use_free[u % 2], u // 2)

            def wait_item(n):
                pe.wait_ge(w_ready, n + 1)

            pe.wait_ge(norm_root, 2)
            for n in range(KT):
                wait_item(n)
                wait_use(n)
                for k in range(KT):
                    last = three(psum[:, n % 2, 0:MEM], lambda a: parts_of(n)[a][:, k * P:(k + 1) * P],
                                 lambda b: M[b][:, k], k == 0, k == KT - 1)
                last.then_inc(use_done, 1)
            for c in range(2):
                for kq in range(KT // 2):
                    n = KT + c * KT // 2 + kq
                    wait_item(n)
                    for kk in range(2):
                        k = 2 * kq + kk
                        for mt in range(MT):
                            for a, b in PASSES:
                                last = nc.tensor.matmul(psum[:, ZB + 2 * c + mt], M[b][:, k, mt * P:(mt + 1) * P],
                                                        parts_of(n)[a][:, kk * HALF:(kk + 1) * HALF],
                                                        start=(k == 0 and (a, b) == (0, 0)), stop=(k == KT - 1 and a == 1))
                    last.then_inc(v_done, 1)

            def q_item(h, i):
                n = q_items[h][i]
                wait_item(n)
                for half in range(2):
                    wait_use(first_use[n] + half)
                    for k in range(KT):
                        if h == 0 and i == 0 and half == 0:
                            pe.wait_ge(h_lo_done, k + 1)
                        last = three(psum[:, half], lambda a: parts_of(n)[a][:, k * P:(k + 1) * P],
                                     lambda b: H[b][:, k, cols(half)], k == 0, k == KT - 1)
                    last.then_inc(use_done, 1)

            def o_item(h, i):
                n = o_items[h][i]
                wait_item(n)
                if i == 0:
                    pe.wait_ge(y_lo_done, 4 * h + 4)
                for m in range(KT // 2):
                    for half in range(2):
                        wait_use(first_use[n] + 2 * m + half)
                        for kk in range(DT):
                            last = three(psum[:, half], lambda a: parts_of(n)[a][:, (kk * 4 + m) * P:(kk * 4 + m + 1) * P],
                                         lambda b: Y[b][:, kk, cols(half)], kk == 0, kk == DT - 1)
                        last.then_inc(use_done, 1)

            def logits(h, half):
                s = 2 * h + half
                if half == 0:
                    wait_q(pe, h)
                if s:
                    pe.wait_ge(exp_done, QB * s)
                else:
                    pe.wait_ge(v_lo_done, 4)
                for qb in range(QB):
                    for kt in range(DT):
                        last = three(psum[:, ZB + qb // 2, qb % 2 * MEM:(qb % 2 + 1) * MEM],
                                     lambda a: Q[a][:, kt, half * HALF + qb * P:half * HALF + (qb + 1) * P],
                                     lambda b: K[b][:, DT * h + kt], kt == 0, kt == DT - 1)
                last.then_inc(z_done, 1)

            def transposes(h, half):
                s = 2 * h + half
                pe.wait_ge(p_done, s + 1)
                if s:
                    pe.wait_ge(pt_lo_done, 2 * s)
                for mt in range(MT):
                    for qb in range(QB):
                        last = nc.tensor.transpose(psum[:, TB + mt, qb * P:(qb + 1) * P],
                                                   p_buf[:, s % 2, qb, mt * P:(mt + 1) * P], ident[:])
                last.then_inc(t_done, 1)

            def values(h, half):
                s = 2 * h + half
                pe.wait_ge(pt_lo_done, 2 * s + 2)
                if s:
                    pe.wait_ge(y_lo_done, 2 * s)
                for dt in range(DT):
                    for mt in range(MT):
                        at_v = h * XA_DIM + dt * P
                        last = three(psum[:, OB + dt], lambda a: V[a][:, mt, at_v:at_v + P],
                                     lambda b: PT[b][:, mt], mt == 0, mt == MT - 1)
                last.then_inc(pv_done, 1)

            for i in range(DT):
                q_item(0, i)
            for h in range(XA_HEADS):
                logits(h, 0)
                if h:
                    for i in range(2):
                        o_item(h - 1, i)
                transposes(h, 0)
                logits(h, 1)
                values(h, 0)
                if h < XA_HEADS - 1:
                    for i in range(DT):
                        q_item(h + 1, i)
                transposes(h, 1)
                values(h, 1)
            for i in range(2):
                o_item(XA_HEADS - 1, i)

        @block.scalar
        def _(act_e):
            def split_hi(n):
                if n < N_ITEMS:
                    wait_item_in(act_e, n)
                    before = [m for m in range(n) if slot_of(m) == slot_of(n)]
                    if before:
                        wait_item_used(act_e, before[-1])
                    nc.scalar.activation(parts_of(n)[0], stage_of(n), ACT.Copy).then_inc(w_hi_done, 1)

            split_hi(0)
            split_hi(1)
            act_e.wait_ge(norm_sum, 2)
            for half in range(2):
                nc.scalar.activation(rstd[:, cols(half)], psum[:, half], ACT.Sqrt, bias=eps[:], scale=1.0 / D).then_inc(norm_root, 1)

            def h_hi_part(k):
                act_e.wait_ge(h_scaled, k + 1)
                nc.scalar.activation(h_hi[:, k], h_f32[:, k % 2], ACT.Copy).then_inc(h_hi_done, 1)

            for n in range(KT):
                split_hi(n + 2)
                act_e.wait_ge(use_done, n + 1)
                nc.scalar.activation(k_hi[:, n], psum[:, n % 2, 0:MEM], ACT.Copy).then_inc(use_hi, 1)
                h_hi_part(n)
            for c in range(2):
                for kq in range(KT // 2):
                    n = KT + c * KT // 2 + kq
                    if n + 2 <= N_KV:
                        split_hi(n + 2)
                act_e.wait_ge(v_done, (c + 1) * KT // 2)
                for mt in range(MT):
                    nc.scalar.activation(v_hi[:, mt, cols(c)], psum[:, ZB + 2 * c + mt], ACT.Copy).then_inc(v_hi_done, 1)

            def q_part(h, i):
                n = q_items[h][i]
                split_hi(n + 1)
                for half in range(2):
                    act_e.wait_ge(use_done, first_use[n] + half + 1)
                    if h:
                        act_e.wait_ge(z_done, 2 * h)
                    nc.scalar.activation(q_hi[:, i, cols(half)], psum[:, half], ACT.Copy).then_inc(use_hi, 1)

            def exps(h, half):
                s = 2 * h + half
                act_e.wait_ge(neg_done, s + 1)
                if s >= 2:
                    act_e.wait_ge(t_done, s - 1)
                for qb in range(QB):
                    nc.scalar.activation(p_buf[:, s % 2, qb], psum[:, ZB + qb // 2, qb % 2 * MEM:(qb % 2 + 1) * MEM], ACT.Exp,
                                         bias=stats[:, 1, s % 2, qb:qb + 1], scale=SCALE,
                                         accum_out=stats[:, 2, s % 2, qb:qb + 1]).then_inc(exp_done, 1)

            def pt_part(h, half):
                s = 2 * h + half
                act_e.wait_ge(t_done, s + 1)
                if s:
                    act_e.wait_ge(pv_done, s)
                for mt in range(MT):
                    nc.scalar.activation(pt_hi[:, mt], psum[:, TB + mt], ACT.Copy).then_inc(pt_hi_done, 1)

            def y_part(h, half):
                s = 2 * h + half
                act_e.wait_ge(pv_done, s + 1)
                if h and half == 0:
                    wait_item_used(act_e, o_items[h - 1][1])
                for dt in range(DT):
                    nc.scalar.activation(y_hi[:, dt, cols(half)], psum[:, OB + dt], ACT.Copy).then_inc(y_hi_done, 1)

            for i in range(DT):
                q_part(0, i)
            for h in range(XA_HEADS):
                exps(h, 0)
                if h:
                    for n in o_items[h - 1]:
                        split_hi(n + 1)
                pt_part(h, 0)
                exps(h, 1)
                y_part(h, 0)
                if h < XA_HEADS - 1:
                    for i in range(DT):
                        q_part(h + 1, i)
                pt_part(h, 1)
                y_part(h, 1)
            split_hi(o_items[XA_HEADS - 1][0] + 1)
            for u in range(2 * KT):
                wait_x2(act_e, u)
                if u >= 2:
                    act_e.wait_ge(ssq_step, u - 1)
                else:
                    act_e.wait_ge(pt_lo_done, 4 * XA_HEADS)
                    act_e.wait_ge(pv_done, 2 * XA_HEADS)
                nc.scalar.activation(sq[:, u % 2], x[:, u // 2, cols(u % 2)], ACT.Square).then_inc(sq_done, 1)

        @block.gpsimd
        def _(pool):
            def split_lo(n, hi, lo, stage):
                pool.wait_ge(w_hi_done, n + 1)
                nc.gpsimd.tensor_tensor(lo, stage, hi.bitcast(F32), ALU.subtract).then_inc(w_ready, 1)

            for n in range(N_KV):
                split_lo(n, *parts_of(n), stage_of(n))
            with pool.Fori(N_KV // 2, N_ITEMS // 2) as i:
                for j in range(2):
                    split_lo(2 * i + j, w_hi[:, j], w_lo[:, j], w_stage[:, j])

        @block.vector
        def _(dve):
            def free(ins, u):
                ins.then_inc(use_free[u % 2], 1)

            for half in range(2):
                dve.wait_ge(norm_root, half + 1)
                nc.vector.reciprocal(rstd[:, cols(half)], rstd[:, cols(half)]).then_inc(norm_rstd, 1)
            nc.vector.memset(ssq[:], 0.0).then_inc(ssq_step, 1)
            dve.wait_ge(norm_rstd, 2)

            def h_scale(k):
                if k >= 2:
                    dve.wait_ge(h_lo_done, k - 1)
                nc.vector.scalar_tensor_tensor(h_f32[:, k % 2], x[:, k], gains[:, g_xa + k:g_xa + k + 1], rstd[:],
                                               ALU.mult, ALU.mult).then_inc(h_scaled, 1)

            h_scale(0)
            h_scale(1)
            for n in range(KT):
                dve.wait_ge(use_hi, n + 1)
                free(nc.vector.tensor_tensor(k_lo[:, n], psum[:, n % 2, 0:MEM], k_hi[:, n].bitcast(F32), ALU.subtract), n)
                dve.wait_ge(h_hi_done, n + 1)
                nc.vector.tensor_tensor(h_lo[:, n], h_f32[:, n % 2], h_hi[:, n].bitcast(F32), ALU.subtract).then_inc(h_lo_done, 1)
                if n + 2 < KT:
                    h_scale(n + 2)
            for c in range(2):
                for mt in range(MT):
                    dve.wait_ge(v_hi_done, 2 * c + mt + 1)
                    nc.vector.tensor_tensor(v_lo[:, mt, cols(c)], psum[:, ZB + 2 * c + mt], v_hi[:, mt, cols(c)].bitcast(F32),
                                            ALU.subtract).then_inc(v_lo_done, 1)

            def q_part(h, i):
                u = first_use[q_items[h][i]]
                taken = KT + 4 * h + 2 * i
                for half in range(2):
                    dve.wait_ge(use_hi, taken + half + 1)
                    free(nc.vector.tensor_tensor(q_lo[:, i, cols(half)], psum[:, half], q_hi[:, i, cols(half)].bitcast(F32),
                                                 ALU.subtract), u + half)

            def z_step(h, half):
                s = 2 * h + half
                z = psum[:, ZB:ZB + 2, :].rearrange("p b (q m) -> p (b q) m", m=MEM)
                dve.wait_ge(z_done, s + 1)
                nc.vector.tensor_reduce(stats[:, 0, s % 2], z, AX.X, ALU.max).then_inc(max_done, 1)
                dve.wait_ge(max_done, s + 1)
                nc.vector.tensor_scalar(stats[:, 1, s % 2], stats[:, 0, s % 2], -SCALE, None, ALU.mult).then_inc(neg_done, 1)
                dve.wait_ge(exp_done, QB * (s + 1))
                nc.vector.reciprocal(stats[:, 3, s % 2], stats[:, 2, s % 2]).then_inc(rec_done, 1)
                dve.wait_ge(rec_done, s + 1)
                nc.vector.tensor_tensor(p_buf[:, s % 2], p_buf[:, s % 2],
                                        stats[:, 3, s % 2].unsqueeze(2).to_broadcast([P, QB, MEM]), ALU.mult).then_inc(p_done, 1)

            def pt_part(h, half):
                s = 2 * h + half
                for mt in range(MT):
                    dve.wait_ge(pt_hi_done, 2 * s + mt + 1)
                    nc.vector.tensor_tensor(pt_lo[:, mt], psum[:, TB + mt], pt_hi[:, mt].bitcast(F32), ALU.subtract).then_inc(pt_lo_done, 1)

            def y_part(h, half):
                s = 2 * h + half
                for dt in range(DT):
                    dve.wait_ge(y_hi_done, 2 * s + dt + 1)
                    nc.vector.tensor_tensor(y_lo[:, dt, cols(half)], psum[:, OB + dt], y_hi[:, dt, cols(half)].bitcast(F32),
                                            ALU.subtract).then_inc(y_lo_done, 1)

            def o_part(h, i):
                n = o_items[h][i]
                for q in range(8):
                    u = first_use[n] + q
                    dve.wait_ge(use_done, u + 1)
                    dst = x[:, 4 * i + q // 2, cols(q % 2)]
                    ins = nc.vector.tensor_tensor(dst, dst, psum[:, q % 2], ALU.add)
                    free(ins, u)
                    if h == XA_HEADS - 1 and 8 * i + q:
                        add_square(8 * i + q - 1)

            def add_square(u):
                dve.wait_ge(sq_done, u + 1)
                dve.wait_ge(ssq_step, max(u, 1))
                nc.vector.tensor_tensor(ssq[:, cols(u % 2)], ssq[:, cols(u % 2)], sq[:, u % 2], ALU.add).then_inc(ssq_step, 1)

            for i in range(DT):
                q_part(0, i)
            for h in range(XA_HEADS):
                z_step(h, 0)
                if h:
                    for i in range(2):
                        o_part(h - 1, i)
                pt_part(h, 0)
                z_step(h, 1)
                y_part(h, 0)
                if h < XA_HEADS - 1:
                    for i in range(DT):
                        q_part(h + 1, i)
                pt_part(h, 1)
                y_part(h, 1)
            for i in range(2):
                o_part(XA_HEADS - 1, i)
            add_square(2 * KT - 1)


HEADS = 8
HD = 64
PAIRS = HEADS // 2
SC = 512
BT = SC // P
QT = S // P
TOPK = 256
FULL = TOPK // P
NEG = -1e30
NOT_CAUSAL = -2e38
TAKEN = -3e38


def build_mixer(nc, ctx, at, psum, shared, w_items, x_dram, mem_dram, wi_dram, taps_dram, spill, merged_dram, yc_dram):
    x, ssq, gains, ones, ident, eps = (shared[n] for n in ("x", "ssq", "gains", "ones", "ident", "eps"))
    I_IDX = 0
    I_CONV = I_IDX + BT + 1
    I_A = I_CONV + 3 * BT
    I_C0 = I_A + 3 * PAIRS
    N_C0 = 4
    I_BM = I_C0 + N_C0
    I_C1 = I_BM + 2 * KT
    I_AM = I_C1 + 3 * PAIRS - N_C0
    I_CM = I_AM + 2 * KT
    I_MIX = I_CM + 2 * KT
    N_ITEMS = I_MIX + KT
    assert I_C1 - I_A - 3 * PAIRS == N_C0 + 2 * KT and 3 * PAIRS - N_C0 == 2 * PAIRS
    STEPS = 2 * QT
    SCALE = HD ** -0.5

    UNITS = [(1, 0), (1, 1), (0, 0), (0, 1), (3, 0), (3, 1), (2, 0), (2, 1)]

    def block_of(i):
        return 2 * UNITS[i // 2][0] + 1 - i % 2

    def head_of(i):
        return UNITS[i // 2][1]

    def groups(k):
        u, h = UNITS[k]
        found = [(t, 4 if t < 2 * u else 3) for t in range(0, 2 * u + 2, 2)]
        return found[::-1] if h else found

    VG = 2
    g_base = [VG + sum(len(groups(j)) for j in range(k)) for k in range(len(UNITS) + 1)]
    NG = g_base[-1]
    assert NG % 2 == 0
    FILL_A = {1: [(0, 0)], 8: [(0, 1)], 10: [(1, 0)], 15: [(1, 1)]}
    FILL_C = {1: [(0, 0)], 8: [(0, 1)], 9: [(1, 0), (1, 1)], 12: [(2, 0)], 13: [(2, 1)], 14: [(3, 0)], 15: [(3, 1)]}
    NARROW = STEPS // 2

    def p_at(i):
        return i * HALF if i < NARROW else i % 4 * S

    def r_at(i):
        return i % 4 * HALF if i < NARROW else i % 2 * S

    def user_before(place, i):
        size = lambda j: HALF if j < NARROW else S
        users = [j for j in range(i) if place(j) < place(i) + size(i) and place(i) < place(j) + size(j)]
        return max(users) + 1 if users else 0

    def units_before(place, i):
        steps = user_before(place, i)
        return g_base[(steps + 1) // 2] if steps else 0

    def schedule(fill):
        ahead = [6, 8, 9, 11, 11, 13, 15, 16]
        events, due, outputs = [], None, 0
        unweighed = []

        def logits_to(n):
            for i in range(sum(e[0] == "logits" for e in events), n):
                events.append(("logits", i))
                if i >= NARROW:
                    unweighed.append(i)
                if i == STEPS - 1:
                    events.append(("last logits",))
                events.extend(("fill", o, half) for o, half in fill.get(i, ()))
                if i == 1:
                    events.append(("v",))

        for k in range(len(UNITS)):
            logits_to(ahead[k])
            for r in range(len(groups(k))):
                if 2 * k in unweighed or 2 * k + 1 in unweighed:
                    events.extend(("weigh", unweighed.pop(0)) for _ in range(len(unweighed)))
                events.append(("transposes", k, r))
                if due:
                    events.append(("values", *due))
                    if due[0] == NARROW // 2 - 1 and not outputs:
                        outputs = len(events)
                due = k, r
                events.extend(("weigh", unweighed.pop(0)) for _ in range(len(unweighed)))
                if k >= NARROW // 2 and r == 0:
                    logits_to(min(2 * k + 4, STEPS))
        events += [("values", *due), ("outputs", 1)]
        events.insert(outputs + 3, ("outputs", 0))
        return events

    with ExitStack() as scope:
        def sem(name):
            return ctx.enter_context(nc.semaphore("m_" + name))

        h_hi = at("m_h_hi", 8192, [P, KT, S], F32R)
        h_lo = at("m_h_lo", 16384, [P, KT, S], F32R)
        w_hi = at("m_w_hi", 24576, [P, 2, WORDS], F32R)
        w_lo = at("m_w_lo", 26624, [P, 2, WORDS], F32R)
        y_hi = at("m_y_hi", 28672, [P, BT, S], F32R)
        y_lo = at("m_y_lo", 32768, [P, BT, S], F32R)
        q_hi = at("m_q_hi", 36864, [P, S], F32R)
        q_lo = at("m_q_lo", 37888, [P, S], F32R)
        k_hi = at("m_k_hi", 38912, [P, S], F32R)
        k_lo = at("m_k_lo", 39936, [P, S], F32R)
        v_hi = at("m_v_hi", 40960, [P, QT, 3 * HD], F32R)
        v_lo = at("m_v_lo", 42496, [P, QT, 3 * HD], F32R)
        t_hi = at("m_t_hi", 44032, [P, 2, HALF], F32R)
        t_lo = at("m_t_lo", 45056, [P, 2, HALF], F32R)
        w_stage = at("m_w_stage", 46080, [P, 2, WORDS])
        v_stage = at("m_v_stage", 48128, [P, S])
        small = at("m_small", 52528, [P, 232])
        bias_at = [52768, 52832, 52960, 49152, 49408, 49728, 50112, 50560]
        bias = [at(f"m_bias{qb}", bias_at[qb], [P, (qb + 1) * P], BF16) for qb in range(QT)]
        est = at("m_est", 51200, [P, 2, HALF])
        iq_hi, iq_lo = y_hi, y_lo
        ik_hi = at("m_ik_hi", 36864, [P, S], F32R)
        ik_lo = at("m_ik_lo", 37888, [P, S], F32R)
        wi = at("m_wi", 38912, [P, KT, HEADS])
        wi_hi = at("m_wi_hi", 38976, [P, KT, HEADS], F32R)
        wi_lo = at("m_wi_lo", 39040, [P, KT, HEADS], F32R)
        wi_rows = at("m_wi_rows", 40960, [HEADS, S])
        score_at = {qb: sum((b + 1) * P for b in range(FULL, qb)) for qb in range(FULL, QT)}
        score = {qb: at(f"m_score{qb}", score_at[qb], [P, (qb + 1) * P]) for qb in range(FULL, QT)}
        relu = at("m_relu", 4224, [P, 2, S])
        norm_sq = at("m_norm_sq", 28672, [P, 2, S])
        u_pad = at("m_u_pad", 4224, [P, S + 2])
        c_buf = at("m_c_buf", 5256, [P, S])
        x_buf = at("m_x_buf", 6280, [P, S])
        c_acc = v_stage
        b_buf = at("m_b_buf", 51200, [P, S])
        proj = at("m_proj", 5120, [P, 2, HALF])
        gate = at("m_gate", 6144, [P, 2, HALF])
        prev = at("m_prev", 7168, [P, 2, HALF])
        k_stage = at("m_k_stage", 0, [P, S])
        q_stage = v_stage
        p_buf = at("m_p_buf", 1024, [P, 4 * S])
        r_buf = at("m_r_buf", 5120, [P, 2 * S])
        yc = [at("m_yc0", 0, [P, S]), at("m_yc1", 48128, [P, S]), at("m_yc2", 51200, [P, S])]
        m_far = at("m_m_far", 0, [P, KT // 2, S])
        m_hi = at("m_m_hi", 36864, [P, KT // 2, S], F32R)
        m_lo = at("m_m_lo", 40960, [P, KT // 2, S], F32R)
        n_hi = at("m_n_hi", 8192, [P, KT // 2, S], F32R)
        n_lo = at("m_n_lo", 12288, [P, KT // 2, S], F32R)
        x_again = at("m_x_again", 16384, [P, KT, S])
        mix_sq = at("m_mix_sq", 45056, [P, 2, HALF])
        m_sq = at("m_m_sq", 28672, [P, KT, MEM])
        mem_hi, mem_lo = shared["memory"]
        m_raw = at("m_m_raw", 34816, [P, KT, MEM])
        m_ssq = at("m_m_ssq", 48128, [P, MEM])
        m_rstd = at("m_m_rstd", 48384, [P, MEM])
        taps = small[:, 0:12]
        rstd = small[:, 104:104 + S // P]
        top8 = small[:, 16:24]
        wi_q = small[:, 24:88]
        stats = small[:, 88:104]
        H, W, Y = (h_hi, h_lo), (w_hi, w_lo), (y_hi, y_lo)
        IQ, IK, WI = (iq_hi, iq_lo), (ik_hi, ik_lo), (wi_hi, wi_lo)
        Q, K, V, T = (q_hi, q_lo), (k_hi, k_lo), (v_hi, v_lo), (t_hi, t_lo)
        ZB, TB, OB = 2, 4, 6

        x_in = [sem(f"x_in{j}") for j in range(4)]
        consts_in = sem("consts_in")
        const_set = sem("const_set")
        norm_sq_done = sem("norm_sq_done")
        ssq_step = sem("ssq_step")
        norm_sum = sem("norm_sum")
        norm_root = sem("norm_root")
        norm_rstd = sem("norm_rstd")
        norm_wide = sem("norm_wide")
        h_scaled = sem("h_scaled")
        h_hi_done = sem("h_hi_done")
        h_lo_dve = sem("h_lo_dve")
        h_lo_pool = sem("h_lo_pool")
        w_in = [sem(f"w_in{j}") for j in range(2)]
        w_hi_done = sem("w_hi_done")
        w_ready = sem("w_ready")
        halves_done = sem("halves_done")
        bank_free = [sem(f"bank_free{j}") for j in range(2)]
        idx_hi = sem("idx_hi")
        wi_hi_done = sem("wi_hi_done")
        wi_lo_done = sem("wi_lo_done")
        wi_sum = sem("wi_sum")
        wi_out = sem("wi_out")
        wi_turned = sem("wi_turned")
        wi_done = sem("wi_done")
        iz_done = sem("iz_done")
        relu_done = sem("relu_done")
        score_step = sem("score_step")
        masked = sem("masked")
        topk_step = sem("topk_step")
        bias_done = sem("bias_done")
        bias_first = sem("bias_first")
        c_act = sem("c_act")
        c_pool = sem("c_pool")
        spilled = [sem(f"spilled{j}") for j in range(2)]
        merge_mult = sem("merge_mult")
        merge_done = sem("merge_done")
        prev_in = [sem(f"prev_in{j}") for j in range(2)]
        merged_out = [sem(f"merged_out{j}") for j in range(2)]
        q_in, k_in, v_in = sem("q_in"), sem("k_in"), sem("v_in")
        qk_hi_done = sem("qk_hi_done")
        qk_lo_done = sem("qk_lo_done")
        z_done = sem("z_done")
        sig_done = sem("sig_done")
        sel_done = sem("sel_done")
        scan_done = sem("scan_done")
        p_done = sem("p_done")
        t_done = sem("t_done")
        t_hi_done = sem("t_hi_done")
        t_lo_done = sem("t_lo_done")
        pv_done = sem("pv_done")
        o_hi_done = sem("o_hi_done")
        o_free = [sem(f"o_free{j}") for j in range(2)]
        add_done = sem("add_done")
        exp_done = sem("exp_done")
        rec_done = sem("rec_done")
        yc_in = sem("yc_in")
        yc_hi_done = sem("yc_hi_done")
        yc_lo_done = sem("yc_lo_done")
        m_hi_done = sem("m_hi_done")
        m_lo_done = sem("m_lo_done")
        n_hi_done = sem("n_hi_done")
        n_lo_done = sem("n_lo_done")
        x_again_in = sem("x_again_in")
        mem_in = sem("mem_in")
        m_sq_done = sem("m_sq_done")
        m_step = sem("m_step")
        m_sum = sem("m_sum")
        m_root = sem("m_root")
        mem_hi_done = sem("mem_hi_done")
        mem_lo_done = sem("mem_lo_done")
        mix_sq_done = sem("mix_sq_done")
        mix_ssq = sem("mix_ssq")
        dve_passed, pool_passed = sem("dve_passed"), sem("pool_passed")

        def v_place(v, r):
            return v[:, 4 * r:4 * r + 4].rearrange("p s (c d) -> p s c d", c=3)[:, :, 0:3:2]

        def v_bank(r):
            return psum[:, TB + r].rearrange("p (s c d) -> p s c d", s=4, c=2)

        def logit_banks(i):
            if i < NARROW:
                return psum[:, ZB + i % 2, 0:(block_of(i) + 1) * P]
            return psum[:, ZB:ZB + 2, :].rearrange("p b c -> p (b c)")[:, 0:(block_of(i) + 1) * P]

        def p_of(i):
            return p_buf[:, p_at(i):p_at(i) + (block_of(i) + 1) * P]

        FIRST_SCORES = (QT - FULL) * HEADS
        SPILLS = 6 * PAIRS

        block = scope.enter_context(nc.Block())

        @block.sync
        def _(sp):
            for half in range(2):
                sp.sem_inc(merged_out[half], 16)
            for j in range(4):
                sp.dma_start(x[:, 2 * j:2 * j + 2], x_dram[2 * j:2 * j + 2].rearrange("k p t -> p k t")).then_inc(x_in[j], 16)
            sp.dma_start(wi[:], wi_dram).then_inc(consts_in, 16)
            sp.dma_start(taps, taps_dram).then_inc(consts_in, 16)
            sp.dma_start(gains[:], shared["gains_dram"]).then_inc(consts_in, 16)

            def weight(n, slot, words=WORDS):
                sp.wait_ge(w_ready, n + 1)
                sp.dma_start(w_stage[:, slot, 0:words], item_of(w_items, n)[:, 0:words]).then_inc(w_in[slot], 16)

            def store_merged(m, merged=merge_done):
                for half in range(2):
                    sp.wait_ge(merged, 2 * m + half + 2)
                    sp.dma_start(item_of(merged_dram, m)[:, cols(half)], gate[:, half]).then_inc(merged_out[half], 16)

            weight(0, 0)
            with sp.Fori(0, (I_BM - 1) // 2) as i:
                for o in range(2):
                    weight(2 * i + o + 1, 1 - o)
            weight(I_BM, I_BM % 2)
            weight(I_BM + 1, 1 - I_BM % 2, HALF)
            with sp.Fori(0, KT - 1) as m:
                weight(2 * m + I_BM + 2, I_BM % 2)
                weight(2 * m + I_BM + 3, 1 - I_BM % 2, HALF)
                store_merged(m, merge_mult)
            def qkv(g):
                sp.wait_ge(qk_lo_done, 2 * g)
                sp.dma_start(k_stage[:], item_of(spill, 3 * g + 1)).then_inc(k_in, 16)
                sp.wait_ge(t_done, (NG * (g - 1) + VG if not isinstance(g, int) or g else 0) + 1)
                sp.dma_start(q_stage[:], item_of(spill, 3 * g)).then_inc(q_in, 16)

            def v_load(g):
                sp.wait_ge(qk_lo_done, 2 * g + 1)
                sp.dma_start(v_stage[:], item_of(spill, 3 * g + 2)).then_inc(v_in, 16)

            for half in range(2):
                sp.wait_ge(spilled[half], 16 * (3 * PAIRS + N_C0) + 16)
            sp.wait_ge(bias_done, QT - FULL)
            sp.wait_ge(bias_first, FULL)
            qkv(0)
            weight(I_C1, I_C1 % 2)
            store_merged(KT - 1, merge_mult)
            v_load(0)
            with sp.Fori(1, PAIRS) as p:
                for o in range(2):
                    weight(2 * p + I_C1 - 1 + o, (I_C1 + 1 + o) % 2)
                qkv(p)
                v_load(p)
            for o in range(2):
                weight(I_AM - 1 + o, (I_AM + 1 + o) % 2)

            def merge_loads(m, base):
                for half in range(2):
                    sp.wait_ge(merge_done, 2 * m + 1)
                    sp.dma_start(prev[:, half], item_of(merged_dram, m)[:, cols(half)]).then_inc(prev_in[half], 16)
                weight(base + 1, 1 - I_AM % 2, HALF)
                weight(base + 2, I_AM % 2)

            sp.wait_ge(merged_out[0], 16 * KT + 16)
            sp.wait_ge(merged_out[1], 16 * KT + 16)
            qkv(PAIRS)
            v_load(PAIRS)
            for half in range(2):
                sp.wait_ge(spilled[half], 16 * SPILLS + 16)
            with sp.Fori(1, PAIRS) as p:
                merge_loads(2 * p - 2, 4 * p + I_AM - 4)
                store_merged(2 * p - 2)
                qkv(p + PAIRS)
                merge_loads(2 * p - 1, 4 * p + I_AM - 2)
                v_load(p + PAIRS)
                store_merged(2 * p - 1)
            merge_loads(KT - 2, I_AM + 2 * (KT - 2))
            store_merged(KT - 2)
            sp.wait_ge(qk_lo_done, 4 * PAIRS)
            sp.wait_ge(t_done, NG * (2 * PAIRS - 1) + VG + 1)
            for half in range(2):
                sp.wait_ge(spilled[half], 16 * (SPILLS + PAIRS - 1) + 16)
            for k in range(BT - 1):
                sp.dma_start(yc[k][:], yc_dram[k]).then_inc(yc_in, 16)
            merge_loads(KT - 1, I_AM + 2 * (KT - 1))
            store_merged(KT - 1)
            for half in range(2):
                sp.wait_ge(merged_out[half], 16 * 2 * KT + 16)
            weight(I_CM + 1, 1 - I_CM % 2, HALF)

            def prev_load(m):
                for half in range(2):
                    sp.wait_ge(merge_done, 2 * KT + 2 * m + 1)
                    sp.dma_start(prev[:, half], item_of(merged_dram, m)[:, cols(half)]).then_inc(prev_in[half], 16)

            prev_load(0)
            with sp.Fori(1, KT) as m:
                weight(2 * m + I_CM, I_CM % 2)
                weight(2 * m + I_CM + 1, 1 - I_CM % 2, HALF)
                prev_load(m)
            for o in range(2):
                weight(I_MIX + o, (I_MIX + o) % 2)
            sp.wait_ge(halves_done, 4 + 2 * (I_MIX - 1))
            for m in range(KT):
                sp.dma_start(x_again[:, m], x_dram[m]).then_inc(x_again_in, 16)
            sp.wait_ge(halves_done, 4 + 2 * I_MIX)
            sp.dma_start(m_raw[:], mem_dram.rearrange("k p t -> p k t")).then_inc(mem_in, 16)
            with sp.Fori(1, KT // 2) as i:
                for o in range(2):
                    weight(2 * i + I_MIX + o, (I_MIX + o) % 2)

        @block.tensor
        def _(pe):
            def three(out, lhs, rhs, start, stop):
                for a, b in PASSES:
                    last = nc.tensor.matmul(out, lhs(a), rhs(b), start=(start and (a, b) == (0, 0)), stop=(stop and a == 1))
                return last

            def item_half(n, slot, half, tiles, src, ready=None):
                if half == 0:
                    pe.wait_ge(w_ready, n + 3)
                pe.wait_ge(bank_free[half], n)
                for k in range(tiles):
                    if ready:
                        ready(k)
                    last = three(psum[:, half], lambda a: W[a][:, slot, k * P:(k + 1) * P],
                                 lambda b: src(b, k)[:, cols(half)], k == 0, k == tiles - 1)
                last.then_inc(halves_done, 1)

            def of_h(b, k):
                return H[b][:, k]

            def of_y(b, k):
                return Y[b][:, k]

            def h_ready(half):
                return lambda k: pe.wait_ge(h_lo_pool if k % 2 else h_lo_dve, half * KT // 2 + k // 2 + 1)

            pe.sem_inc(halves_done, 4)
            pe.sem_inc(pv_done, 2)
            for start_at_1 in (z_done, t_done):
                pe.sem_inc(start_at_1, 1)
            pe.wait_ge(ssq_step, KT)
            pe.wait_ge(const_set, 4)
            token_sums(nc, psum, ssq, ones).then_inc(norm_sum, 1)
            pe.wait_ge(norm_rstd, 1)
            for half in range(2):
                spread_factors(nc, psum, rstd, ident, half).then_inc(norm_wide, 1)
            item_half(0, 0, 0, KT, of_h, h_ready(0))
            item_half(0, 0, 1, KT, of_h, h_ready(1))
            for n in range(1, I_CONV):
                for half in range(2):
                    item_half(n, n % 2, half, KT, of_h)
            pe.wait_ge(wi_lo_done, 1)
            for half in range(2):
                for k in range(KT):
                    last = three(psum[0:HEADS, OB + half], lambda a: WI[a][:, k], lambda b: H[b][:, k, cols(half)], k == 0, k == KT - 1)
            last.then_inc(wi_sum, 1)
            pe.wait_ge(wi_out, 2)
            pe.wait_ge(const_set, 4)
            for t in range(QT):
                last = nc.tensor.transpose(psum[:, OB, t * HEADS:(t + 1) * HEADS], wi_rows[:, t * P:(t + 1) * P], ident[0:HEADS, 0:HEADS])
            last.then_inc(wi_turned, 1)
            for half in range(2):
                pe.wait_ge(bank_free[half], I_CONV)
            s = 0
            for qb in range(FULL, QT):
                width = (qb + 1) * P
                for h in range(HEADS):
                    lanes = slice(h % 2 * HD, h % 2 * HD + HD)
                    if s >= 2:
                        pe.wait_ge(relu_done, s - 1)
                    for c in range(0, width, HALF):
                        w = min(HALF, width - c)
                        last = three(psum[:, ZB + 2 * (s % 2) + c // HALF, 0:w], lambda a: IQ[a][lanes, h // 2, qb * P:(qb + 1) * P],
                                     lambda b: IK[b][lanes, c:c + w], True, True)
                    last.then_inc(iz_done, 1)
                    s += 1
            with pe.Fori(0, (I_BM - I_CONV) // 2) as i:
                for o in range(2):
                    for half in range(2):
                        item_half(2 * i + I_CONV + o, (I_CONV + o) % 2, half, KT, of_h)
            pe.wait_ge(c_pool, 5 * BT + 1)
            with pe.Fori(0, KT) as m:
                for o, (tiles, src) in enumerate(((KT, of_h), (BT, of_y))):
                    for half in range(2):
                        item_half(2 * m + I_BM + o, (I_BM + o) % 2, half, tiles, src)

            def v_transposes(g):
                pe.wait_ge(v_in, 16 * g + 16)
                for r in range(VG):
                    pe.wait_ge(t_lo_done, NG * g + r + 1)
                    for st in range(4):
                        last = nc.tensor.transpose(psum[:, TB + r, st * P:(st + 1) * P],
                                                   v_stage[:, (4 * r + st) * P:(4 * r + st + 1) * P], ident[:])
                    last.then_inc(t_done, 1)

            def logits(i):
                qb, h = block_of(i), head_of(i)
                lanes = slice(h * HD, h * HD + HD)
                width = (qb + 1) * P
                for c in range(0, width, HALF):
                    w = min(HALF, width - c)
                    last = three(logit_banks(i)[:, c:c + w], lambda a: Q[a][lanes, qb * P:(qb + 1) * P],
                                 lambda b: K[b][lanes, c:c + w], True, True)
                last.then_inc(z_done, 1)

            def transposes(g, k, r):
                if r == 0:
                    pe.wait_ge(p_done, STEPS * g + 2 * k + 3)
                e, (t0, count) = g_base[k] + r, groups(k)[r]
                pe.wait_ge(t_lo_done, NG * g + e + 1)
                blocks = [(t0, 1), (t0, 0), (t0 + 1, 1), (t0 + 1, 0)] if count == 4 else [(t0, 1), (t0, 0), (t0 + 1, 0)]
                for n, (t, narrower) in enumerate(blocks):
                    last = nc.tensor.transpose(psum[:, TB + e % 2, n * P:(n + 1) * P],
                                               p_of(2 * k + narrower)[:, t * P:(t + 1) * P], ident[:])
                last.then_inc(t_done, 1)

            def values(g, k, r):
                u, h = UNITS[k]
                if r == 0 and k % 4 == 0:
                    pe.wait_ge(o_free[u // 2], g + 1)
                e, (t0, count) = g_base[k] + r, groups(k)[r]
                pe.wait_ge(t_lo_done, NG * g + e + 3)
                for n in ((1, 0) if h else (0, 1)):
                    t = t0 + n
                    width = P if count == 3 and n else 2 * P
                    right = (u % 2 + 1) * 2 * P
                    last = three(psum[:, OB + u // 2, right - width:right],
                                 lambda a: V[a][:, t, h * HD:h * HD + P],
                                 lambda b: T[b][:, e % 2, n * 2 * P:n * 2 * P + width],
                                 h == 0 and t == 0, h == 1 and t == 0)
                last.then_inc(pv_done, 1)

            def attention(g, fill, filler, z_read):
                pe.wait_ge(qk_lo_done, 2 * g + 2)
                for event, *which in schedule(fill):
                    if event == "logits":
                        i = which[0]
                        z_read(max(i - 1, 0) if i < NARROW else i)
                        logits(i)
                    elif event == "v":
                        v_transposes(g)
                    elif event == "transposes":
                        transposes(g, *which)
                    elif event == "values":
                        values(g, *which)
                    elif event == "fill":
                        filler(*which)

            pe.wait_ge(const_set, 7)
            with pe.Fori(0, PAIRS) as p:
                attention(p, FILL_A, lambda o, half: item_half(2 * p + I_C1 + o, (I_C1 + o) % 2, half, KT, of_h),
                          lambda steps: pe.wait_ge(sig_done, 2 * STEPS * p + 2 * steps + 1))

            def merge_half(n0, o, half):
                item_half(n0 + o, (I_AM + o) % 2, half, *((BT, of_y) if o % 2 else (KT, of_h)))

            def sparse_pair(p):
                attention(p + PAIRS, FILL_C, lambda o, half: merge_half(4 * p + I_AM, o, half),
                          lambda steps: pe.wait_ge(add_done, STEPS * p + steps + 1))

            with pe.Fori(0, PAIRS - 1) as p:
                sparse_pair(p)
            sparse_pair(PAIRS - 1)
            with pe.Fori(0, KT) as m:
                for half in range(2):
                    item_half(2 * m + I_CM, I_CM % 2, half, KT, of_h)
                pe.wait_ge(yc_lo_done, BT + 1)
                for half in range(2):
                    item_half(2 * m + I_CM + 1, 1 - I_CM % 2, half, BT, of_y)

            def of_m(b, k):
                if k < KT // 2:
                    return (m_hi, m_lo)[b][:, k]
                return (n_hi, n_lo)[b][:, k - KT // 2]

            def m_ready(k):
                if k < KT // 2:
                    pe.wait_ge(m_lo_done, 2 * k + 2)
                else:
                    pe.wait_ge(n_lo_done, k - KT // 2 + 1)

            item_half(I_MIX, I_MIX % 2, 0, KT, of_m, m_ready)
            item_half(I_MIX, I_MIX % 2, 1, KT, of_m)
            for half in range(2):
                item_half(I_MIX + 1, 1 - I_MIX % 2, half, KT, of_m)
            pe.wait_ge(m_step, 1)
            nc.tensor.matmul(psum[:, OB, 0:MEM], ones[:], m_ssq[:], start=True, stop=True).then_inc(m_sum, 1)
            with pe.Fori(1, KT // 2) as i:
                for o in range(2):
                    for half in range(2):
                        item_half(2 * i + I_MIX + o, (I_MIX + o) % 2, half, KT, of_m)

        @block.scalar
        def _(act_e):
            def split_hi(n, slot, words=WORDS):
                act_e.wait_ge(w_in[slot], 8 * (n - slot) + 16)
                act_e.wait_ge(halves_done, 2 * n + 2)
                nc.scalar.activation(w_hi[:, slot, 0:words], w_stage[:, slot, 0:words], ACT.Copy).then_inc(w_hi_done, 1)

            def arrived(n, half):
                act_e.wait_ge(halves_done, 2 * n + half + 5)

            for start_at_1 in (exp_done, sig_done, c_act):
                act_e.sem_inc(start_at_1, 1)
            for half in range(2):
                act_e.sem_inc(spilled[half], 16)
            for k in range(KT):
                act_e.wait_ge(x_in[k // 2], 16)
                if k >= 2:
                    act_e.wait_ge(ssq_step, k - 1)
                nc.scalar.activation(norm_sq[:, k % 2], x[:, k], ACT.Square).then_inc(norm_sq_done, 1)
            act_e.wait_ge(const_set, 2)
            act_e.wait_ge(norm_sum, 1)
            nc.scalar.activation(rstd, psum[:, SUM_BANK, 0:S // P], ACT.Sqrt, bias=eps[:], scale=1.0 / D).then_inc(norm_root, 1)
            split_hi(0, 0)
            act_e.wait_ge(consts_in, 48)
            nc.scalar.activation(wi_hi[:], wi[:], ACT.Copy).then_inc(wi_hi_done, 1)
            for half in range(2):
                for k in range(KT):
                    act_e.wait_ge(h_scaled, half * KT + k + 1)
                    nc.scalar.activation(h_hi[:, k, cols(half)], x[:, k, cols(half)], ACT.Copy).then_inc(h_hi_done, 1)
            for n in range(I_CONV):
                split_hi(n + 1, (n + 1) % 2)
                for half in range(2):
                    arrived(n, half)
                    dst = iq_hi[:, n, cols(half)] if n < BT else ik_hi[:, cols(half)]
                    nc.scalar.activation(dst, psum[:, half], ACT.Copy).then_inc(idx_hi, 1)
            s = 0
            for qb in range(FULL, QT):
                width = (qb + 1) * P
                for h in range(HEADS):
                    act_e.wait_ge(iz_done, s + 1)
                    if s >= 2:
                        act_e.wait_ge(score_step, s - 1)
                    z = psum[:, ZB + 2 * (s % 2):ZB + 2 * (s % 2) + 2, :].rearrange("p b c -> p (b c)")
                    nc.scalar.activation(relu[:, s % 2, 0:width], z[:, 0:width], ACT.Relu, scale=HD ** -0.5).then_inc(relu_done, 1)
                    s += 1
            act_e.wait_ge(score_step, FIRST_SCORES)

            def copies(n, dst, before=None):
                for half in range(2):
                    arrived(n, half)
                    if before:
                        before(half)
                    nc.scalar.activation(dst(half), psum[:, half], ACT.Copy).then_inc(bank_free[half], 1)

            with act_e.Fori(0, BT // 2) as i:
                for tt in range(2):
                    t, n, slot = 2 * i + tt, 6 * i + I_CONV + 3 * tt, (I_CONV + 3 * tt) % 2
                    tap = lambda w: taps[:, bass.ds(3 * t + w, 1)]
                    split_hi(n + 1, 1 - slot)
                    act_e.wait_ge(c_pool, 5 * t + 1)
                    copies(n, lambda half: c_buf[:, cols(half)])
                    split_hi(n + 2, slot)
                    copies(n + 1, lambda half: x_buf[:, cols(half)])
                    split_hi(n + 3, 1 - slot)
                    act_e.wait_ge(c_pool, 5 * t + 2)
                    nc.scalar.activation(c_acc[:], u_pad[:, 2:S + 2], ACT.Copy, scale=tap(2)).then_inc(c_act, 1)
                    nc.scalar.activation(x_buf[:], u_pad[:, 1:S + 1], ACT.Copy, scale=tap(1)).then_inc(c_act, 1)
                    act_e.wait_ge(c_pool, 5 * t + 3)
                    nc.scalar.activation(x_buf[:], u_pad[:, 0:S], ACT.Copy, scale=tap(0)).then_inc(c_act, 1)
                    copies(n + 2, lambda half: b_buf[:, cols(half)])
                    act_e.wait_ge(c_pool, 5 * t + 5)
                    nc.scalar.activation(tile_of(y_hi, t), c_acc[:], ACT.Copy).then_inc(c_act, 1)

            def spill_half(n, tile, half):
                arrived(n, half)
                act_e.wait_ge(spilled[half], 16 * tile + 16)
                nc.scalar.activation(est[:, half], psum[:, half], ACT.Copy).then_inc(bank_free[half], 1)

            def spill_store(n, tile, half):
                act_e.wait_ge(bank_free[half], n + 1)
                act_e.dma_start(item_of(spill, tile)[:, cols(half)], est[:, half]).then_inc(spilled[half], 16)

            act_e.wait_ge(c_pool, 5 * BT + 1)
            with act_e.Fori(0, (I_BM - I_A) // 2) as i:
                for o in range(2):
                    n, tile = 2 * i + I_A + o, 2 * i + o
                    split_hi(n + 1, (I_A + o + 1) % 2)
                    for half in range(2):
                        spill_half(n, tile, half)
                        spill_store(n, tile, half)

            def gate_half(n, half, stored):
                arrived(n, half)
                act_e.wait_ge(merged_out[half], stored + 16)
                nc.scalar.activation(gate[:, half], psum[:, half], ACT.Sigmoid).then_inc(bank_free[half], 1)

            def proj_half(n, half, mults):
                arrived(n, half)
                act_e.wait_ge(merge_mult, mults + 1)
                nc.scalar.activation(proj[:, half], psum[:, half], ACT.Copy).then_inc(bank_free[half], 1)

            with act_e.Fori(0, KT) as m:
                n = 2 * m + I_BM
                split_hi(n + 1, (I_BM + 1) % 2, HALF)
                for half in range(2):
                    gate_half(n, half, 16 * m)
                split_hi(n + 2, I_BM % 2)
                for half in range(2):
                    proj_half(n + 1, half, 2 * m)

            def qk_split(g):
                act_e.wait_ge(z_done, STEPS * g + 1)
                for c, (dst, src, done) in enumerate(((q_hi, q_stage, q_in), (k_hi, k_stage, k_in))):
                    act_e.wait_ge(done, 16 * g + 16)
                    nc.scalar.activation(dst[:], src[:], ACT.Copy).then_inc(qk_hi_done, 1)

            def v_parts(g):
                act_e.wait_ge(pv_done, (NG - VG) * g + 2)
                for r in range(VG):
                    act_e.wait_ge(t_done, NG * g + r + 2)
                    nc.scalar.activation(v_place(v_hi, r), v_bank(r), ACT.Copy).then_inc(t_hi_done, 1)

            def t_part(g, k, r):
                e, count = g_base[k] + r, groups(k)[r][1]
                act_e.wait_ge(t_done, NG * g + e + 2)
                act_e.wait_ge(pv_done, (NG - VG) * g + e - VG + 1)
                nc.scalar.activation(t_hi[:, e % 2, 0:count * P], psum[:, TB + e % 2, 0:count * P], ACT.Copy).then_inc(t_hi_done, 1)

            def outputs_ready(g, half):
                act_e.wait_ge(pv_done, (NG - VG) * g + g_base[4 * (half + 1)] - VG + 2)

            qk_split(0)
            for half in range(2):
                act_e.wait_ge(merged_out[half], 16 * KT + 16)
            with act_e.Fori(0, PAIRS) as p:
                n, tile = 2 * p + I_C1, 2 * p + 3 * PAIRS + N_C0
                for event, *which in schedule(FILL_A):
                    if event == "logits":
                        i = which[0]
                        z = logit_banks(i)
                        act_e.wait_ge(z_done, STEPS * p + i + 2)
                        act_e.wait_ge(p_done, STEPS * p + user_before(r_at, i) + 1)
                        nc.scalar.activation(r_buf[:, r_at(i):r_at(i) + z.shape[1]], z, ACT.Sigmoid, scale=-SCALE).then_inc(sig_done, 1)
                        act_e.wait_ge(t_done, NG * p + units_before(p_at, i) + 1)
                        nc.scalar.activation(p_of(i), z, ACT.Sigmoid, scale=SCALE).then_inc(sig_done, 1)
                    elif event == "last logits":
                        qk_split(p + 1)
                    elif event == "v":
                        v_parts(p)
                    elif event == "transposes":
                        t_part(p, *which)
                    elif event == "fill":
                        o, half = which
                        if half == 0:
                            split_hi(n + o + 1, (I_C1 + o + 1) % 2)
                        spill_half(n + o, tile + o, half)
                        spill_store(n + o, tile + o, half)
                    elif event == "outputs":
                        half = which[0]
                        outputs_ready(p, half)
                        nc.scalar.activation(tile_of(y_hi, p)[:, cols(half)], psum[:, OB + half], ACT.Copy).then_inc(o_hi_done, 1)

            def sparse_pair(p):
                g, n = p + PAIRS, 4 * p + I_AM
                for event, *which in schedule(FILL_C):
                    if event == "logits":
                        i = which[0]
                        act_e.wait_ge(add_done, STEPS * p + i + 2)
                        act_e.wait_ge(rec_done, STEPS * p + max(i - 3, 0) + 1)
                        nc.scalar.activation(p_of(i), p_of(i), ACT.Exp, bias=stats[:, i % 4:i % 4 + 1], scale=-1.0,
                                             accum_out=stats[:, 4 + i % 4:5 + i % 4]).then_inc(exp_done, 1)
                    elif event == "last logits" and not isinstance(p, int):
                        qk_split(g + 1)
                    elif event == "v":
                        v_parts(g)
                    elif event == "transposes":
                        t_part(g, *which)
                    elif event == "fill":
                        o, half = which
                        m = 2 * p + o // 2
                        if half == 0:
                            split_hi(n + o + 1, (I_AM + o + 1) % 2, WORDS if o % 2 else HALF)
                        if o % 2 == 0:
                            gate_half(n + o, half, 16 * m + 16 * KT)
                        else:
                            proj_half(n + o, half, 2 * m + 2 * KT)
                    elif event == "outputs" and isinstance(p, int):
                        if which[0] == 1:
                            act_e.wait_ge(halves_done, 4 + 2 * I_CM)
                            for half in range(2):
                                outputs_ready(g, half)
                                nc.scalar.activation(y_hi[:, p, cols(half)], psum[:, OB + half], ACT.Copy).then_inc(o_hi_done, 1)
                    elif event == "outputs":
                        half = which[0]
                        outputs_ready(g, half)
                        act_e.wait_ge(spilled[half], 16 * p + 16 * SPILLS + 16)
                        nc.scalar.activation(est[:, half], psum[:, OB + half], ACT.Copy).then_inc(o_free[half], 1)
                        act_e.wait_ge(o_free[half], g + 2)
                        act_e.dma_start(item_of(yc_dram, p)[:, cols(half)], est[:, half]).then_inc(spilled[half], 16)

            act_e.wait_ge(p_done, STEPS * PAIRS + 1)
            with act_e.Fori(0, PAIRS - 1) as p:
                sparse_pair(p)
            sparse_pair(PAIRS - 1)
            split_hi(I_CM + 1, 1 - I_CM % 2, HALF)
            for half in range(2):
                gate_half(I_CM, half, 16 * 2 * KT)
            act_e.wait_ge(yc_in, 16 * (BT - 1))
            for k in range(BT - 1):
                nc.scalar.activation(y_hi[:, k], yc[k][:], ACT.Copy).then_inc(yc_hi_done, 1)
            split_hi(I_CM + 2, I_CM % 2)
            for half in range(2):
                proj_half(I_CM + 1, half, 2 * 2 * KT)

            def m_part(m):
                for half in range(2):
                    act_e.wait_ge(merge_done, 2 * m + 2 * KT + half + 2)
                    nc.scalar.activation(tile_of(m_hi, m)[:, cols(half)], gate[:, half], ACT.Copy).then_inc(m_hi_done, 1)

            def merge_tile(m, gate_used):
                n = 2 * m + I_CM
                split_hi(n + 1, 1 - I_CM % 2, HALF)
                for half in range(2):
                    arrived(n, half)
                    gate_used(half)
                    nc.scalar.activation(gate[:, half], psum[:, half], ACT.Sigmoid).then_inc(bank_free[half], 1)
                split_hi(n + 2, I_CM % 2)
                for half in range(2):
                    proj_half(n + 1, half, 2 * m + 4 * KT)

            with act_e.Fori(0, KT // 2) as m:
                m_part(m)
                merge_tile(m + 1, lambda half: act_e.wait_ge(m_lo_done, 2 * m + half + 1))
            with act_e.Fori(KT // 2 + 1, KT) as m:
                merge_tile(m, lambda half: act_e.wait_ge(merge_done, 2 * m + 2 * KT - 1 + half + 1))
            act_e.wait_ge(halves_done, 4 + 2 * (I_MIX - 1))
            for k in range(KT // 2):
                act_e.wait_ge(merge_done, 2 * KT + KT + 2 * k + 3)
                nc.scalar.activation(n_hi[:, k], m_far[:, k], ACT.Copy).then_inc(n_hi_done, 1)
            split_hi(I_MIX + 1, 1 - I_MIX % 2)
            for m in range(KT):
                if m and m + 1 < KT:
                    split_hi(I_MIX + m + 1, (I_MIX + m + 1) % 2)
                for half in range(2):
                    v = 2 * m + half
                    act_e.wait_ge(bank_free[half], I_MIX + m + 1)
                    if v >= 2:
                        act_e.wait_ge(mix_ssq, v - 1)
                    nc.scalar.activation(mix_sq[:, half], x[:, m, cols(half)], ACT.Square).then_inc(mix_sq_done, 1)
                if m == 0:
                    act_e.wait_ge(mem_in, 16)
                    nc.scalar.activation(m_sq[:], m_raw[:], ACT.Square).then_inc(m_sq_done, 1)
                if m == 2:
                    act_e.wait_ge(m_sum, 1)
                    nc.scalar.activation(m_rstd[:], psum[:, OB, 0:MEM], ACT.Sqrt, bias=eps[:], scale=1.0 / D).then_inc(m_root, 1)
                if m == 5:
                    act_e.wait_ge(m_step, 2 + KT)
                    nc.scalar.activation(mem_hi[:], m_raw[:], ACT.Copy).then_inc(mem_hi_done, 1)

        @block.gpsimd
        def _(pool):
            def split_lo(n, slot, words=WORDS):
                pool.wait_ge(w_hi_done, n + 1)
                nc.gpsimd.tensor_tensor(w_lo[:, slot, 0:words], w_stage[:, slot, 0:words], w_hi[:, slot, 0:words].bitcast(F32),
                                        ALU.subtract).then_inc(w_ready, 1)

            pool.sem_inc(w_ready, 2)
            for start_at_1 in (c_pool, merge_mult, merge_done, p_done):
                pool.sem_inc(start_at_1, 1)
            nc.gpsimd.memset(ones[:], 1.0).then_inc(const_set, 1)
            nc.gpsimd.memset(eps[:], EPS).then_inc(const_set, 1)
            nc.gpsimd.memset(ident[:], 0.0).then_inc(const_set, 1)
            pool.wait_ge(const_set, 3)
            nc.gpsimd.affine_select(out=ident[:], in_=ident[:], compare_op=ALU.not_equal, fill=1.0, base=0,
                                    pattern=[[-1, P]], channel_multiplier=1).then_inc(const_set, 1)
            for qb in range(FULL):
                nc.gpsimd.memset(bias[qb][:], 0.0).then_inc(const_set, 1)
            pool.wait_ge(const_set, 6)
            for qb in range(FULL):
                diag = bias[qb][:, qb * P:(qb + 1) * P]
                nc.gpsimd.affine_select(out=diag, in_=diag, compare_op=ALU.is_ge, fill=NEG, base=0,
                                        pattern=[[-1, P]], channel_multiplier=1).then_inc(bias_first, 1)
            split_lo(0, 0)
            for half in range(2):
                for k in range(1, KT, 2):
                    pool.wait_ge(h_hi_done, half * KT + k + 1)
                    nc.gpsimd.tensor_tensor(h_lo[:, k, cols(half)], x[:, k, cols(half)], h_hi[:, k, cols(half)].bitcast(F32),
                                            ALU.subtract).then_inc(h_lo_pool, 1)
            for n in range(I_CONV):
                split_lo(n + 1, (n + 1) % 2)
            for qb in range(FULL, QT):
                pool.wait_ge(score_step, (qb - FULL + 1) * HEADS)
                diag = score[qb][:, qb * P:(qb + 1) * P]
                nc.gpsimd.affine_select(out=diag, in_=diag, compare_op=ALU.is_ge, fill=NOT_CAUSAL, base=0,
                                        pattern=[[-1, P]], channel_multiplier=1).then_inc(masked, 1)
            nc.gpsimd.memset(u_pad[:, 0:2], 0.0).then_inc(const_set, 1)
            pool.wait_ge(const_set, 7)
            with pool.Fori(0, BT // 2) as i:
                for tt in range(2):
                    t, n, slot = 2 * i + tt, 6 * i + I_CONV + 3 * tt, (I_CONV + 3 * tt) % 2
                    split_lo(n + 1, 1 - slot)
                    split_lo(n + 2, slot)
                    for half in range(2):
                        pool.wait_ge(bank_free[half], n + 2)
                    pool.wait_ge(c_act, 4 * t + 1)
                    nc.gpsimd.tensor_tensor(u_pad[:, 2:S + 2], c_buf[:], x_buf[:], ALU.mult).then_inc(c_pool, 1)
                    split_lo(n + 3, 1 - slot)
                    for w in range(2):
                        pool.wait_ge(c_act, 4 * t + 2 + w + 1)
                        nc.gpsimd.tensor_tensor(c_acc[:], c_acc[:], x_buf[:], ALU.add).then_inc(c_pool, 1)
                    for half in range(2):
                        pool.wait_ge(bank_free[half], n + 3)
                    pool.wait_ge(c_pool, 5 * t + 4)
                    nc.gpsimd.tensor_tensor(c_acc[:], c_acc[:], b_buf[:], ALU.mult).then_inc(c_pool, 1)
                    pool.wait_ge(c_act, 4 * t + 5)
                    nc.gpsimd.tensor_tensor(tile_of(y_lo, t), c_acc[:], tile_of(y_hi, t).bitcast(F32), ALU.subtract).then_inc(c_pool, 1)
            with pool.Fori(0, (I_BM - I_A) // 2) as i:
                for o in range(2):
                    split_lo(2 * i + I_A + o + 1, (I_A + o + 1) % 2)

            def mult(n, half):
                pool.wait_ge(bank_free[half], n + 2)
                nc.gpsimd.tensor_tensor(gate[:, half], gate[:, half], proj[:, half], ALU.mult).then_inc(merge_mult, 1)

            with pool.Fori(0, KT) as m:
                n = 2 * m + I_BM
                split_lo(n + 1, (I_BM + 1) % 2, HALF)
                split_lo(n + 2, I_BM % 2)
                for half in range(2):
                    mult(n, half)

            def qk_split(g):
                for dst, hi, src, c in ((q_lo, q_hi, q_stage, 0), (k_lo, k_hi, k_stage, 1)):
                    pool.wait_ge(qk_hi_done, 2 * g + c + 1)
                    nc.gpsimd.tensor_tensor(dst[:], src[:], hi[:].bitcast(F32), ALU.subtract).then_inc(qk_lo_done, 1)

            pool.wait_ge(bias_done, QT - FULL)
            for v in (v_hi, v_lo):
                nc.gpsimd.memset(v[:, :, HD:2 * HD].bitcast(F32), 0.0).then_inc(const_set, 1)
            qk_split(0)
            with pool.Fori(0, PAIRS) as p:
                n = 2 * p + I_C1

                def weigh(i):
                    pool.wait_ge(sel_done, 2 * STEPS * p + 2 * i + 2)
                    pool.wait_ge(scan_done, STEPS * p + i + 1)
                    w = (block_of(i) + 1) * P - 1
                    nc.gpsimd.tensor_tensor(p_of(i)[:, 0:w], p_of(i)[:, 0:w], r_buf[:, r_at(i) + 1:r_at(i) + 1 + w], ALU.mult).then_inc(p_done, 1)

                for event, *which in schedule(FILL_A):
                    if event == "logits":
                        i = which[0]
                        w = (block_of(i) + 1) * P
                        for c, (buf, fill) in enumerate(((r_buf[:, r_at(i):r_at(i) + w], 1.0), (p_of(i), 0.0))):
                            pool.wait_ge(sig_done, 2 * STEPS * p + 2 * i + c + 2)
                            pool.sem_inc(pool_passed, 1)
                            diag = buf[:, w - P:w]
                            nc.gpsimd.affine_select(out=diag, in_=diag, compare_op=ALU.is_gt, fill=fill, base=0,
                                                    pattern=[[-1, P]], channel_multiplier=1).then_inc(sel_done, 1)
                        if 0 < i <= NARROW:
                            weigh(i - 1)
                    elif event == "weigh":
                        weigh(which[0])
                    elif event == "last logits":
                        qk_split(p + 1)
                    elif event == "fill":
                        o, half = which
                        if half == 0:
                            split_lo(n + o + 1, (I_C1 + o + 1) % 2)

            def sparse_pair(p):
                g, n = p + PAIRS, 4 * p + I_AM
                for event, *which in schedule(FILL_C):
                    if event == "logits":
                        i = which[0]
                        pool.wait_ge(rec_done, STEPS * p + i + 2)
                        pool.sem_inc(pool_passed, 1)
                        nc.gpsimd.tensor_scalar(p_of(i), p_of(i), stats[:, 8 + i % 4:9 + i % 4], 1.0, ALU.mult, ALU.mult).then_inc(p_done, 1)
                    elif event == "last logits" and not isinstance(p, int):
                        qk_split(g + 1)
                    elif event == "fill":
                        o, half = which
                        m = 2 * p + o // 2
                        if half == 0:
                            split_lo(n + o + 1, (I_AM + o + 1) % 2, WORDS if o % 2 else HALF)
                        if o % 2:
                            mult(n + o - 1, half)
                            pool.wait_ge(merge_mult, 2 * m + 2 * KT + half + 2)
                            pool.wait_ge(prev_in[half], 16 * m + 16)
                            nc.gpsimd.tensor_tensor(gate[:, half], gate[:, half], prev[:, half], ALU.add).then_inc(merge_done, 1)

            with pool.Fori(0, PAIRS - 1) as p:
                sparse_pair(p)
            sparse_pair(PAIRS - 1)

            def merge_tile(m, dst):
                n = 2 * m + I_CM
                split_lo(n + 1, 1 - I_CM % 2, HALF)
                split_lo(n + 2, I_CM % 2)
                for half in range(2):
                    mult(n, half)
                    pool.wait_ge(merge_mult, 2 * m + 4 * KT + half + 2)
                    pool.wait_ge(prev_in[half], 16 * m + 16 * KT + 16)
                    nc.gpsimd.tensor_tensor(dst(half), gate[:, half], prev[:, half], ALU.add).then_inc(merge_done, 1)

            with pool.Fori(0, KT // 2) as m:
                merge_tile(m, lambda half: gate[:, half])
            with pool.Fori(KT // 2, KT) as m:
                merge_tile(m, lambda half: tile_of(m_far, m - KT // 2)[:, cols(half)])
            for n in range(I_MIX + 1, N_ITEMS):
                split_lo(n, n % 2)

        @block.vector
        def _(dve):
            dve.sem_inc(t_lo_done, 2)
            for start_at_1 in (topk_step, add_done, rec_done, *o_free):
                dve.sem_inc(start_at_1, 1)
            for k in range(KT):
                dve.wait_ge(norm_sq_done, k + 1)
                if k == 0:
                    nc.vector.tensor_copy(ssq[:], norm_sq[:, 0]).then_inc(ssq_step, 1)
                else:
                    dve.wait_ge(ssq_step, k)
                    nc.vector.tensor_tensor(ssq[:], ssq[:], norm_sq[:, k % 2], ALU.add).then_inc(ssq_step, 1)
            dve.wait_ge(consts_in, 48)
            dve.wait_ge(norm_root, 1)
            nc.vector.reciprocal(rstd, rstd).then_inc(norm_rstd, 1)
            for half in range(2):
                dve.wait_ge(norm_wide, half + 1)
                for k in range(KT):
                    h = x[:, k, cols(half)]
                    nc.vector.scalar_tensor_tensor(h, h, gains[:, k:k + 1], psum[:, WIDE_BANK + half], ALU.mult, ALU.mult).then_inc(h_scaled, 1)
                    if k % 2:
                        dve.wait_ge(h_hi_done, half * KT + k)
                        nc.vector.tensor_tensor(h_lo[:, k - 1, cols(half)], x[:, k - 1, cols(half)],
                                                h_hi[:, k - 1, cols(half)].bitcast(F32), ALU.subtract).then_inc(h_lo_dve, 1)
            dve.wait_ge(wi_hi_done, 1)
            nc.vector.tensor_tensor(wi_lo[:], wi[:], wi_hi[:].bitcast(F32), ALU.subtract).then_inc(wi_lo_done, 1)
            for n in range(I_CONV):
                for half in range(2):
                    dve.wait_ge(idx_hi, 2 * n + half + 1)
                    hi, lo = ((iq_hi[:, n], iq_lo[:, n]) if n < BT else (ik_hi[:], ik_lo[:]))
                    nc.vector.tensor_tensor(lo[:, cols(half)], psum[:, half], hi[:, cols(half)].bitcast(F32), ALU.subtract).then_inc(bank_free[half], 1)
            dve.wait_ge(wi_sum, 1)
            for half in range(2):
                nc.vector.tensor_copy(wi_rows[:, cols(half)], psum[0:HEADS, OB + half]).then_inc(wi_out, 1)
            dve.wait_ge(wi_turned, 1)
            nc.vector.tensor_scalar(wi_q, psum[:, OB, 0:QT * HEADS], HEADS ** -0.5, None, ALU.mult).then_inc(wi_done, 1)
            dve.wait_ge(wi_done, 1)
            dve.wait_ge(h_lo_pool, KT)
            s = 0
            for qb in range(FULL, QT):
                for h in range(HEADS):
                    dve.wait_ge(relu_done, s + 1)
                    r = relu[:, s % 2, 0:(qb + 1) * P]
                    w = wi_q[:, qb * HEADS + h:qb * HEADS + h + 1]
                    if h == 0:
                        nc.vector.tensor_scalar(score[qb][:], r, w, None, ALU.mult).then_inc(score_step, 1)
                    else:
                        dve.wait_ge(score_step, s)
                        nc.vector.scalar_tensor_tensor(score[qb][:], r, w, score[qb][:], ALU.mult, ALU.add).then_inc(score_step, 1)
                    s += 1
            ROUNDS = TOPK // 8
            UNROLL = 4
            for b, qb in enumerate(range(FULL, QT)):
                dve.wait_ge(masked, b + 1)
                with dve.Fori(0, ROUNDS // UNROLL) as i:
                    for u in range(UNROLL):
                        step = 2 * UNROLL * i + 2 * ROUNDS * b + 2 * u
                        dve.wait_ge(topk_step, step + 1)
                        dve.sem_inc(dve_passed, 1)
                        nc.vector.max(top8, score[qb][:]).then_inc(topk_step, 1)
                        dve.wait_ge(topk_step, step + 2)
                        dve.sem_inc(dve_passed, 1)
                        nc.vector.match_replace(out=score[qb][:], in_to_replace=top8, in_values=score[qb][:], imm_value=TAKEN).then_inc(topk_step, 1)
                dve.wait_ge(topk_step, 2 * ROUNDS * (b + 1) + 1)
                nc.vector.tensor_scalar(bias[qb][:], score[qb][:], (NOT_CAUSAL + TAKEN) / 2, NEG, ALU.is_gt, ALU.mult).then_inc(bias_done, 1)

            def v_parts(g):
                for r in range(VG):
                    dve.wait_ge(t_hi_done, NG * g + r + 1)
                    nc.vector.tensor_tensor(v_place(v_lo, r), v_bank(r), v_place(v_hi, r).bitcast(F32), ALU.subtract).then_inc(t_lo_done, 1)

            def t_part(g, k, r):
                e, count = g_base[k] + r, groups(k)[r][1]
                dve.wait_ge(t_hi_done, NG * g + e + 1)
                nc.vector.tensor_tensor(t_lo[:, e % 2, 0:count * P], psum[:, TB + e % 2, 0:count * P],
                                        t_hi[:, e % 2, 0:count * P].bitcast(F32), ALU.subtract).then_inc(t_lo_done, 1)

            dve.wait_ge(const_set, 9)
            with dve.Fori(0, PAIRS) as p:

                def scan(i):
                    dve.wait_ge(sel_done, 2 * STEPS * p + 2 * i + 1)
                    back = r_buf[:, r_at(i):r_at(i) + (block_of(i) + 1) * P][:, ::-1]
                    nc.vector.tensor_tensor_scan(back, back, back, 1.0, ALU.mult, ALU.bypass).then_inc(scan_done, 1)

                for event, *which in schedule(FILL_A):
                    if event == "logits":
                        i = which[0]
                        if 0 < i <= NARROW:
                            scan(i - 1)
                        if i >= NARROW:
                            scan(i)
                    elif event == "v":
                        v_parts(p)
                    elif event == "transposes":
                        t_part(p, *which)
                    elif event == "outputs":
                        half = which[0]
                        dve.wait_ge(o_hi_done, 2 * p + half + 1)
                        nc.vector.tensor_tensor(tile_of(y_lo, p)[:, cols(half)], psum[:, OB + half],
                                                tile_of(y_hi, p)[:, cols(half)].bitcast(F32), ALU.subtract).then_inc(o_free[half], 1)

            def sparse_pair(p):
                g = p + PAIRS

                def invert(i):
                    dve.wait_ge(exp_done, STEPS * p + i + 2)
                    dve.wait_ge(p_done, STEPS * g + max(i - 3, 0) + 1)
                    nc.vector.reciprocal(stats[:, 8 + i % 4:9 + i % 4], stats[:, 4 + i % 4:5 + i % 4]).then_inc(rec_done, 1)

                inverted = 0
                for event, *which in schedule(FILL_C):
                    if event == "logits":
                        i = which[0]
                        if inverted < i:
                            invert(i - 1)
                            inverted = i
                        dve.wait_ge(z_done, STEPS * g + i + 2)
                        dve.wait_ge(t_done, NG * g + units_before(p_at, i) + 1)
                        dve.wait_ge(exp_done, STEPS * p + max(i - 3, 0) + 1)
                        dve.sem_inc(dve_passed, 1)
                        nc.vector.tensor_tensor_reduce(p_of(i), logit_banks(i), bias[block_of(i)][:], -SCALE, 3e38, ALU.add, ALU.min,
                                                       stats[:, i % 4:i % 4 + 1]).then_inc(add_done, 1)
                    elif event == "last logits":
                        invert(STEPS - 1)
                        inverted = STEPS
                    elif event == "v":
                        v_parts(g)
                    elif event == "transposes":
                        if i >= NARROW and inverted <= i:
                            invert(i)
                            inverted = i + 1
                        t_part(g, *which)

            with dve.Fori(0, PAIRS - 1) as p:
                sparse_pair(p)
            sparse_pair(PAIRS - 1)
            dve.wait_ge(halves_done, 4 + 2 * I_CM)
            for half in range(2):
                dve.wait_ge(o_hi_done, 2 * PAIRS + half + 1)
                nc.vector.tensor_tensor(y_lo[:, PAIRS - 1, cols(half)], psum[:, OB + half],
                                        y_hi[:, PAIRS - 1, cols(half)].bitcast(F32), ALU.subtract).then_inc(yc_lo_done, 1)
            for k in range(BT - 1):
                dve.wait_ge(yc_hi_done, k + 1)
                nc.vector.tensor_tensor(y_lo[:, k], yc[k][:], y_hi[:, k].bitcast(F32), ALU.subtract).then_inc(yc_lo_done, 1)
            with dve.Fori(0, KT // 2) as m:
                for half in range(2):
                    dve.wait_ge(m_hi_done, 2 * m + half + 1)
                    nc.vector.tensor_tensor(tile_of(m_lo, m)[:, cols(half)], gate[:, half],
                                            tile_of(m_hi, m)[:, cols(half)].bitcast(F32), ALU.subtract).then_inc(m_lo_done, 1)
            for k in range(KT // 2):
                dve.wait_ge(n_hi_done, k + 1)
                nc.vector.tensor_tensor(n_lo[:, k], m_far[:, k], n_hi[:, k].bitcast(F32), ALU.subtract).then_inc(n_lo_done, 1)
            dve.wait_ge(n_lo_done, KT // 2)
            dve.wait_ge(x_again_in, 16 * KT)
            for v in range(2 * KT + 1):
                if v < 2 * KT:
                    m, half = v // 2, v % 2
                    dve.wait_ge(halves_done, 4 + 2 * I_MIX + v + 1)
                    nc.vector.tensor_tensor(x[:, m, cols(half)], psum[:, half], x_again[:, m, cols(half)], ALU.add).then_inc(bank_free[half], 1)
                if v:
                    half = (v - 1) % 2
                    dve.wait_ge(mix_sq_done, v)
                    if v >= 3:
                        dve.wait_ge(mix_ssq, v - 2)
                        nc.vector.tensor_tensor(ssq[:, cols(half)], ssq[:, cols(half)], mix_sq[:, half], ALU.add).then_inc(mix_ssq, 1)
                    else:
                        nc.vector.tensor_copy(ssq[:, cols(half)], mix_sq[:, half]).then_inc(mix_ssq, 1)
                if v == 2:
                    dve.wait_ge(m_sq_done, 1)
                    nc.vector.tensor_reduce(m_ssq[:], m_sq[:].rearrange("p k t -> p t k"), AX.X, ALU.add).then_inc(m_step, 1)
                if v == 6:
                    dve.wait_ge(m_root, 1)
                    nc.vector.reciprocal(m_rstd[:], m_rstd[:]).then_inc(m_step, 1)
                    dve.wait_ge(m_step, 2)
                    for k in range(KT):
                        nc.vector.scalar_tensor_tensor(m_raw[:, k], m_raw[:, k], gains[:, 2 * KT + k:2 * KT + k + 1], m_rstd[:],
                                                       ALU.mult, ALU.mult).then_inc(m_step, 1)
                if v == 12:
                    dve.wait_ge(mem_hi_done, 1)
                    nc.vector.tensor_tensor(mem_lo[:], m_raw[:], mem_hi[:].bitcast(F32), ALU.subtract).then_inc(mem_lo_done, 1)


def build(nc, arrays, out):
    with ExitStack() as ctx:
        at = sbuf_map(nc)
        psum = ctx.enter_context(nc.psum_tensor("psum", [P, 8, HALF], F32))
        shared = {
            "x": at("x", 0, [P, KT, S]),
            "ssq": at("ssq", 51200, [P, S]),
            "gains": at("gains", 52224, [P, 5 * KT]),
            "ones": at("ones", 52264, [P, P]),
            "ident": at("ident", 52392, [P, P]),
            "eps": at("eps", 52520, [P, 1]),
            "gains_dram": arrays["gains"],
            "memory": (at("mem_hi", 30720, [P, KT, MEM], F32R), at("mem_lo", 32768, [P, KT, MEM], F32R)),
        }
        scratch = {name: nc.dram_tensor(name, shape, F32, kind="Internal").ap() for name, shape in
                   (("qkv_dram", [6 * PAIRS, P, S]), ("merged_dram", [KT, P, S]), ("yc_dram", [BT, P, S]), ("x2_dram", [KT, P, S]))}
        build_mixer(nc, ctx, at, psum, shared, arrays["mixer_w"], arrays["x"], arrays["mem"], arrays["idx_w"], arrays["taps"],
                    scratch["qkv_dram"], scratch["merged_dram"], scratch["yc_dram"])
        build_cross(nc, ctx, at, psum, shared, arrays["cross_w"], scratch["x2_dram"])
        build_ffn(nc, ctx, at, psum, shared, arrays["ffn_w"], arrays["ffn_conv_w"], arrays["ffn_conv_b"], scratch["x2_dram"], out)


def kernel(x, mem, norm_mix, w_in, sc_conv_w, w_sb_out, w_sc_out, w_dsa_out, w_mix_o, norm_xa, norm_mem, w_xa_q, w_xa_kv,
           w_xa_o, norm_ffn, w_ffn_in, ffn_conv_w, ffn_conv_b, w_ffn_down, norm_final):
    import concourse.bacc as bacc
    from concourse.bass_utils import run_bass_kernel_spmd

    def tiles(w):
        k, m = w.shape[0] // P, w.shape[1] // P
        return w.reshape(k, P, m, P).transpose(2, 1, 0, 3).reshape(m, P, k * P)

    def columns(w, start, width):
        return tiles(w[:, start:start + width])

    def trio(a, b, c):
        return [w for t in range(len(a)) for w in (a[t], b[t], c[t])]

    w_in = np.asarray(w_in)[0]
    SB, CONV, DSA, IDX, IDX_K = 0, 3 * SC, 6 * SC, 9 * SC, 10 * SC
    IDX_W, GATES = IDX_K + HD, IDX_K + HD + HEADS
    idx_k = w_in[:, IDX_K:IDX_K + HD]
    b, c, u = (columns(w_in, CONV + i * SC, SC) for i in range(3))
    conv = trio(c, u, b)
    sb = trio(*(columns(w_in, SB + i * SC, SC) for i in range(3)))
    dsa = trio(*(columns(w_in, DSA + i * SC, SC) for i in range(3)))

    def merge(branch, w):
        gates, proj = columns(w_in, GATES + branch * D, D), tiles(np.asarray(w)[0])
        proj = np.concatenate([proj, np.zeros_like(proj)], axis=2)
        return [w for m in range(KT) for w in (gates[m], proj[m])]

    mixer_w = [*columns(w_in, IDX, SC), *tiles(np.concatenate([idx_k, idx_k], axis=1)), *conv, *sb, *dsa[:4],
               *merge(1, w_sc_out), *dsa[4:], *merge(0, w_sb_out), *merge(2, w_dsa_out), *tiles(np.asarray(w_mix_o)[0])]

    w_kv, w_q, w_o = (np.asarray(w)[0] for w in (w_xa_kv, w_xa_q, w_xa_o))
    xk, xq = tiles(w_kv[:, :D]), tiles(w_q)
    xv = w_kv[:, D:].reshape(KT // 2, 2, P, 2, HALF).transpose(3, 0, 2, 1, 4).reshape(KT, P, WORDS)
    xo = w_o.reshape(XA_HEADS, 2, P, 2, 4, P).transpose(0, 3, 2, 1, 4, 5).reshape(XA_HEADS, 2, P, WORDS)
    cross_w = [*xk, *xv, xq[0], xq[1]]
    for h in range(XA_HEADS):
        cross_w += ([*xo[h - 1]] if h else []) + ([*xq[2 * h + 2:2 * h + 4]] if h + 1 < XA_HEADS else [])
    cross_w += [*xo[XA_HEADS - 1]]

    w_up, w_down = np.asarray(w_ffn_in)[0], np.asarray(w_ffn_down)[0]
    fa, fu = tiles(w_up[:, :DFF]), tiles(w_up[:, DFF:])
    down = w_down.reshape(FT // 2, 2, P, 2, 4, P).transpose(3, 0, 2, 1, 4, 5).reshape(FT, P, WORDS)
    ffn_w = [w for f in range(FT) for w in (fa[f], fu[f])] + [*down]

    gains = np.stack([np.asarray(g).reshape(KT, P) for g in (norm_mix, norm_xa, norm_mem, norm_ffn, norm_final)])
    arrays = {
        "x": np.asarray(x)[0].T.reshape(KT, P, S),
        "mem": np.asarray(mem)[0].T.reshape(KT, P, MEM),
        "gains": gains.transpose(2, 0, 1).reshape(P, 5 * KT),
        "mixer_w": np.stack(mixer_w),
        "idx_w": w_in[:, IDX_W:IDX_W + HEADS].reshape(KT, P, HEADS).transpose(1, 0, 2),
        "taps": np.asarray(sc_conv_w)[0].reshape(3, BT, P).transpose(2, 1, 0).reshape(P, 3 * BT),
        "cross_w": np.stack(cross_w),
        "ffn_w": np.stack(ffn_w),
        "ffn_conv_w": np.asarray(ffn_conv_w)[0].reshape(3, FT, P).transpose(2, 1, 0),
        "ffn_conv_b": np.asarray(ffn_conv_b)[0].reshape(FT, P).T,
    }
    arrays = {name: np.ascontiguousarray(a) for name, a in arrays.items()}
    nc = bacc.Bacc("TRN2", target_bir_lowering=False, num_devices=1)
    drams = {name: nc.dram_tensor(name + "_in", list(a.shape), F32, kind="ExternalInput").ap() for name, a in arrays.items()}
    out = nc.dram_tensor("out", [KT, P, S], F32, kind="ExternalOutput").ap()
    build(nc, drams, out)
    result = run_bass_kernel_spmd(nc, [{name + "_in": a for name, a in arrays.items()}], core_ids=[0])
    return result.results[0]["out"].reshape(D, S).T[None]
```
